# Optimizing a Trainium2 kernel written in Bass

```python
import math
import jax, jax.numpy as jnp
from jax import lax
import numpy as np

D_MODEL = 2048
BATCH = 1
SEQ = 512
DEPTH = 1

GMLP_CHUNK = 128
GMLP_GROUPS = 4
GMLP_GROUP_DIM = 128
GMLP_WIDTH = GMLP_GROUPS * GMLP_GROUP_DIM

DN_HEADS = 8
DN_HEAD_DIM = 128
DN_WIDTH = DN_HEADS * DN_HEAD_DIM
DN_CONV = 4
DN_CHUNK = 64

XA_HEADS = 4
XA_HEAD_DIM = 128
XA_WIDTH = XA_HEADS * XA_HEAD_DIM
N_MEM = 256

MIX_WIDTH = GMLP_WIDTH + DN_WIDTH + XA_WIDTH
EPS = 1e-6

SEG_WIDTHS = (GMLP_WIDTH, GMLP_WIDTH, GMLP_WIDTH,
              DN_WIDTH, DN_WIDTH, DN_WIDTH, DN_WIDTH, DN_HEADS, DN_HEADS,
              XA_WIDTH, XA_WIDTH)
IN_WIDTH = sum(SEG_WIDTHS)
SPLIT_POINTS = tuple(sum(SEG_WIDTHS[:i + 1]) for i in range(len(SEG_WIDTHS) - 1))


def rmsnorm(x, g):
    xf = x.astype(jnp.float32)
    y = xf * lax.rsqrt(jnp.mean(xf * xf, axis=-1, keepdims=True) + EPS)
    return (y * g.astype(jnp.float32)).astype(x.dtype)

def layernorm(x, g, b):
    xf = x.astype(jnp.float32)
    mu = jnp.mean(xf, axis=-1, keepdims=True)
    xc = xf - mu
    y = xc * lax.rsqrt(jnp.mean(xc * xc, axis=-1, keepdims=True) + EPS)
    return (y * g.astype(jnp.float32) + b.astype(jnp.float32)).astype(x.dtype)

def l2norm(x):
    xf = x.astype(jnp.float32)
    return xf * lax.rsqrt(jnp.sum(xf * xf, axis=-1, keepdims=True) + EPS)

def gmlp_spatial_gating(u, v, ws, bs, ln_g, ln_b):
    B, S, _ = u.shape
    u = jax.nn.gelu(u)
    v = layernorm(jax.nn.gelu(v), ln_g, ln_b)
    nc = S // GMLP_CHUNK
    v = v.reshape(B, nc, GMLP_CHUNK, GMLP_GROUPS, GMLP_GROUP_DIM)
    causal = jnp.tril(jnp.ones((GMLP_CHUNK, GMLP_CHUNK), dtype=bool))
    w = jnp.where(causal[None], ws, 0)
    s = jnp.einsum('gts,bcsgd->bctgd', w, v) + bs.T[None, None, :, :, None]
    return u * s.reshape(B, S, GMLP_WIDTH)

def causal_conv_silu(x, w):
    K = w.shape[0]
    S = x.shape[1]
    xp = jnp.pad(x, ((0, 0), (K - 1, 0), (0, 0)))
    y = sum(w[k] * xp[:, k:k + S] for k in range(K))
    return jax.nn.silu(y)

def gated_delta_rule(q, k, v, g, beta):
    f32 = jnp.float32
    q, k, v, g, beta = (t.astype(f32) for t in (q, k, v, g, beta))
    B, H, S, Dk = q.shape
    Dv = v.shape[-1]
    C = DN_CHUNK
    N = S // C
    q = q.reshape(B, H, N, C, Dk)
    k = k.reshape(B, H, N, C, Dk)
    v = v.reshape(B, H, N, C, Dv)
    g = g.reshape(B, H, N, C)
    beta = beta.reshape(B, H, N, C)

    g_cum = jnp.cumsum(g, axis=-1)
    tri = jnp.tril(jnp.ones((C, C), dtype=bool))
    strict = jnp.tril(jnp.ones((C, C), dtype=bool), k=-1)
    diff = g_cum[..., :, None] - g_cum[..., None, :]
    decay = jnp.exp(jnp.where(tri, diff, -jnp.inf))

    kb = k * beta[..., None]
    vb = v * beta[..., None]
    a = jnp.where(strict, jnp.einsum('bhnid,bhnjd->bhnij', kb, k) * decay, 0.0)
    eye = jnp.eye(C, dtype=f32)
    T = lax.linalg.triangular_solve(a + eye, jnp.broadcast_to(eye, a.shape),
                                    left_side=True, lower=True, unit_diagonal=True)
    value = jnp.einsum('bhnij,bhnjd->bhnid', T, vb)
    k_cumdecay = jnp.einsum('bhnij,bhnjd->bhnid', T, kb * jnp.exp(g_cum)[..., None])
    attn_intra = jnp.where(tri, jnp.einsum('bhnid,bhnjd->bhnij', q, k) * decay, 0.0)
    q_g = q * jnp.exp(g_cum)[..., None]
    g_last = g_cum[..., -1]
    k_dec = k * jnp.exp(g_last[..., None] - g_cum)[..., None]

    def step(state, inp):
        qg_c, kcd_c, val_c, ai_c, kd_c, gl_c = inp
        v_new = val_c - jnp.einsum('bhid,bhde->bhie', kcd_c, state)
        o_c = jnp.einsum('bhid,bhde->bhie', qg_c, state) + jnp.einsum('bhij,bhje->bhie', ai_c, v_new)
        state = state * jnp.exp(gl_c)[..., None, None] + jnp.einsum('bhid,bhie->bhde', kd_c, v_new)
        return state, o_c

    xs = tuple(jnp.moveaxis(t, 2, 0) for t in (q_g, k_cumdecay, value, attn_intra, k_dec, g_last))
    s0 = jnp.zeros((B, H, Dk, Dv), f32)
    _, o = lax.scan(step, s0, xs)
    return jnp.moveaxis(o, 0, 2).reshape(B, H, S, Dv)

def first_inputs(seed: int = 0) -> dict:
    key = jax.random.key(seed)
    ks = jax.random.split(key, 16)
    f32 = jnp.float32
    nrm = lambda k_, shp: jax.random.normal(k_, shp, f32)
    x = nrm(ks[0], (BATCH, SEQ, D_MODEL))
    mem = nrm(ks[1], (BATCH, N_MEM, D_MODEL))
    ln_g = 1.0 + 0.1 * nrm(ks[2], (DEPTH, D_MODEL))
    w_in = nrm(ks[3], (DEPTH, D_MODEL, IN_WIDTH)) * D_MODEL ** -0.5
    gmlp_ln_g = 1.0 + 0.1 * nrm(ks[4], (DEPTH, GMLP_WIDTH))
    gmlp_ln_b = 0.1 * nrm(ks[5], (DEPTH, GMLP_WIDTH))
    gmlp_ws = nrm(ks[6], (DEPTH, GMLP_GROUPS, GMLP_CHUNK, GMLP_CHUNK)) * GMLP_CHUNK ** -0.5
    gmlp_bs = 1.0 + 0.1 * nrm(ks[7], (DEPTH, GMLP_GROUPS, GMLP_CHUNK))
    conv_w = nrm(ks[8], (DEPTH, DN_CONV, 3 * DN_WIDTH)) * DN_CONV ** -0.5
    dn_a_log = jnp.log(jax.random.uniform(ks[9], (DEPTH, DN_HEADS), f32, minval=1.0, maxval=16.0))
    dt = jnp.exp(jax.random.uniform(ks[10], (DEPTH, DN_HEADS), f32,
                                    minval=math.log(1e-3), maxval=math.log(1e-1)))
    dn_dt_bias = dt + jnp.log(-jnp.expm1(-dt))
    dn_norm_g = 1.0 + 0.1 * nrm(ks[11], (DEPTH, DN_HEAD_DIM))
    mem_norm_g = 1.0 + 0.1 * nrm(ks[12], (DEPTH, D_MODEL))
    w_mem_kv = nrm(ks[13], (DEPTH, D_MODEL, 2 * XA_WIDTH)) * D_MODEL ** -0.5
    w_out = nrm(ks[14], (DEPTH, MIX_WIDTH, D_MODEL)) * MIX_WIDTH ** -0.5
    final_g = 1.0 + 0.1 * nrm(ks[15], (D_MODEL,))
    return {"x": x, "mem": mem, "ln_g": ln_g, "w_in": w_in,
            "gmlp_ln_g": gmlp_ln_g, "gmlp_ln_b": gmlp_ln_b, "gmlp_ws": gmlp_ws, "gmlp_bs": gmlp_bs,
            "conv_w": conv_w, "dn_a_log": dn_a_log, "dn_dt_bias": dn_dt_bias, "dn_norm_g": dn_norm_g,
            "mem_norm_g": mem_norm_g, "w_mem_kv": w_mem_kv, "w_out": w_out, "final_g": final_g}

def first_block(x, mem, ln_g, w_in, gmlp_ln_g, gmlp_ln_b, gmlp_ws, gmlp_bs, conv_w, dn_a_log,
              dn_dt_bias, dn_norm_g, mem_norm_g, w_mem_kv, w_out, final_g):
    B, S, _ = x.shape
    M = mem.shape[1]
    for l in range(DEPTH):
        h = rmsnorm(x, ln_g[l])
        proj = h @ w_in[l]
        (g_u, g_v, g_z, d_q, d_k, d_v, d_z, d_a, d_b, c_q, c_z) = jnp.split(proj, SPLIT_POINTS, axis=-1)

        out_a = gmlp_spatial_gating(g_u, g_v, gmlp_ws[l], gmlp_bs[l], gmlp_ln_g[l], gmlp_ln_b[l]) * jax.nn.silu(g_z)

        qkv = causal_conv_silu(jnp.concatenate([d_q, d_k, d_v], axis=-1), conv_w[l])
        q, k, v = jnp.split(qkv, 3, axis=-1)
        to_heads = lambda t: t.reshape(B, S, DN_HEADS, DN_HEAD_DIM).transpose(0, 2, 1, 3)
        q = l2norm(to_heads(q)) * DN_HEAD_DIM ** -0.5
        k = l2norm(to_heads(k))
        v = to_heads(v)
        g = -jnp.exp(dn_a_log[l].astype(jnp.float32)) * jax.nn.softplus(
            d_a.astype(jnp.float32) + dn_dt_bias[l].astype(jnp.float32))
        beta = jax.nn.sigmoid(d_b.astype(jnp.float32))
        o = gated_delta_rule(q, k, v, g.transpose(0, 2, 1), beta.transpose(0, 2, 1))
        o = o.transpose(0, 2, 1, 3).astype(x.dtype)
        o = rmsnorm(o, dn_norm_g[l]) * jax.nn.silu(d_z.reshape(B, S, DN_HEADS, DN_HEAD_DIM))
        out_b = o.reshape(B, S, DN_WIDTH)

        m = rmsnorm(mem, mem_norm_g[l])
        mk, mv = jnp.split(m @ w_mem_kv[l], 2, axis=-1)
        mk = mk.reshape(B, M, XA_HEADS, XA_HEAD_DIM)
        mv = mv.reshape(B, M, XA_HEADS, XA_HEAD_DIM)
        cq = c_q.reshape(B, S, XA_HEADS, XA_HEAD_DIM)
        scores = jnp.einsum('bshd,bmhd->bhsm', cq, mk).astype(jnp.float32) * XA_HEAD_DIM ** -0.5
        p = jax.nn.softmax(scores, axis=-1).astype(mv.dtype)
        out_c = jnp.einsum('bhsm,bmhd->bshd', p, mv).reshape(B, S, XA_WIDTH) * jax.nn.silu(c_z)

        mixed = jnp.concatenate([out_a, out_b, out_c], axis=-1)
        x = x + mixed @ w_out[l]
    return rmsnorm(x, final_g)


CHUNK = 64
Q_BLOCK = 128
HEAD_DIM = 128
D_MIX = D_MODEL
D_SB = D_MIX // 2
D_CH = D_MIX - D_SB
N_HEADS_SB = D_SB // HEAD_DIM
N_HEADS_CH = D_CH // HEAD_DIM
LEFT_CHUNKS = 8
BAND = LEFT_CHUNKS + 1
REL_CLIP = 256
N_REL = REL_CLIP + CHUNK
D_IN = 4 * D_SB + 4 * D_CH
NORM_EPS = 1e-6
NEG_BIG = -1e30


def rms_norm(x, g):
    xf = x.astype(jnp.float32)
    y = xf * lax.rsqrt(jnp.mean(xf * xf, axis=-1, keepdims=True) + NORM_EPS)
    return (y * g.astype(jnp.float32)).astype(x.dtype)

def split_heads(t, n_heads):
    b, s, _ = t.shape
    return t.reshape(b, s, n_heads, HEAD_DIM).transpose(0, 2, 1, 3)

def merge_heads(t):
    b, h, s, d = t.shape
    return t.transpose(0, 2, 1, 3).reshape(b, s, h * d)

def stick_breaking_attention(q, k, v):
    seq = q.shape[2]
    scale = q.shape[-1] ** -0.5
    outs = []
    for blk in range(seq // Q_BLOCK):
        t0 = blk * Q_BLOCK
        t1 = t0 + Q_BLOCK
        qb = q[:, :, t0:t1]
        kb = k[:, :, :t1]
        vb = v[:, :, :t1]
        z = jnp.einsum('bhtd,bhsd->bhts', qb, kb).astype(jnp.float32) * scale
        t_idx = jnp.arange(t0, t1)[:, None]
        s_idx = jnp.arange(t1)[None, :]
        causal = s_idx < t_idx
        log_stay = jnp.where(causal, jax.nn.log_sigmoid(-z), 0.0)
        after = lax.cumsum(log_stay, axis=3, reverse=True) - log_stay
        w = jnp.where(causal, jnp.exp(jax.nn.log_sigmoid(z) + after), 0.0)
        outs.append(jnp.einsum('bhts,bhsd->bhtd', w.astype(v.dtype), vb))
    return jnp.concatenate(outs, axis=2)

def chunk_band_attention(q, k, v, q_gain, k_gain, rel_table):
    b, h, seq, d = q.shape
    nc = seq // CHUNK
    q = rms_norm(q, q_gain)
    k = rms_norm(k, k_gain)
    qc = q.reshape(b, h, nc, CHUNK, d)
    pad = ((0, 0), (0, 0), (LEFT_CHUNKS * CHUNK, 0), (0, 0))
    kc = jnp.pad(k, pad).reshape(b, h, nc + LEFT_CHUNKS, CHUNK, d)
    vc = jnp.pad(v, pad).reshape(b, h, nc + LEFT_CHUNKS, CHUNK, d)
    band_idx = jnp.arange(nc)[:, None] + jnp.arange(BAND)[None, :]
    kband = kc[:, :, band_idx].reshape(b, h, nc, BAND * CHUNK, d)
    vband = vc[:, :, band_idx].reshape(b, h, nc, BAND * CHUNK, d)
    scores = jnp.einsum('bhcid,bhcpd->bhcip', qc, kband).astype(jnp.float32) * (d ** -0.5)
    i_pos = np.arange(CHUNK)[:, None]
    p_pos = np.arange(BAND * CHUNK)[None, :]
    dist = LEFT_CHUNKS * CHUNK + i_pos - p_pos
    rel_idx = np.clip(dist, -(CHUNK - 1), REL_CLIP) + (CHUNK - 1)
    bias = rel_table.astype(jnp.float32)[:, rel_idx]
    scores = scores + bias[None, :, None]
    valid = jnp.repeat(band_idx >= LEFT_CHUNKS, CHUNK, axis=1)
    scores = jnp.where(valid[None, None, :, None, :], scores, NEG_BIG)
    probs = jax.nn.softmax(scores, axis=-1)
    out = jnp.einsum('bhcip,bhcpd->bhcid', probs.astype(v.dtype), vband)
    return out.reshape(b, h, seq, d)

def second_inputs(seed: int = 0) -> dict:
    key = jax.random.key(seed)
    ks = jax.random.split(key, 8)
    x = jax.random.normal(ks[0], (BATCH, SEQ, D_MODEL), jnp.float32)
    norm_g = 1.0 + 0.02 * jax.random.normal(ks[1], (DEPTH, D_MODEL), jnp.float32)
    w_in = jax.random.normal(ks[2], (DEPTH, D_MODEL, D_IN), jnp.float32) * D_MODEL ** -0.5
    q_norm_g = 1.0 + 0.02 * jax.random.normal(ks[3], (DEPTH, HEAD_DIM), jnp.float32)
    k_norm_g = 1.0 + 0.02 * jax.random.normal(ks[4], (DEPTH, HEAD_DIM), jnp.float32)
    rel_bias = 0.1 * jax.random.normal(ks[5], (DEPTH, N_HEADS_CH, N_REL), jnp.float32)
    w_out = jax.random.normal(ks[6], (DEPTH, D_MIX, D_MODEL), jnp.float32) * D_MIX ** -0.5
    return {"x": x, "norm_g": norm_g, "w_in": w_in, "q_norm_g": q_norm_g,
            "k_norm_g": k_norm_g, "rel_bias": rel_bias, "w_out": w_out}

def second_block(x, norm_g, w_in, q_norm_g, k_norm_g, rel_bias, w_out):
    splits = np.cumsum([D_SB, D_SB, D_SB, D_SB, D_CH, D_CH, D_CH])
    for layer in range(DEPTH):
        h = rms_norm(x, norm_g[layer])
        proj = jnp.einsum('bsd,de->bse', h, w_in[layer])
        qa, ka, va, ga, qb, kb, vb, gb = jnp.split(proj, splits, axis=-1)
        ya = stick_breaking_attention(split_heads(qa, N_HEADS_SB),
                                      split_heads(ka, N_HEADS_SB),
                                      split_heads(va, N_HEADS_SB))
        yb = chunk_band_attention(split_heads(qb, N_HEADS_CH),
                                  split_heads(kb, N_HEADS_CH),
                                  split_heads(vb, N_HEADS_CH),
                                  q_norm_g[layer], k_norm_g[layer], rel_bias[layer])
        mixed = jnp.concatenate([merge_heads(ya) * jax.nn.silu(ga),
                                 merge_heads(yb) * jax.nn.silu(gb)], axis=-1)
        x = x + jnp.einsum('bse,ed->bsd', mixed, w_out[layer])
    return x


def setup_inputs(seed=0):
    out = dict(first_inputs(seed))
    for name, value in second_inputs(seed + 1).items():
        if name != "x":
            out[name + "_2"] = value
    return out


def reference(
    x, mem, ln_g, w_in, gmlp_ln_g, gmlp_ln_b, gmlp_ws, gmlp_bs, conv_w, dn_a_log, dn_dt_bias,
    dn_norm_g, mem_norm_g, w_mem_kv, w_out, final_g, norm_g_2, w_in_2, q_norm_g_2, k_norm_g_2,
    rel_bias_2, w_out_2,
):
    x = first_block(
        x, mem, ln_g, w_in, gmlp_ln_g, gmlp_ln_b, gmlp_ws, gmlp_bs, conv_w, dn_a_log,
        dn_dt_bias, dn_norm_g, mem_norm_g, w_mem_kv, w_out, final_g,
    )
    return second_block(
        x, norm_g_2, w_in_2, q_norm_g_2, k_norm_g_2, rel_bias_2, w_out_2,
    )


_drawn_inputs = setup_inputs


def setup_inputs(seed=0):
    import zlib

    import numpy as np

    out = dict(_drawn_inputs(seed))
    spreads = {}
    factors = {'gmlp_ln_g': 4.169,
     'gmlp_ln_b': 3.996,
     'gmlp_bs': 3.055,
     'mem_norm_g': 8.0,
     'norm_g_2': 6.546,
     'q_norm_g_2': 8.0,
     'k_norm_g_2': 8.0,
     'rel_bias_2': 8.0}
    for name, (base, spread) in spreads.items():
        noise = np.random.default_rng([zlib.crc32(name.encode()), seed]).standard_normal(out[name].shape)
        drawn = base * np.exp(spread * noise) if base else spread * noise
        out[name] = __import__('jax').numpy.asarray(drawn.astype(out[name].dtype))
    for name, factor in factors.items():
        out[name] = (out[name] * factor).astype(out[name].dtype)
    return out
```

```python
from contextlib import ExitStack

import numpy as np

import concourse.bass as bass
from concourse import mybir

P = 128
S = 512
D = 2048
KT = D // P
NB = S // P
EPS = 1e-6
SCALE = float(P) ** -0.5
NEG = -1e30
GM, DN, XA, MEM = 4, 8, 4, 256
SILU_FLOOR = -40.0
GELU_CUBE = 0.044715
GELU_SLOPE = 2.0 * (2.0 / 3.141592653589793) ** 0.5

U_MEM = 0
U_AB = U_MEM + 2 * XA
U_V = U_AB + 1
U_ZU = U_V + GM
U_X = U_ZU + 2 * GM
U_DN = U_X + 2 * XA
U_O1 = U_DN + 4 * DN
U_D2 = U_O1 + KT
U_O2 = U_D2 + 8 * DN
U_END = U_O2 + KT

CONSTS = ["ident", "ones", "tri_from", "neg_tri", "neg_ones", "strict", "hide"] + [f"level{k}" for k in range(7)]
LEVELS = 7
C_LN, C_MEM, C_FIN, C_LN2 = 0, KT, 2 * KT, 3 * KT
C_GG, C_GB = 4 * KT, 4 * KT + GM
C_CONV = C_GB + GM
C_DNG = C_CONV + DN * 3 * 4
C_QG, C_KG = C_DNG + 1, C_DNG + 2
C_ALOG, C_DT = C_DNG + 3, C_DNG + 3 + DN
C_ALL = C_DT + DN

F32 = mybir.dt.float32
F32R = mybir.dt.float32r
ACT = mybir.ActivationFunctionType
ALU = mybir.AluOpType
AX = mybir.AxisListType.X


class Steps:

    def __init__(self, eng, sem):
        self.eng, self.sem, self.base, self.n = eng, sem, 0, 0

    def then(self, ins):
        self.n += 1
        ins.then_inc(self.sem, 1)
        self.eng.wait_ge(self.sem, self.base + self.n)

    def enter(self, i, per):
        self.start, self.per = self.n + self.base, per
        self.base, self.n = self.start + i * per, 0

    def leave(self, times):
        assert self.n == self.per, (self.n, self.per)
        self.base, self.n = self.start + times * self.per, 0


def build(nc, w, xT, memT, consts, params, ws_t, bs_b, rel, x1_dram, outT):
    with ExitStack() as ctx:
        def sb(name, shape, dt=F32):
            return ctx.enter_context(nc.sbuf_tensor(name, shape, dt))

        act_hi = sb("act_hi", [P, KT * S], F32R)
        act_lo = sb("act_lo", [P, KT * S], F32R)
        big = sb("big", [P, KT * S])
        raw = [sb(f"raw{i}", [P, KT * P]) for i in range(2)]
        w_hi = [sb(f"w_hi{i}", [P, KT * P], F32R) for i in range(2)]
        w_lo = [sb(f"w_lo{i}", [P, KT * P], F32R) for i in range(2)]
        scratch = sb("scratch", [P, 33 * S])
        cst = sb("cst", [P, len(CONSTS) * P])
        par = sb("par", [P, C_ALL])
        eps = sb("eps", [P, 1])
        g2 = sb("g2", [P, KT])
        gate = {n: sb("gate_" + n, [P, NB * DN]) for n in ("a", "t", "g", "gc", "beta", "ekd", "ebg", "egl")}
        small = sb("small", [P, 16])
        bank = [ctx.enter_context(nc.psum_tensor(f"gemm{i}", [P, S], F32)) for i in range(2)]
        pb = [ctx.enter_context(nc.psum_tensor(f"pb{i}", [P, S], F32)) for i in range(6)]

        def tl(i, n=1):
            return scratch[:, i * S:(i + n) * S]

        C = {n: cst[:, i * P:(i + 1) * P] for i, n in enumerate(CONSTS)}
        m_hi, m_lo = act_lo[:, 0:KT * MEM], act_lo[:, KT * MEM:2 * KT * MEM]
        Y, E, SS, SQ = tl(0), tl(1), tl(2), tl(3)
        GV, PG, VTOK = tl(4, 4), tl(8, 4), tl(12, 4)
        MK, MV = tl(16, 2), tl(18, 2)
        CQ, CZ, PM, PT = tl(20), tl(21), tl(22, 2), tl(24, 2)
        MVI = tl(26)[:, 0:2 * P]
        GSQ, GR, GMEAN = tl(24, 4), tl(28), tl(29)
        QT, KTT, VT, SZ = tl(20), tl(21), tl(22), tl(23)
        GSEL, BSEL, EG, DEC, KB, AT, AI, KBG, KDEC = (tl(i) for i in range(24, 33))
        VB, QG, XI, YI, UI = (tl(i) for i in range(4, 9))
        ML, NK, VN, ST, OSQ, OR = tl(9, 2), tl(11), tl(12)[:, 0:P], tl(15)[:, 0:P], tl(13), tl(14)
        QA, KA, VA, VATOK, SGA = (tl(i) for i in range(4, 9))
        LB, SPB, WB = tl(9, 3), tl(12, 3), tl(15, 3)
        QB, KBN, VBT, VBTOK, SGB, BIAS = (tl(i) for i in range(18, 24))
        PB, PTB = tl(24, 3), tl(27, 3)
        ACC1, ACC2, R1, R12, XIN, X2, OUTS = tl(4), tl(5), tl(32), tl(31), tl(6, 2), tl(8), tl(10, 2)
        MEMRAW, MR, XR = tl(4, 8), tl(12), tl(13)

        wsT, bsb = tl(30), tl(31)

        def blk(a, c, n=1):
            return a[:, c * P:(c + n) * P]

        def v3(a):
            return a.rearrange("p (c t) -> p c t", t=P)

        UP = [0, 512, 896, 1152]
        UN = [S - P * b for b in range(NB)]
        DO = [0, 128, 384, 768]
        DNN = [P * (b + 1) for b in range(NB)]

        names = """consts_in mem_in x_in w_in0 w_in1 hi lo unit evac act_hi act_lo
            mem_sq mem_acc mem_ss mem_r mem_n x_sq x_acc x_ss x_r x_n
            mv_tok mv_ps mixed
            dve_steps act_steps pool_steps
            ab_rows ab_ps ab_tok ab_exp ab_ln ab_alog ab_g ab_cum ab_beta ab_e ab_fin ab_gc
            ge_sq ge_t ge_sig gv_done z_y z_sig
            ln_m1 ln_c ln_sq ln_m2 ln_r ln_v ln_tp ln_tok sp_w sp_o
            x_sc x_max x_exp x_p x_tp x_pt x_o xz_y xz_sig
            dn_y dn_sig dn_s dn_sq dn_ss dn_r dn_n
            sel gb eg bb kb dec_in dec_e dec_m kk at ai tp kbg m_lvl x1 y1 u_ps u_sb w_ps xy nk_ps nk
            vn_ps vn o_ps s_ps st o_sq o_ss o_r qg m_free
            o1_x0 o1_x1 o1_sq o1_acc o1_st o1_ss o1_r1 o1_t o1_r2 o1_r12 o1_n
            a_q a_k a_v a_vps a_vtok a_z a_abs a_l a_sp a_cum a_diag a_w a_o
            g_y g_sig b_sq b_ss b_r b_n b_v b_vps b_vtok b_bias b_sc b_add b_max b_exp b_p b_tp b_pt b_o b_bfree
            o2_x0 o2_x1 o2_xf o2_st0 o2_st1 init""".split()
        sem = {n: ctx.enter_context(nc.semaphore(n)) for n in names}
        gate_v = {n: t[:, :].rearrange("p (c h) -> p c h", h=DN) for n, t in gate.items()}
        block = ctx.enter_context(nc.Block())

        @block.sync
        def _(sp):
            def load(u, slot):
                sp.dma_start(raw[slot][:, :], w[u]).then_inc(sem[f"w_in{slot}"], 16)

            load(0, 0)
            load(1, 1)
            with sp.Fori(0, (U_END - 3) // 2) as i:
                for slot in range(2):
                    sp.wait_ge(sem["hi"], 8 * i + 4 * slot + 4)
                    sp.wait_ge(sem["lo"], 8 * i + 4 * slot + 4)
                    load(2 * i + 2 + slot, slot)
            sp.wait_ge(sem["hi"], 4 * (U_END - 2))
            sp.wait_ge(sem["lo"], 4 * (U_END - 2))
            load(U_END - 1, 0)

        @block.gpsimd
        def _(pool):
            def sel(h):
                nc.gpsimd.tensor_copy(v3(GSEL), gate_v["g"][:, :, bass.ds(h, 1)].broadcast_to([P, NB, P]))
                nc.gpsimd.tensor_copy(v3(BSEL), gate_v["beta"][:, :, bass.ds(h, 1)].broadcast_to([P, NB, P])).then_inc(sem["sel"], 1)

            pool.wait_ge(sem["ab_fin"], 1)
            pool.wait_ge(sem["mixed"], GM + XA)
            sel(0)

            def levels(h):
                pool.wait_ge(sem["at"], h + 1)
                for k in range(LEVELS):
                    if k >= 2:
                        pool.wait_ge(sem["xy"], LEVELS * h + k - 1)
                    nc.gpsimd.tensor_tensor(v3(blk(ML, NB * (k % 2), NB)), v3(AT),
                                            C[f"level{k}"].rearrange("p (c t) -> p c t", c=1).broadcast_to([P, NB, P]),
                                            ALU.mult).then_inc(sem["m_lvl"], 1)

            def head(h, last=False):
                levels(h)
                if not last:
                    pool.wait_ge(sem["bb"], h + 1)
                    sel(h + 1)

            with pool.Fori(0, DN - 1) as h:
                head(h)
            head(DN - 1, True)
            for s in range(2):
                if s == 0:
                    pool.wait_ge(sem["mixed"], KT)
                pool.dma_start(blk(XIN, NB * s, NB), xT[s]).then_inc(sem[f"o1_x{s}"], 16)
            with pool.Fori(0, KT // 2 - 1) as i:
                for s in range(2):
                    pool.wait_ge(sem["evac"], 2 * i + (U_O1 + s + 1))
                    pool.dma_start(x1_dram[2 * i + s], big[:, bass.ds((2 * i + s) * S, S)]).then_inc(sem["o1_st"], 16)
                    pool.dma_start(blk(XIN, NB * s, NB), xT[2 * i + s + 2]).then_inc(sem[f"o1_x{s}"], 16)
            for s in range(2):
                pool.wait_ge(sem["evac"], U_O1 + KT - 1 + s)
                pool.dma_start(x1_dram[KT - 2 + s], big[:, (KT - 2 + s) * S:(KT - 1 + s) * S]).then_inc(sem["o1_st"], 16)
            pool.wait_ge(sem["o1_r12"], 1)
            pool.dma_start(BIAS, rel[0]).then_inc(sem["b_bias"], 16)
            with pool.Fori(1, DN) as h:
                pool.wait_ge(sem["b_add"], NB * h)
                pool.dma_start(BIAS, rel[h]).then_inc(sem["b_bias"], 16)
            pool.wait_ge(sem["mixed"], 2 * KT)
            for s in range(2):
                pool.dma_start(blk(XIN, NB * s, NB), x1_dram[s]).then_inc(sem[f"o2_x{s}"], 16)
            with pool.Fori(0, KT // 2 - 1) as i:
                for s in range(2):
                    pool.wait_ge(sem["evac"], 2 * i + (U_O2 + s + 1))
                    pool.dma_start(outT[2 * i + s], blk(OUTS, NB * s, NB)).then_inc(sem[f"o2_st{s}"], 16)
                    pool.dma_start(blk(XIN, NB * s, NB), x1_dram[2 * i + s + 2]).then_inc(sem[f"o2_x{s}"], 16)
            for s in range(2):
                pool.wait_ge(sem["evac"], U_O2 + KT - 1 + s)
                pool.dma_start(outT[KT - 2 + s], blk(OUTS, NB * s, NB)).then_inc(sem[f"o2_st{s}"], 16)
            for s in range(2):
                pool.wait_ge(sem[f"o2_st{s}"], 8 * KT)

        @block.scalar
        def _(act):
            st = Steps(act, sem["act_steps"])
            A = nc.scalar.activation

            def hi(u, slot):
                act.wait_ge(sem[f"w_in{slot}"], 8 * (u - slot) + 16)
                if not isinstance(u, int) or u >= 2:
                    act.wait_ge(sem["unit"], u - 1)
                for q in range(4):
                    c = slice(q * S, (q + 1) * S)
                    A(w_hi[slot][:, c], raw[slot][:, c], ACT.Copy).then_inc(sem["hi"], 1)

            def sigmoid(ready, n, done):
                act.wait_ge(sem[ready], n)
                st.then(A(E, SS, ACT.Exp, scale=-1.0))
                st.then(A(E, E, ACT.Ln, bias=1.0))
                A(E, E, ACT.Exp, scale=-1.0).then_inc(sem[done], 1)

            def rsqrt(dst, src, scale, ready, n, done):
                act.wait_ge(sem[ready], n)
                st.then(A(dst, src, ACT.Ln, bias=eps[:, 0:1], scale=scale))
                A(dst, dst, ACT.Exp, scale=-0.5).then_inc(sem[done], 1)

            def operand_hi(k, n=S):
                t = bass.ds(k * n, n)
                A(act_hi[:, t], big[:, t], ACT.Copy).then_inc(sem["act_hi"], 1)

            act.dma_start(MEMRAW, memT).then_inc(sem["mem_in"], 16)
            act.dma_start(cst[:, :], consts).then_inc(sem["consts_in"], 16)
            act.dma_start(par[:, :], params).then_inc(sem["consts_in"], 16)
            act.dma_start(big[:, :].rearrange("p (k t) -> p k t", t=S), xT.rearrange("k p t -> p k t")).then_inc(sem["x_in"], 16)
            act.dma_start(wsT[:, :], ws_t).then_inc(sem["consts_in"], 16)
            act.dma_start(bsb[:, :], bs_b).then_inc(sem["consts_in"], 16)
            act.wait_ge(sem["init"], 1)
            act.wait_ge(sem["mem_in"], 16)
            for k in range(KT // 2):
                if k >= 2:
                    act.wait_ge(sem["mem_acc"], k - 1)
                A(tl(k % 2), MEMRAW[:, k * S:(k + 1) * S], ACT.Square).then_inc(sem["mem_sq"], 1)
            hi(0, 0)
            rsqrt(MR[:, 0:MEM], pb[0][:, 0:MEM], 1.0 / D, "mem_ss", 1, "mem_r")
            for k in range(KT):
                c = slice(k * MEM, (k + 1) * MEM)
                act.wait_ge(sem["mem_n"], k + 1)
                A(m_hi[:, c], MEMRAW[:, c], ACT.Copy).then_inc(sem["act_hi"], 1)
            hi(1, 1)
            act.wait_ge(sem["x_in"], 16)
            for u in range(6):
                hi(u + 2, u % 2)
                if u < 4:
                    for k in range(4 * u, 4 * u + 4):
                        if k >= 2:
                            act.wait_ge(sem["x_acc"], k - 1)
                        A(tl(k % 2), big[:, k * S:(k + 1) * S], ACT.Square).then_inc(sem["x_sq"], 1)
                elif u == 5:
                    rsqrt(XR, pb[1][:, :], 1.0 / D, "x_ss", 1, "x_r")
                    with act.Fori(0, KT) as k:
                        act.wait_ge(sem["x_n"], k + 1)
                        operand_hi(k)
            hi(U_AB, U_AB % 2)
            hi(U_AB + 1, (U_AB + 1) % 2)
            act.wait_ge(sem["ab_exp"], 1)
            st.then(A(gate["t"][:, :], gate["t"][:, :], ACT.Exp, scale=-1.0))
            A(gate["t"][:, :], gate["t"][:, :], ACT.Ln, bias=1.0).then_inc(sem["ab_ln"], 1)
            A(small[:, 0:DN], par[:, C_ALOG:C_ALOG + DN], ACT.Exp).then_inc(sem["ab_alog"], 1)
            A(gate["beta"][:, :], gate["beta"][:, :], ACT.Exp, scale=-1.0).then_inc(sem["ab_beta"], 1)
            act.wait_ge(sem["ab_gc"], 1)
            A(gate["ebg"][:, :], gate["gc"][:, :], ACT.Exp)
            A(gate["egl"][:, :], gate["a"][:, :], ACT.Exp)
            A(gate["ekd"][:, :], gate["t"][:, :], ACT.Exp).then_inc(sem["ab_e"], 1)
            hi(U_V + 1, (U_V + 1) % 2)

            def gelu(u, n):
                act.wait_ge(sem["evac"], u + 1)
                A(SQ, Y, ACT.Square).then_inc(sem["ge_sq"], 1)
                act.wait_ge(sem["ge_t"], n)
                st.then(A(E, SQ, ACT.Exp, scale=-GELU_SLOPE))
                st.then(A(E, E, ACT.Ln, bias=1.0))
                A(E, E, ACT.Exp, scale=-1.0).then_inc(sem["ge_sig"], 1)

            with act.Fori(0, GM // 2) as i:
                st.enter(i, 4)
                for j in range(2):
                    u0 = U_V + j
                    hi(2 * i + u0 + 2, u0 % 2)
                    gelu(2 * i + u0, 2 * i + j + 1)
                st.leave(GM // 2)
            with act.Fori(0, GM) as i:
                st.enter(i, 4)
                hi(2 * i + U_ZU + 2, U_ZU % 2)
                sigmoid("z_y", i + 1, "z_sig")
                hi(2 * i + U_ZU + 3, (U_ZU + 1) % 2)
                gelu(2 * i + (U_ZU + 1), GM + i + 1)
                st.leave(GM)
            with act.Fori(0, XA) as i:
                st.enter(i, 2)
                hi(2 * i + U_X + 2, U_X % 2)
                for b in range(2):
                    act.wait_ge(sem["x_max"], 2 * i + b + 1)
                    for c in (2 * b, 2 * b + 1):
                        m = slice((c % 2) * MEM, (c % 2 + 1) * MEM)
                        ins = A(PM[:, c * MEM:(c + 1) * MEM], pb[b][:, m], ACT.Exp, bias=small[:, c:c + 1],
                                accum_out=small[:, 4 + c:5 + c])
                ins.then_inc(sem["x_exp"], 1)
                act.wait_ge(sem["x_tp"], 2 * i + 1)
                A(v3(MVI), v3(MV).rearrange("p (b h) d -> p b h d", h=XA)[:, :, bass.ds(i, 1), :].rearrange("p b h d -> p b (h d)"),
                  ACT.Copy)
                A(PT[:, 0:S], pb[2][:, :], ACT.Copy).then_inc(sem["x_pt"], 1)
                act.wait_ge(sem["x_tp"], 2 * i + 2)
                A(PT[:, S:2 * S], pb[3][:, :], ACT.Copy).then_inc(sem["x_pt"], 1)
                hi(2 * i + U_X + 3, (U_X + 1) % 2)
                sigmoid("xz_y", i + 1, "xz_sig")
                st.leave(XA)

            def tables(h):
                act.wait_ge(sem["gb"], h + 1)
                A(EG, pb[1][:, :], ACT.Exp).then_inc(sem["eg"], 1)
                act.wait_ge(sem["dec_in"], h + 1)
                A(DEC, DEC, ACT.Exp).then_inc(sem["dec_e"], 1)

            def level(h, k):
                act.wait_ge(sem["u_ps"], LEVELS * h + k + 1)
                A(UI, pb[2][:, :], ACT.Copy).then_inc(sem["u_sb"], 1)

            def negated_keys(h):
                act.wait_ge(sem["nk_ps"], h + 1)
                A(NK, pb[4][:, :], ACT.Copy, scale=-1.0).then_inc(sem["nk"], 1)

            def new_values(h):
                for c in range(NB):
                    act.wait_ge(sem["vn_ps"], NB * h + c + 1)
                    A(VN, pb[1][:, 0:P], ACT.Copy).then_inc(sem["vn"], 1)

            def out_norm(h):
                act.wait_ge(sem["o_ps"], h + 1)
                A(OSQ, pb[5][:, :], ACT.Square).then_inc(sem["o_sq"], 1)
                rsqrt(OR, pb[0][:, :], 1.0 / P, "o_ss", h + 1, "o_r")

            def none():
                pass

            def dn_unit(h, j, mid1=none, mid2=none):
                u0 = U_DN + j
                hi(4 * h + u0 + 2, u0 % 2)
                mid1()
                sigmoid("dn_y", 4 * h + j + 1, "dn_sig")
                mid2()
                if j < 2:
                    act.wait_ge(sem["dn_s"], 2 * h + j + 1)
                    A(SQ, SS, ACT.Square).then_inc(sem["dn_sq"], 1)
                    rsqrt(E, pb[0][:, :], 1.0, "dn_ss", 2 * h + j + 1, "dn_r")

            def gmlp_norm():
                for g in range(GM):
                    act.wait_ge(sem["ln_c"], g + 1)
                    A(blk(GSQ, NB * g, NB), blk(GV, NB * g, NB), ACT.Square).then_inc(sem["ln_sq"], 1)
                rsqrt(GR, pb[3][:, :], 1.0 / (GM * P), "ln_m2", 1, "ln_r")
                for g in range(GM):
                    act.wait_ge(sem["ln_tp"], g + 1)
                    A(v3(VTOK)[:, g::GM, :], v3(pb[2 + g % 2][:, :]), ACT.Copy).then_inc(sem["ln_tok"], 1)

            gmlp_norm()
            for j in range(4):
                dn_unit(0, j)
            with act.Fori(1, DN) as h:
                st.enter(h - 1, 4 * 2 + 2 + 1)
                tables(h - 1)
                level(h - 1, 0)
                level(h - 1, 1)
                dn_unit(h, 0, lambda: level(h - 1, 2), lambda: level(h - 1, 3))
                dn_unit(h, 1, lambda: level(h - 1, 4), lambda: level(h - 1, 5))

                def rest():
                    level(h - 1, 6)
                    negated_keys(h - 1)
                    new_values(h - 1)

                dn_unit(h, 2, rest, lambda: out_norm(h - 1))
                dn_unit(h, 3)
                st.leave(DN - 1)
            last = DN - 1
            tables(last)
            for k in range(LEVELS):
                level(last, k)
            negated_keys(last)
            new_values(last)
            out_norm(last)

            act.wait_ge(sem["mixed"], KT)
            act.wait_ge(sem["unit"], U_O1)
            with act.Fori(0, KT) as k:
                operand_hi(k)
            with act.Fori(0, KT // 2) as i:
                for j in range(2):
                    u0 = U_O1 + j
                    n = 2 * i + j + 1
                    hi(2 * i + u0 + 2, u0 % 2)
                    act.wait_ge(sem["evac"], 2 * i + (u0 + 1))
                    act.wait_ge(sem["o1_acc"], n)
                    x1 = big[:, bass.ds((2 * i + j) * S, S)]
                    A(SQ, x1, ACT.Square)
                    A(SS, x1, ACT.Square, scale=par[:, bass.ds(2 * i + j + C_FIN, 1)]).then_inc(sem["o1_sq"], 1)
            rsqrt(R1, pb[0][:, :], 1.0 / D, "o1_ss", 1, "o1_r1")
            rsqrt(R12, R12, 1.0 / D, "o1_t", 1, "o1_r2")
            with act.Fori(0, KT) as k:
                act.wait_ge(sem["x_n"], k + (KT + 1))
                operand_hi(k)

            with act.Fori(0, DN) as h:
                st.enter(h, 2 * NB + 2 + 2 + 2)
                u = 8 * h + U_D2

                def next_hi(j):
                    hi(u + j + 2, (U_D2 + j) % 2)

                for j in range(3):
                    next_hi(j)
                for b in range(NB):
                    lb = LB[:, UP[b]:UP[b] + UN[b]]
                    act.wait_ge(sem["a_z"], NB * h + b + 1)
                    st.then(A(lb, pb[b][:, 0:UN[b]], ACT.Abs))
                    st.then(A(lb, lb, ACT.Exp, scale=-1.0))
                    A(lb, lb, ACT.Ln, bias=1.0).then_inc(sem["a_l"], 1)
                next_hi(3)
                for i, b in enumerate(reversed(range(NB))):
                    wb = WB[:, UP[b]:UP[b] + UN[b]]
                    act.wait_ge(sem["a_diag"], NB * h + i + 1)
                    ins = A(wb[:, 0:P], wb[:, 0:P], ACT.Exp)
                    if UN[b] > P:
                        ins = A(wb[:, P:], pb[b][:, P:UN[b]], ACT.Exp)
                    ins.then_inc(sem["a_w"], 1)
                sigmoid("g_y", 2 * h + 1, "g_sig")
                for j in range(2):
                    next_hi(4 + j)
                    act.wait_ge(sem["evac"], u + (5 + j))
                    A(SQ, Y, ACT.Square).then_inc(sem["b_sq"], 1)
                    rsqrt(E, pb[5][:, :], 1.0 / P, "b_ss", 2 * h + j + 1, "b_r")
                for c in range(NB):
                    pc = PB[:, DO[c]:DO[c] + DNN[c]]
                    act.wait_ge(sem["b_max"], NB * h + c + 1)
                    A(pc, pc, ACT.Exp, bias=small[:, c:c + 1], accum_out=small[:, 4 + c:5 + c]).then_inc(sem["b_exp"], 1)
                next_hi(6)
                act.wait_ge(sem["b_vps"], h + 1)
                A(VBTOK, pb[4][:, :], ACT.Copy).then_inc(sem["b_vtok"], 1)
                for b in range(NB):
                    act.wait_ge(sem["b_tp"], NB * h + b + 1)
                    A(PTB[:, UP[b]:UP[b] + UN[b]], pb[b][:, 0:UN[b]], ACT.Copy).then_inc(sem["b_pt"], 1)
                next_hi(7)
                sigmoid("g_y", 2 * h + 2, "g_sig")
                st.leave(DN)
            act.wait_ge(sem["mixed"], 2 * KT)
            act.wait_ge(sem["unit"], U_O2)
            with act.Fori(0, KT) as k:
                operand_hi(k)
            with act.Fori(0, KT // 2 - 1) as i:
                for j in range(2):
                    u0 = U_O2 + j
                    hi(2 * i + u0 + 2, u0 % 2)

        @block.vector
        def _(dve):
            st = Steps(dve, sem["dve_steps"])
            V = nc.vector

            def lo(u, slot):
                for q in range(4):
                    dve.wait_ge(sem["hi"], 4 * u + (q + 1))
                    c = slice(q * S, (q + 1) * S)
                    V.tensor_tensor(w_lo[slot][:, c], raw[slot][:, c], w_hi[slot][:, c].bitcast(F32), ALU.subtract)\
                        .then_inc(sem["lo"], 1)

            def unit(u):
                dve.wait_ge(sem["unit"], u + 1)

            def operand_lo(k, before):
                t = bass.ds(k * S, S)
                dve.wait_ge(sem["act_hi"], k + (before + 1))
                V.tensor_tensor(act_lo[:, t], big[:, t], act_hi[:, t].bitcast(F32), ALU.subtract).then_inc(sem["act_lo"], 1)

            def chunks(mask):
                return mask.rearrange("p (c t) -> p c t", c=1).broadcast_to([P, NB, P])

            V.memset(eps[:, :], EPS).then_inc(sem["init"], 1)
            st.then(V.memset(SS, 0.0))
            for k in range(KT // 2):
                dve.wait_ge(sem["mem_sq"], k + 1)
                V.tensor_tensor(SS, SS, tl(k % 2), ALU.add).then_inc(sem["mem_acc"], 1)
                dve.wait_ge(sem["mem_acc"], k + 1)
            V.tensor_tensor(SS[:, 0:MEM], SS[:, 0:MEM], SS[:, MEM:2 * MEM], ALU.add).then_inc(sem["mem_acc"], 1)
            lo(0, 0)
            dve.wait_ge(sem["consts_in"], 64)
            dve.wait_ge(sem["mem_r"], 1)
            for k in range(KT):
                m = MEMRAW[:, k * MEM:(k + 1) * MEM]
                V.scalar_tensor_tensor(m, m, par[:, C_MEM + k:C_MEM + k + 1], MR[:, 0:MEM], ALU.mult, ALU.mult)\
                    .then_inc(sem["mem_n"], 1)
            for k in range(KT):
                c = slice(k * MEM, (k + 1) * MEM)
                dve.wait_ge(sem["act_hi"], k + 1)
                V.tensor_tensor(m_lo[:, c], MEMRAW[:, c], m_hi[:, c].bitcast(F32), ALU.subtract).then_inc(sem["act_lo"], 1)
            lo(1, 1)
            st.then(V.tensor_tensor(g2[:, :], par[:, C_FIN:C_FIN + KT], par[:, C_LN2:C_LN2 + KT], ALU.mult))
            st.then(V.memset(SQ, 0.0))
            for u in range(8):
                if u < 7:
                    lo(u + 2, u % 2)
                if u < 4:
                    for k in range(4 * u, 4 * u + 4):
                        dve.wait_ge(sem["x_sq"], k + 1)
                        V.tensor_tensor(SQ, SQ, tl(k % 2), ALU.add).then_inc(sem["x_acc"], 1)
                        dve.wait_ge(sem["x_acc"], k + 1)
                unit(u)
                n = u // 2
                if u % 2 == 0:
                    V.tensor_copy(MK[:, n * MEM:(n + 1) * MEM], bank[0][:, 0:MEM]).then_inc(sem["evac"], 1)
                else:
                    V.tensor_copy(SS[:, 0:MEM], bank[1][:, 0:MEM]).then_inc(sem["evac"], 1)
                    dve.wait_ge(sem["mv_ps"], n + 1)
                    V.tensor_copy(v3(MV)[:, n::XA, :], v3(pb[0][:, 0:MEM])).then_inc(sem["mv_tok"], 1)
                if u == 5:
                    dve.wait_ge(sem["x_r"], 1)
                    with dve.Fori(0, KT) as k:
                        x = big[:, bass.ds(k * S, S)]
                        V.scalar_tensor_tensor(x, x, par[:, bass.ds(k + C_LN, 1)], XR, ALU.mult, ALU.mult)\
                            .then_inc(sem["x_n"], 1)
            with dve.Fori(0, KT) as k:
                operand_lo(k, KT)
            lo(U_AB + 1, (U_AB + 1) % 2)
            unit(U_AB)
            V.tensor_copy(SS, bank[U_AB % 2][:, :]).then_inc(sem["evac"], 1)
            dve.wait_ge(sem["ab_ps"], 1)
            rows = v3(pb[0][:, :])
            gv = gate_v
            bias8 = par[:, C_DT:C_DT + DN].rearrange("p (c h) -> p c h", c=1).broadcast_to([P, NB, DN])
            V.tensor_scalar(gv["beta"], rows[:, :, 32:32 + DN], SILU_FLOOR, None, ALU.max)
            st.then(V.tensor_tensor(gv["a"], rows[:, :, 0:DN], bias8, ALU.add))
            st.then(V.tensor_scalar(gv["g"], gv["a"], -1.0, None, ALU.mult))
            V.tensor_tensor(gv["t"], gv["a"], gv["g"], ALU.max).then_inc(sem["ab_exp"], 1)
            dve.wait_ge(sem["ab_ln"], 1)
            st.then(V.scalar_tensor_tensor(gate["a"][:, :], gate["a"][:, :], 0.0, gate["t"][:, :], ALU.max, ALU.add))
            dve.wait_ge(sem["ab_alog"], 1)
            a8 = small[:, 0:DN].rearrange("p (c h) -> p c h", c=1).broadcast_to([P, NB, DN])
            V.scalar_tensor_tensor(gv["g"], gv["a"], -1.0, a8, ALU.mult, ALU.mult).then_inc(sem["ab_g"], 1)
            dve.wait_ge(sem["ab_beta"], 1)
            st.then(V.tensor_scalar(gate["beta"][:, :], gate["beta"][:, :], 1.0, None, ALU.add))
            st.then(V.reciprocal(gate["beta"][:, :], gate["beta"][:, :]))
            dve.wait_ge(sem["ab_cum"], 1)
            n = NB * DN
            V.tensor_copy(gate["gc"][:, :], pb[0][:, 0:n])
            st.then(V.tensor_copy(gate["a"][:, :], pb[0][:, n:2 * n]))
            V.tensor_tensor(gate["t"][:, :], gate["a"][:, :], gate["gc"][:, :], ALU.subtract).then_inc(sem["ab_gc"], 1)
            dve.wait_ge(sem["ab_e"], 1)
            V.tensor_tensor(gate["ebg"][:, :], gate["ebg"][:, :], gate["beta"][:, :], ALU.mult).then_inc(sem["ab_fin"], 1)
            lo(U_V + 1, (U_V + 1) % 2)

            def gelu(u, slot, n, dst, other=None):
                unit(u)
                V.tensor_copy(Y, bank[slot][:, :]).then_inc(sem["evac"], 1)
                dve.wait_ge(sem["ge_sq"], n)
                st.then(V.tensor_scalar(SQ, SQ, GELU_CUBE, 1.0, ALU.mult, ALU.add))
                st.then(V.tensor_tensor(SQ, SQ, Y, ALU.mult))
                V.tensor_scalar(SQ, SQ, SILU_FLOOR / GELU_SLOPE, None, ALU.max).then_inc(sem["ge_t"], 1)
                dve.wait_ge(sem["ge_sig"], n)
                if other is None:
                    st.then(V.tensor_tensor(dst, Y, E, ALU.mult))
                else:
                    st.then(V.tensor_tensor(Y, Y, E, ALU.mult))
                    st.then(V.tensor_tensor(dst, Y, other, ALU.mult))

            def silu(u, slot, ready, done, n, dst):
                unit(u)
                V.tensor_scalar(SS, bank[slot][:, :], SILU_FLOOR, None, ALU.max).then_inc(sem[ready], 1)
                dve.wait_ge(sem[done], n)
                V.tensor_tensor(dst, bank[slot][:, :], E, ALU.mult).then_inc(sem["evac"], 1)
                dve.wait_ge(sem["evac"], u + 1)

            with dve.Fori(0, GM // 2) as i:
                st.enter(i, 2 * 3)
                for j in range(2):
                    u0 = U_V + j
                    lo(2 * i + u0 + 2, u0 % 2)
                    gelu(2 * i + u0, u0 % 2, 2 * i + j + 1, GV[:, bass.ds((2 * i + j) * S, S)])
                st.leave(GM // 2)
            with dve.Fori(0, GM) as i:
                st.enter(i, 4)
                lo(2 * i + U_ZU + 2, U_ZU % 2)
                silu(2 * i + U_ZU, U_ZU % 2, "z_y", "z_sig", i + 1, CQ)
                lo(2 * i + U_ZU + 3, (U_ZU + 1) % 2)
                gelu(2 * i + U_ZU + 1, (U_ZU + 1) % 2, GM + i + 1, PG[:, bass.ds(i * S, S)], CQ)
                st.leave(GM)
            with dve.Fori(0, XA) as i:
                st.enter(i, 1)
                u = 2 * i + U_X
                lo(u + 2, U_X % 2)
                unit(u)
                V.tensor_scalar(CQ, bank[U_X % 2][:, :], SCALE, None, ALU.mult).then_inc(sem["evac"], 1)
                for b in range(2):
                    dve.wait_ge(sem["x_sc"], 2 * i + b + 1)
                    V.tensor_reduce(small[:, 2 * b:2 * b + 2], pb[b][:, :].rearrange("p (c m) -> p c m", m=MEM),
                                    AX, ALU.max, negate=True).then_inc(sem["x_max"], 1)
                dve.wait_ge(sem["x_exp"], i + 1)
                st.then(V.reciprocal(small[:, 4:8], small[:, 4:8]))
                pm = PM.rearrange("p (c m) -> p c m", m=MEM)
                V.tensor_tensor(pm, pm, small[:, 4:8].rearrange("p (c m) -> p c m", m=1).broadcast_to([P, NB, MEM]),
                                ALU.mult).then_inc(sem["x_p"], 1)
                lo(u + 3, (U_X + 1) % 2)
                silu(u + 1, (U_X + 1) % 2, "xz_y", "xz_sig", i + 1, CZ)
                dve.wait_ge(sem["x_o"], i + 1)
                V.tensor_tensor(big[:, bass.ds((i + GM + DN) * S, S)], pb[4][:, :], CZ, ALU.mult).then_inc(sem["mixed"], 1)
                dve.wait_ge(sem["mixed"], i + 1)
                st.leave(XA)

            dve.wait_ge(sem["ln_m1"], 1)
            st.then(V.tensor_scalar(GMEAN, pb[2][:, :], 1.0 / (GM * P), None, ALU.mult))
            for g in range(GM):
                v = blk(GV, NB * g, NB)
                V.tensor_tensor(v, v, GMEAN, ALU.subtract).then_inc(sem["ln_c"], 1)
            dve.wait_ge(sem["ln_r"], 1)
            for g in range(GM):
                v = blk(GV, NB * g, NB)
                st.then(V.tensor_tensor(v, v, GR, ALU.mult))
                V.tensor_scalar(v, v, par[:, C_GG + g:C_GG + g + 1], par[:, C_GB + g:C_GB + g + 1], ALU.mult, ALU.add)\
                    .then_inc(sem["ln_v"], 1)
            V.tensor_tensor(v3(wsT[:, :]), v3(wsT[:, :]), chunks(C["tri_from"]), ALU.mult).then_inc(sem["sp_w"], 1)
            for g in range(GM):
                dve.wait_ge(sem["sp_o"], g + 1)
                st.then(V.tensor_tensor(v3(GSQ[:, 0:S]), v3(pb[4 + g % 2][:, :]), chunks(blk(bsb[:, :], g)), ALU.add))
                V.tensor_tensor(big[:, g * S:(g + 1) * S], GSQ[:, 0:S], blk(PG, NB * g, NB), ALU.mult).then_inc(sem["mixed"], 1)
                dve.wait_ge(sem["mixed"], XA + g + 1)

            def none():
                pass

            def dn_unit(h, j, mid1=none, mid2=none):
                u0 = U_DN + j
                u = 4 * h + u0
                lo(u + 2, u0 % 2)
                if j == 3:
                    mid1()
                    silu(u, u0 % 2, "dn_y", "dn_sig", 4 * h + j + 1, SZ)
                    return
                unit(u)
                b = bank[u0 % 2][:, :]

                def tap(k):
                    return par[:, bass.ds(12 * h + (C_CONV + 4 * j + k), 1)]

                st.then(V.tensor_scalar(Y, b, tap(3), None, ALU.mult))
                for k in (2, 1):
                    st.then(V.scalar_tensor_tensor(Y[:, 3 - k:], b[:, :S - 3 + k], tap(k), Y[:, 3 - k:], ALU.mult, ALU.add))
                V.scalar_tensor_tensor(Y[:, 3:], b[:, :S - 3], tap(0), Y[:, 3:], ALU.mult, ALU.add).then_inc(sem["evac"], 1)
                dve.wait_ge(sem["evac"], u + 1)
                V.tensor_scalar(SS, Y, SILU_FLOOR, None, ALU.max).then_inc(sem["dn_y"], 1)
                mid1()
                dve.wait_ge(sem["dn_sig"], 4 * h + j + 1)
                if j == 2:
                    V.tensor_tensor(VT, Y, E, ALU.mult).then_inc(sem["dn_n"], 1)
                    mid2()
                    return
                V.tensor_tensor(SS, Y, E, ALU.mult).then_inc(sem["dn_s"], 1)
                mid2()
                dve.wait_ge(sem["dn_r"], 2 * h + j + 1)
                V.scalar_tensor_tensor([QT, KTT][j], SS, SCALE if j == 0 else 1.0, E, ALU.mult, ALU.mult)\
                    .then_inc(sem["dn_n"], 1)

            def tables(h):
                dve.wait_ge(sem["bb"], h + 1)
                V.tensor_tensor(KB, KTT, pb[2][:, :], ALU.mult).then_inc(sem["kb"], 1)
                dve.wait_ge(sem["eg"], h + 1)
                for c in range(NB):
                    ins = V.tensor_scalar(blk(DEC, c), pb[1][:, c * P:(c + 1) * P],
                                          gate["gc"][:, bass.ds(h + DN * c, 1)], 0.0, ALU.subtract, ALU.min)
                ins.then_inc(sem["dec_in"], 1)
                V.tensor_tensor(QG, QT, EG, ALU.mult).then_inc(sem["qg"], 1)
                dve.wait_ge(sem["dec_e"], h + 1)
                st.then(V.tensor_tensor(v3(DEC), v3(DEC), chunks(C["tri_from"]), ALU.mult))
                dve.wait_ge(sem["kk"], 2 * h + 1)
                V.tensor_tensor(AT, pb[3][:, :], DEC, ALU.mult).then_inc(sem["at"], 1)
                dve.wait_ge(sem["kk"], 2 * h + 2)
                V.tensor_tensor(AI, pb[4][:, :], DEC, ALU.mult).then_inc(sem["ai"], 1)

                def col(name):
                    return gate_v[name][:, :, bass.ds(h, 1)].broadcast_to([P, NB, P])

                dve.wait_ge(sem["tp"], 2 * h + 1)
                V.tensor_tensor(v3(KBG), v3(pb[5][:, :]), col("ebg"), ALU.mult)
                V.tensor_tensor(v3(KDEC), v3(pb[5][:, :]), col("ekd"), ALU.mult)
                dve.wait_ge(sem["tp"], 2 * h + 2)
                V.tensor_tensor(v3(VB), v3(pb[1][:, :]), col("beta"), ALU.mult).then_inc(sem["kbg"], 1)

            def level(h, k):
                n = LEVELS * h + (k + 1)
                if k == 0:
                    dve.wait_ge(sem["m_lvl"], n)
                    V.tensor_tensor(v3(YI), chunks(C["ident"]), v3(blk(ML, 0, NB)), ALU.subtract)
                    dve.wait_ge(sem["u_sb"], n)
                    V.tensor_tensor(v3(XI), chunks(C["ident"]), v3(UI), ALU.subtract).then_inc(sem["xy"], 1)
                    return
                dve.wait_ge(sem["w_ps"], (LEVELS - 1) * h + k)
                if k < LEVELS - 1:
                    V.tensor_tensor(XI, XI, pb[3][:, :], ALU.subtract)
                V.tensor_tensor(YI, YI, pb[4][:, :], ALU.subtract).then_inc(sem["xy"], 1)

            def states(h):
                for c in range(NB - 1):
                    dve.wait_ge(sem["s_ps"], (NB - 1) * h + c + 1)
                    if c == 0:
                        V.tensor_copy(ST, pb[3][:, 0:P]).then_inc(sem["st"], 1)
                    else:
                        V.scalar_tensor_tensor(ST, ST, gate["egl"][:, bass.ds(h + DN * c, 1)], pb[3][:, 0:P],
                                               ALU.mult, ALU.add).then_inc(sem["st"], 1)
                    dve.wait_ge(sem["st"], (NB - 1) * h + c + 1)

            def head_out(h):
                dve.wait_ge(sem["o_r"], h + 1)
                st.then(V.scalar_tensor_tensor(OSQ, pb[5][:, :], par[:, C_DNG:C_DNG + 1], OR, ALU.mult, ALU.mult))
                V.tensor_tensor(big[:, bass.ds((h + GM) * S, S)], OSQ, SZ, ALU.mult).then_inc(sem["mixed"], 1)
                dve.wait_ge(sem["mixed"], h + (GM + XA + 1))

            for j in range(4):
                dn_unit(0, j)
            with dve.Fori(1, DN) as h:
                st.enter(h - 1, 3 * 3 + 1 + 1)
                tables(h - 1)
                level(h - 1, 0)
                level(h - 1, 1)
                dn_unit(h, 0, lambda: level(h - 1, 2), lambda: level(h - 1, 3))
                dn_unit(h, 1, lambda: level(h - 1, 4), lambda: level(h - 1, 5))

                def rest():
                    level(h - 1, 6)
                    states(h - 1)

                dn_unit(h, 2, rest)
                dn_unit(h, 3, lambda: head_out(h - 1))
                st.leave(DN - 1)
            last = DN - 1
            tables(last)
            for k in range(LEVELS):
                level(last, k)
            states(last)
            head_out(last)

            with dve.Fori(0, KT) as k:
                operand_lo(k, 2 * KT)
            V.memset(ACC1, 0.0)
            V.memset(ACC2, 0.0).then_inc(sem["o1_acc"], 1)
            with dve.Fori(0, KT // 2) as i:
                for j in range(2):
                    u0 = U_O1 + j
                    n = 2 * i + j + 1
                    lo(2 * i + u0 + 2, u0 % 2)
                    unit(2 * i + u0)
                    dve.wait_ge(sem[f"o1_x{j}"], 16 * i + 16)
                    V.tensor_tensor(big[:, bass.ds((2 * i + j) * S, S)], bank[u0 % 2][:, :], blk(XIN, NB * j, NB), ALU.add)\
                        .then_inc(sem["evac"], 1)
                    dve.wait_ge(sem["o1_sq"], n)
                    dve.wait_ge(sem["o1_acc"], n)
                    V.tensor_tensor(ACC1, ACC1, SQ, ALU.add)
                    V.tensor_tensor(ACC2, ACC2, SS, ALU.add).then_inc(sem["o1_acc"], 1)
            dve.wait_ge(sem["o1_r1"], 1)
            st.then(V.tensor_tensor(R12, R1, R1, ALU.mult))
            dve.wait_ge(sem["o1_ss"], 2)
            V.tensor_tensor(R12, R12, pb[1][:, :], ALU.mult).then_inc(sem["o1_t"], 1)
            dve.wait_ge(sem["o1_r2"], 1)
            V.tensor_tensor(R12, R12, R1, ALU.mult).then_inc(sem["o1_r12"], 1)
            dve.wait_ge(sem["o1_r12"], 1)
            dve.wait_ge(sem["o1_st"], 16 * KT)
            with dve.Fori(0, KT) as k:
                x = big[:, bass.ds(k * S, S)]
                V.scalar_tensor_tensor(x, x, g2[:, bass.ds(k, 1)], R12, ALU.mult, ALU.mult).then_inc(sem["x_n"], 1)
                dve.wait_ge(sem["x_n"], k + (KT + 1))
                operand_lo(k, 3 * KT)

            with dve.Fori(0, DN) as h:
                st.enter(h, NB + 1 + 1 + NB)
                u = 8 * h + U_D2

                def slot(j):
                    return (U_D2 + j) % 2

                def next_lo(j):
                    lo(u + j + 2, slot(j))

                for j, dst in enumerate((QA, KA, VA)):
                    next_lo(j)
                    unit(u + j)
                    V.tensor_scalar(dst, bank[slot(j)][:, :], SCALE if j == 0 else 1.0, None, ALU.mult).then_inc(sem["evac"], 1)
                dve.wait_ge(sem["a_vps"], h + 1)
                V.tensor_copy(VATOK, pb[4][:, :]).then_inc(sem["a_vtok"], 1)
                for b in range(NB):
                    spb = SPB[:, UP[b]:UP[b] + UN[b]]
                    dve.wait_ge(sem["a_l"], NB * h + b + 1)
                    st.then(V.scalar_tensor_tensor(spb, pb[b][:, 0:UN[b]], 0.0, LB[:, UP[b]:UP[b] + UN[b]], ALU.max, ALU.add))
                    V.tensor_tensor(spb[:, 0:P], spb[:, 0:P], C["strict"], ALU.mult).then_inc(sem["a_sp"], 1)
                next_lo(3)
                for i, b in enumerate(reversed(range(NB))):
                    dve.wait_ge(sem["a_cum"], NB * h + i + 1)
                    V.scalar_tensor_tensor(WB[:, UP[b]:UP[b] + P], pb[b][:, 0:P], 0.0, C["hide"], ALU.min, ALU.add)\
                        .then_inc(sem["a_diag"], 1)
                silu(u + 3, slot(3), "g_y", "g_sig", 2 * h + 1, SGA)
                for j in range(2):
                    next_lo(4 + j)
                    unit(u + 4 + j)
                    V.tensor_copy(Y, bank[slot(4 + j)][:, :]).then_inc(sem["evac"], 1)
                    if j == 0:
                        dve.wait_ge(sem["a_o"], h + 1)
                        V.tensor_tensor(big[:, bass.ds(h * S, S)], pb[4][:, :], SGA, ALU.mult).then_inc(sem["mixed"], 1)
                        dve.wait_ge(sem["mixed"], 2 * h + (KT + 1))
                    dve.wait_ge(sem["b_r"], 2 * h + j + 1)
                    if j == 0:
                        st.then(V.tensor_scalar(QB, Y, par[:, C_QG:C_QG + 1], SCALE, ALU.mult, ALU.mult))
                        V.tensor_tensor(QB, QB, E, ALU.mult).then_inc(sem["b_n"], 1)
                    else:
                        V.scalar_tensor_tensor(KBN, Y, par[:, C_KG:C_KG + 1], E, ALU.mult, ALU.mult).then_inc(sem["b_n"], 1)
                dve.wait_ge(sem["b_bias"], 16 * h + 16)
                st.then(V.memset(BIAS[0:64, S - 64:S], NEG))
                for c in range(NB):
                    pc = PB[:, DO[c]:DO[c] + DNN[c]]
                    dve.wait_ge(sem["b_sc"], NB * h + c + 1)
                    V.tensor_tensor(pc, pb[c][:, 0:DNN[c]], BIAS[:, S - DNN[c]:S], ALU.add).then_inc(sem["b_add"], 1)
                    dve.wait_ge(sem["b_add"], NB * h + c + 1)
                    V.tensor_reduce(small[:, c:c + 1], pc, AX, ALU.max, negate=True).then_inc(sem["b_max"], 1)
                next_lo(6)
                unit(u + 6)
                V.tensor_copy(VBT, bank[slot(6)][:, :]).then_inc(sem["evac"], 1)
                for c in range(NB):
                    pc = PB[:, DO[c]:DO[c] + DNN[c]]
                    dve.wait_ge(sem["b_exp"], NB * h + c + 1)
                    st.then(V.reciprocal(small[:, 4 + c:5 + c], small[:, 4 + c:5 + c]))
                    V.tensor_scalar(pc, pc, small[:, 4 + c:5 + c], None, ALU.mult).then_inc(sem["b_p"], 1)
                next_lo(7)
                silu(u + 7, slot(7), "g_y", "g_sig", 2 * h + 2, SGB)
                dve.wait_ge(sem["b_o"], h + 1)
                V.tensor_tensor(big[:, bass.ds((h + DN) * S, S)], pb[4][:, :], SGB, ALU.mult).then_inc(sem["mixed"], 1)
                dve.wait_ge(sem["mixed"], 2 * h + (KT + 2))
                st.leave(DN)
            with dve.Fori(0, KT) as k:
                operand_lo(k, 4 * KT)

            def out_tile(i, j, more=True):
                u0 = U_O2 + j
                n = 2 * i + j + 1
                if more:
                    lo(2 * i + u0 + 2, u0 % 2)
                dve.wait_ge(sem[f"o2_x{j}"], 16 * i + 16)
                dve.wait_ge(sem["evac"], 2 * i + u0)
                V.scalar_tensor_tensor(X2, blk(XIN, NB * j, NB), par[:, bass.ds(2 * i + j + C_FIN, 1)], R1, ALU.mult, ALU.mult)\
                    .then_inc(sem["o2_xf"], 1)
                dve.wait_ge(sem["o2_xf"], n)
                unit(2 * i + u0)
                V.tensor_tensor(blk(OUTS, NB * j, NB), bank[u0 % 2][:, :], X2, ALU.add)\
                    .then_inc(sem["evac"], 1)

            for j in range(2):
                out_tile(0, j)
            with dve.Fori(1, KT // 2 - 1) as i:
                for j in range(2):
                    dve.wait_ge(sem[f"o2_st{j}"], 16 * i)
                    out_tile(i, j)
            for j in range(2):
                dve.wait_ge(sem[f"o2_st{j}"], 16 * (KT // 2 - 1))
                out_tile(KT // 2 - 1, j, False)

        @block.tensor
        def _(pe):
            def mm(out, a, b, start=True, stop=True, skip=False):
                return nc.tensor.matmul(out, a, b, start=start, stop=stop, skip_group_check=skip)

            def tp(out, a):
                return nc.tensor.transpose(out, a, C["ident"])

            def gemm(u, slot, k0=0, k1=KT, before=None, mem=False):
                out = bank[slot][:, 0:MEM] if mem else bank[slot][:, :]
                if k0 == 0 and not mem:
                    pe.wait_ge(sem["evac"], u - 1)
                for k in range(k0, k1):
                    if k % 4 == 0:
                        pe.wait_ge(sem["hi"], 4 * u + (k // 4 + 1))
                        pe.wait_ge(sem["lo"], 4 * u + (k // 4 + 1))
                    if before is not None:
                        pe.wait_ge(sem["act_hi"], before + k + 1)
                        pe.wait_ge(sem["act_lo"], before + k + 1)
                    n = MEM if mem else S
                    ah, al = [m_hi, m_lo] if mem else [act_hi[:, :], act_lo[:, :]]
                    ah, al = ah[:, k * n:(k + 1) * n], al[:, k * n:(k + 1) * n]
                    wh, wl = w_hi[slot][:, k * P:(k + 1) * P], w_lo[slot][:, k * P:(k + 1) * P]
                    mm(out, wh, ah, k == 0, False)
                    mm(out, wh, al, False, False)
                    ins = mm(out, wl, ah, False, k == KT - 1)
                if k1 == KT:
                    ins.then_inc(sem["unit"], 1)

            pe.wait_ge(sem["consts_in"], 64)
            pe.wait_ge(sem["mem_acc"], KT // 2 + 1)
            mm(pb[0][:, 0:MEM], C["ones"], SS[:, 0:MEM]).then_inc(sem["mem_ss"], 1)
            pe.wait_ge(sem["act_lo"], KT)

            def mem_pair(i):
                gemm(2 * i, 0, mem=True)
                gemm(2 * i + 1, 1, mem=True)
                pe.wait_ge(sem["evac"], 2 * i + 2)
                for b in range(2):
                    ins = tp(pb[0][:, b * P:(b + 1) * P], SS[:, b * P:(b + 1) * P])
                ins.then_inc(sem["mv_ps"], 1)

            with pe.Fori(0, XA - 1) as i:
                mem_pair(i)
            pe.wait_ge(sem["x_acc"], KT)
            mm(pb[1][:, :], C["ones"], SQ).then_inc(sem["x_ss"], 1)
            mem_pair(XA - 1)
            gemm(U_AB, U_AB % 2, before=KT)
            gemm(U_V, U_V % 2, 0, 4)
            pe.wait_ge(sem["evac"], U_AB + 1)
            pe.wait_ge(sem["mv_tok"], XA)
            for c in range(NB):
                ins = tp(pb[0][:, c * P:(c + 1) * P], blk(SS, c))
            ins.then_inc(sem["ab_ps"], 1)
            gemm(U_V, U_V % 2, 4, 14)
            pe.wait_ge(sem["ab_g"], 1)
            n = NB * DN
            mm(pb[0][:, 0:n], C["tri_from"], gate["g"][:, :])
            mm(pb[0][:, n:2 * n], C["ones"], gate["g"][:, :]).then_inc(sem["ab_cum"], 1)
            gemm(U_V, U_V % 2, 14, KT)
            gemm(U_V + 1, (U_V + 1) % 2)
            with pe.Fori(1, (GM + 2 * GM) // 2) as i:
                for j in range(2):
                    gemm(2 * i + (U_V + j), (U_V + j) % 2)
            with pe.Fori(0, XA) as i:
                u = 2 * i + U_X
                z = (U_X + 1) % 2
                gemm(u, U_X % 2)
                gemm(u + 1, z, 0, 4)
                pe.wait_ge(sem["evac"], u + 1)
                for c in range(NB):
                    ins = mm(pb[c // 2][:, (c % 2) * MEM:(c % 2 + 1) * MEM], blk(CQ, c), MK[:, bass.ds(i * MEM, MEM)])
                    if c % 2:
                        ins.then_inc(sem["x_sc"], 1)
                gemm(u + 1, z, 4, 13)
                pe.wait_ge(sem["x_p"], i + 1)
                for b in range(2):
                    for c in range(NB):
                        ins = tp(pb[2 + b][:, c * P:(c + 1) * P], PM[:, c * MEM + b * P:c * MEM + (b + 1) * P])
                    ins.then_inc(sem["x_tp"], 1)
                gemm(u + 1, z, 13, KT)
                pe.wait_ge(sem["x_pt"], 2 * i + 2)
                mm(pb[4][:, :], MVI[:, 0:P], PT[:, 0:S], True, False)
                mm(pb[4][:, :], MVI[:, P:2 * P], PT[:, S:2 * S], False, True).then_inc(sem["x_o"], 1)

            def norm_sum(h, j):
                pe.wait_ge(sem["dn_sq"], 2 * h + j + 1)
                mm(pb[0][:, :], C["ones"], SQ).then_inc(sem["dn_ss"], 1)

            def dn_gemm(h, j, k0, k1):
                gemm(4 * h + (U_DN + j), (U_DN + j) % 2, k0, k1)

            dn_gemm(0, 0, 0, 1)
            for g in range(GM):
                ins = mm(pb[2][:, :], C["ones"], blk(GV, NB * g, NB), g == 0, g == GM - 1)
            ins.then_inc(sem["ln_m1"], 1)
            dn_gemm(0, 0, 1, 8)
            for g in range(GM):
                pe.wait_ge(sem["ln_sq"], g + 1)
                ins = mm(pb[3][:, :], C["ones"], blk(GSQ, NB * g, NB), g == 0, g == GM - 1)
            ins.then_inc(sem["ln_m2"], 1)
            dn_gemm(0, 0, 8, KT)
            for g in range(GM):
                pe.wait_ge(sem["ln_v"], g + 1)
                if g == 1:
                    pe.wait_ge(sem["ln_r"], 1)
                if g >= 2:
                    pe.wait_ge(sem["ln_tok"], g - 1)
                for c in range(NB):
                    ins = tp(pb[2 + g % 2][:, c * P:(c + 1) * P], blk(GV, NB * g + c))
                ins.then_inc(sem["ln_tp"], 1)
            pe.wait_ge(sem["sp_w"], 1)
            for g in range(GM):
                pe.wait_ge(sem["ln_tok"], g + 1)
                if g == 0:
                    pe.wait_ge(sem["mixed"], XA)
                if g >= 2:
                    pe.wait_ge(sem["mixed"], XA + g - 1)
                for c in range(NB):
                    ins = mm(pb[4 + g % 2][:, c * P:(c + 1) * P], blk(VTOK, c * GM + g), blk(wsT[:, :], g))
                ins.then_inc(sem["sp_o"], 1)
            for j in range(2):
                dn_gemm(0, j + 1, 0, 13)
                norm_sum(0, j)
                dn_gemm(0, j + 1, 13, KT)
            dn_gemm(0, 3, 0, KT)

            def gate_rows(h):
                pe.wait_ge(sem["sel"], h + 1)
                for c in range(NB):
                    ins = mm(pb[1][:, c * P:(c + 1) * P], blk(GSEL, c), C["tri_from"])
                ins.then_inc(sem["gb"], 1)
                for c in range(NB):
                    ins = mm(pb[2][:, c * P:(c + 1) * P], blk(BSEL, c), C["ident"])
                ins.then_inc(sem["bb"], 1)

            def products(h):
                pe.wait_ge(sem["kb"], h + 1)
                for c in range(NB):
                    ins = mm(pb[3][:, c * P:(c + 1) * P], blk(KTT, c), blk(KB, c))
                ins.then_inc(sem["kk"], 1)
                for c in range(NB):
                    ins = mm(pb[4][:, c * P:(c + 1) * P], blk(KTT, c), blk(QT, c))
                ins.then_inc(sem["kk"], 1)
                for c in range(NB):
                    ins = tp(pb[5][:, c * P:(c + 1) * P], blk(KTT, c))
                ins.then_inc(sem["tp"], 1)
                pe.wait_ge(sem["dec_in"], h + 1)
                for c in range(NB):
                    ins = tp(pb[1][:, c * P:(c + 1) * P], blk(VT, c))
                ins.then_inc(sem["tp"], 1)

            def level_u(h, k):
                pe.wait_ge(sem["m_lvl"], LEVELS * h + (k + 1))
                if k:
                    pe.wait_ge(sem["xy"], LEVELS * h + k)
                m = blk(ML, NB * (k % 2), NB)
                for c in range(NB):
                    x = blk(XI, c) if k else C["ident"]
                    ins = mm(pb[2][:, c * P:(c + 1) * P], blk(m, c), x)
                ins.then_inc(sem["u_ps"], 1)

            def level_w(h, k):
                pe.wait_ge(sem["u_sb"], LEVELS * h + (k + 1))
                for c in range(NB):
                    if k < LEVELS - 1:
                        mm(pb[3][:, c * P:(c + 1) * P], blk(YI, c), blk(UI, c))
                    ins = mm(pb[4][:, c * P:(c + 1) * P], blk(UI, c), blk(YI, c))
                ins.then_inc(sem["w_ps"], 1)

            def negated_keys(h):
                pe.wait_ge(sem["xy"], LEVELS * (h + 1))
                pe.wait_ge(sem["kbg"], h + 1)
                for c in range(NB):
                    ins = mm(pb[4][:, c * P:(c + 1) * P], blk(KBG, c), blk(YI, c))
                ins.then_inc(sem["nk_ps"], 1)

            def new_values(h, c):
                v = pb[1][:, 0:P]
                if c:
                    pe.wait_ge(sem["st"], (NB - 1) * h + c)
                else:
                    pe.wait_ge(sem["nk"], h + 1)
                ins = mm(v, blk(YI, c), blk(VB, c), True, c == 0)
                if c:
                    ins = mm(v, blk(NK, c), ST, False, True)
                ins.then_inc(sem["vn_ps"], 1)

            def chunk_out(h, c):
                o = pb[5][:, c * P:(c + 1) * P]
                pe.wait_ge(sem["vn"], NB * h + c + 1)
                ins = mm(o, VN, blk(AI, c), True, c == 0)
                if c:
                    ins = mm(o, ST, blk(QG, c), False, True)
                if c == NB - 1:
                    ins.then_inc(sem["o_ps"], 1)
                else:
                    mm(pb[3][:, 0:P], blk(KDEC, c), VN).then_inc(sem["s_ps"], 1)

            def out_sum(h):
                pe.wait_ge(sem["o_sq"], h + 1)
                mm(pb[0][:, :], C["ones"], OSQ).then_inc(sem["o_ss"], 1)

            with pe.Fori(1, DN) as h:
                p = h - 1
                dn_gemm(h, 0, 0, 1)
                gate_rows(p)
                dn_gemm(h, 0, 1, 4)
                products(p)
                dn_gemm(h, 0, 4, 9)
                level_u(p, 0)
                dn_gemm(h, 0, 9, 12)
                level_u(p, 1)
                dn_gemm(h, 0, 12, 14)
                level_w(p, 1)
                dn_gemm(h, 0, 14, KT)
                for j, k in ((1, 2), (2, 4)):
                    dn_gemm(h, j, 0, 1)
                    level_u(p, k)
                    dn_gemm(h, j, 1, 4)
                    level_w(p, k)
                    dn_gemm(h, j, 4, 9)
                    level_u(p, k + 1)
                    dn_gemm(h, j, 9, 11)
                    level_w(p, k + 1)
                    dn_gemm(h, j, 11, 14)
                    norm_sum(h, j - 1)
                    dn_gemm(h, j, 14, KT)
                dn_gemm(h, 3, 0, 1)
                level_u(p, 6)
                dn_gemm(h, 3, 1, 3)
                level_w(p, 6)
                dn_gemm(h, 3, 3, 4)
                negated_keys(p)
                dn_gemm(h, 3, 4, 5)
                for c in range(NB):
                    new_values(p, c)
                    dn_gemm(h, 3, 5 + 2 * c, 6 + 2 * c)
                    chunk_out(p, c)
                    dn_gemm(h, 3, 6 + 2 * c, 7 + 2 * c)
                dn_gemm(h, 3, 13, 15)
                out_sum(p)
                dn_gemm(h, 3, 15, KT)
            last = DN - 1
            gate_rows(last)
            products(last)
            level_u(last, 0)
            for k in range(1, LEVELS):
                level_u(last, k)
                level_w(last, k)
            negated_keys(last)
            for c in range(NB):
                new_values(last, c)
                chunk_out(last, c)
            out_sum(last)

            def projection(u0, before, pairs):
                for j in range(2):
                    gemm(u0 + j, (u0 + j) % 2, before=before if j == 0 else None)
                with pe.Fori(1, pairs) as i:
                    for j in range(2):
                        gemm(2 * i + (u0 + j), (u0 + j) % 2)

            projection(U_O1, 2 * KT, KT // 2)
            pe.wait_ge(sem["o1_acc"], KT + 1)
            mm(pb[0][:, :], C["ones"], ACC1).then_inc(sem["o1_ss"], 1)
            mm(pb[1][:, :], C["ones"], ACC2).then_inc(sem["o1_ss"], 1)

            with pe.Fori(0, DN) as h:
                u = 8 * h + U_D2

                def d2(j, k0=0, k1=KT):
                    gemm(u + j, (U_D2 + j) % 2, k0, k1, before=3 * KT if j == 0 else None)

                d2(0)
                d2(1)
                d2(2)
                d2(3, 0, 2)
                pe.wait_ge(sem["evac"], u + 3)
                for c in range(NB):
                    ins = tp(pb[4][:, c * P:(c + 1) * P], blk(VA, c))
                ins.then_inc(sem["a_vps"], 1)
                for b in range(NB):
                    mm(pb[b][:, 0:UN[b]], blk(KA, b), QA[:, b * P:S], True, True).then_inc(sem["a_z"], 1)
                d2(3, 2)
                d2(4, 0, 3)
                for i, b in enumerate(reversed(range(NB))):
                    pe.wait_ge(sem["a_sp"], NB * h + b + 1)
                    if i == 0:
                        pe.wait_ge(sem["a_sp"], NB * h + NB)
                    ins = mm(pb[b][:, 0:UN[b]], C["neg_tri"], SPB[:, UP[b]:UP[b] + UN[b]], False, b == NB - 1, skip=True)
                    for later in range(b + 1, NB):
                        ins = mm(pb[b][:, (later - b) * P:UN[b]], C["neg_ones"], SPB[:, UP[later]:UP[later] + UN[later]],
                                 False, later == NB - 1, skip=True)
                    ins.then_inc(sem["a_cum"], 1)
                d2(4, 3, 12)
                pe.wait_ge(sem["a_w"], NB * h + NB)
                pe.wait_ge(sem["a_vtok"], h + 1)
                for b in range(NB):
                    ins = mm(pb[4][:, b * P:S], blk(VATOK, b), WB[:, UP[b]:UP[b] + UN[b]], b == 0, b == NB - 1, skip=True)
                ins.then_inc(sem["a_o"], 1)
                d2(4, 12)
                for j in range(2):
                    d2(5 + j, 0, 8)
                    pe.wait_ge(sem["b_sq"], 2 * h + j + 1)
                    mm(pb[5][:, :], C["ones"], SQ).then_inc(sem["b_ss"], 1)
                    d2(5 + j, 8, 12)
                    if j == 1:
                        pe.wait_ge(sem["b_n"], 2 * h + 2)
                        for c in range(NB):
                            mm(pb[c][:, 0:DNN[c]], blk(QB, c), KBN[:, 0:DNN[c]]).then_inc(sem["b_sc"], 1)
                    d2(5 + j, 12)
                d2(7, 0, 6)
                pe.wait_ge(sem["evac"], u + 7)
                pe.wait_ge(sem["mixed"], 2 * h + (KT + 1))
                for c in range(NB):
                    ins = tp(pb[4][:, c * P:(c + 1) * P], blk(VBT, c))
                ins.then_inc(sem["b_vps"], 1)
                d2(7, 6, 12)
                pe.wait_ge(sem["b_p"], NB * h + NB)
                for b in range(NB):
                    for c in range(b, NB):
                        ins = tp(pb[b][:, (c - b) * P:(c - b + 1) * P], PB[:, DO[c] + b * P:DO[c] + (b + 1) * P])
                    ins.then_inc(sem["b_tp"], 1)
                d2(7, 12)
                pe.wait_ge(sem["b_vtok"], h + 1)
                pe.wait_ge(sem["b_pt"], NB * h + NB)
                for b in range(NB):
                    ins = mm(pb[4][:, b * P:S], blk(VBTOK, b), PTB[:, UP[b]:UP[b] + UN[b]], b == 0, b == NB - 1, skip=True)
                ins.then_inc(sem["b_o"], 1)
            projection(U_O2, 4 * KT, KT // 2)


def constants():
    j, i = np.meshgrid(np.arange(P), np.arange(P), indexing="ij")
    m = {"ident": i == j, "ones": i >= 0, "tri_from": i >= j, "neg_tri": -1.0 * (j >= i), "neg_ones": -1.0 * (i >= 0),
         "strict": i > j, "hide": np.where(i > j, 0.0, NEG)}
    for k in range(LEVELS):
        m[f"level{k}"] = (i >> k == (j >> k) + 1) & ((j >> k) % 2 == 0)
    return np.concatenate([m[n].astype(np.float32) for n in CONSTS], axis=1)


def kernel(**inputs):
    import concourse.bacc as bacc
    from concourse.bass_utils import run_bass_kernel_spmd

    f = {n: np.asarray(a) for n, a in inputs.items()}

    def tiles(m):
        return m.reshape(KT, P, -1, P).transpose(2, 1, 0, 3).reshape(-1, P, KT * P)

    w1 = f["w_in"][0]
    gm, dn, xa = GM * P, DN * P, XA * P
    at = np.cumsum([0, gm, gm, gm, dn, dn, dn, dn, DN, DN, xa, xa])
    gu, gv_, gz, dq, dk, dv, dz, da, db, cq, cz = (w1[:, at[i]:at[i + 1]] for i in range(11))
    ab = np.zeros((D, P), np.float32)
    ab[:, 0:DN] = da
    ab[:, 32:32 + DN] = db

    def interleave(*parts):
        t = [tiles(p) for p in parts]
        return np.stack(t, axis=1).reshape(-1, P, KT * P)

    kv = f["w_mem_kv"][0]
    w2 = f["w_in_2"][0]
    w = np.concatenate([
        interleave(kv[:, :xa], kv[:, xa:]), tiles(ab), tiles(gv_), interleave(gz, gu), interleave(cq, cz),
        interleave(dq, dk, dv, dz), tiles(f["w_out"][0]),
        interleave(*(w2[:, i * dn:(i + 1) * dn] for i in range(8))), tiles(f["w_out_2"][0])])
    assert w.shape[0] == U_END

    def cols(v):
        return v.reshape(-1, P).T

    conv = f["conv_w"][0].reshape(4, 3, DN, P).transpose(3, 2, 1, 0).reshape(P, DN * 3 * 4)
    params = np.concatenate([
        cols(f["ln_g"][0]), cols(f["mem_norm_g"][0]), cols(f["final_g"]), cols(f["norm_g_2"][0]),
        cols(f["gmlp_ln_g"][0]), cols(f["gmlp_ln_b"][0]), conv, cols(f["dn_norm_g"][0]), cols(f["q_norm_g_2"][0]),
        cols(f["k_norm_g_2"][0]), np.broadcast_to(f["dn_a_log"][0], (P, DN)), np.broadcast_to(f["dn_dt_bias"][0], (P, DN))],
        axis=1)
    p, x = np.arange(P)[:, None], np.arange(S)[None, :]
    rel = f["rel_bias_2"][0][:, np.clip(p - x + (S - P), -63, 256) + 63]
    arrays = {
        "w": w,
        "xT": f["x"][0].T.reshape(KT, P, S),
        "memT": f["mem"][0].T.reshape(KT, P, MEM).transpose(1, 0, 2).reshape(P, KT * MEM),
        "consts": constants(),
        "params": params,
        "ws_t": f["gmlp_ws"][0].transpose(2, 0, 1).reshape(P, GM * P),
        "bs_b": np.broadcast_to(f["gmlp_bs"][0].reshape(1, GM * P), (P, GM * P)),
        "rel": rel,
    }
    arrays = {n: np.ascontiguousarray(a) for n, a in arrays.items()}
    nc = bacc.Bacc("TRN2", target_bir_lowering=False, num_devices=1, dynamic_dma_scratch_size=4096)
    args = [nc.dram_tensor(f"in_{n}", a.shape, F32, kind="ExternalInput").ap() for n, a in arrays.items()]
    x1 = nc.dram_tensor("x1", (KT, P, S), F32, kind="Internal").ap()
    out = nc.dram_tensor("outT", (KT, P, S), F32, kind="ExternalOutput").ap()
    build(nc, *args, x1, out)
    r = run_bass_kernel_spmd(nc, [{f"in_{n}": a for n, a in arrays.items()}], core_ids=[0])
    return r.results[0]["outT"].reshape(1, D, S).transpose(0, 2, 1)
```

```python
from contextlib import ExitStack

import numpy as np

import concourse.bass as bass
from concourse import mybir

P = 128
S = 512
D = 2048
KT = D // P
NB = S // P
EPS = 1e-6
SCALE = float(P) ** -0.5
NEG = -1e30
GM, DN, XA, MEM = 4, 8, 4, 256
SILU_FLOOR = -40.0
GELU_CUBE = 0.044715
GELU_SLOPE = 2.0 * (2.0 / 3.141592653589793) ** 0.5

U_MEM = 0
U_AB = U_MEM + 2 * XA
U_V = U_AB + 1
U_X = U_V + GM
U_DN = U_X + 2 * XA
U_ZU = U_DN + 4 * DN
U_O1 = U_ZU + 2 * GM
U_D2 = U_O1 + KT
U_O2 = U_D2 + 8 * DN
U_END = U_O2 + KT
M1 = XA + DN

CONSTS = ["ident", "ones", "tri_from", "neg_tri", "neg_ones", "strict", "hide"] + [f"level{k}" for k in range(7)]
LEVELS = 7
C_LN, C_MEM, C_FIN, C_LN2 = 0, KT, 2 * KT, 3 * KT
C_GG, C_GB = 4 * KT, 4 * KT + GM
C_CONV = C_GB + GM
C_DNG = C_CONV + DN * 3 * 4
C_QG, C_KG = C_DNG + 1, C_DNG + 2
C_ALOG, C_DT = C_DNG + 3, C_DNG + 3 + DN
C_ALL = C_DT + DN

F32 = mybir.dt.float32
F32R = mybir.dt.float32r
ACT = mybir.ActivationFunctionType
ALU = mybir.AluOpType
AX = mybir.AxisListType.X


class Steps:

    def __init__(self, eng, sem):
        self.eng, self.sem, self.base, self.n = eng, sem, 0, 0

    def then(self, ins):
        self.n += 1
        ins.then_inc(self.sem, 1)
        self.eng.wait_ge(self.sem, self.base + self.n)

    def enter(self, i, per):
        self.start, self.per = self.n + self.base, per
        self.base, self.n = self.start + i * per, 0

    def leave(self, times):
        assert self.n == self.per, (self.n, self.per)
        self.base, self.n = self.start + times * self.per, 0


def build(nc, w, xT, memT, consts, params, ws_t, bs_b, rel, x1_dram, outT):
    with ExitStack() as ctx:
        def sb(name, shape, dt=F32):
            return ctx.enter_context(nc.sbuf_tensor(name, shape, dt))

        act_hi = sb("act_hi", [P, KT * S], F32R)
        act_lo = sb("act_lo", [P, KT * S], F32R)
        big = sb("big", [P, KT * S])
        raw = [sb(f"raw{i}", [P, KT * P]) for i in range(2)]
        w_hi = [sb(f"w_hi{i}", [P, KT * P], F32R) for i in range(2)]
        w_lo = [sb(f"w_lo{i}", [P, KT * P], F32R) for i in range(2)]
        scratch = sb("scratch", [P, 33 * S])
        cst = sb("cst", [P, len(CONSTS) * P])
        par = sb("par", [P, C_ALL])
        eps = sb("eps", [P, 1])
        g2 = sb("g2", [P, KT])
        gate = {n: sb("gate_" + n, [P, NB * DN]) for n in ("a", "t", "g", "gc", "beta", "ekd", "ebg", "egl")}
        small = sb("small", [P, 16])
        bank = [ctx.enter_context(nc.psum_tensor(f"gemm{i}", [P, S], F32)) for i in range(2)]
        pb = [ctx.enter_context(nc.psum_tensor(f"pb{i}", [P, S], F32)) for i in range(6)]

        def tl(i, n=1):
            return scratch[:, i * S:(i + n) * S]

        C = {n: cst[:, i * P:(i + 1) * P] for i, n in enumerate(CONSTS)}
        m_hi, m_lo = act_lo[:, 0:KT * MEM], act_lo[:, KT * MEM:2 * KT * MEM]
        Y, E, SS, SQ = tl(0), tl(1), tl(2), tl(3)
        GV, VTOK = tl(4, 4), tl(12, 4)
        MK, MV = tl(16, 2), tl(18, 2)
        GZ = tl(20)
        CQ, CZ, PM, PT = tl(20), tl(21), tl(22, 2), tl(24, 2)
        MVI = tl(26)[:, 0:2 * P]
        GSQ, GR, GMEAN = tl(24, 4), tl(28), tl(29)
        QT, KTT, VT, SZ = tl(20), tl(21), tl(22), tl(23)
        GSEL, BSEL, EG, DEC, KB, AT, AI, KBG, KDEC = (tl(i) for i in range(24, 33))
        VB, QG, XI, YI, UI = (tl(i) for i in range(4, 9))
        ML, NK, VN, ST, OSQ, OR = tl(9, 2), tl(11), tl(12)[:, 0:P], tl(15)[:, 0:P], tl(13), tl(14)
        QA, KA, VA, VATOK, SGA = (tl(i) for i in range(4, 9))
        LB, SPB, WB = tl(9, 3), tl(12, 3), tl(15, 3)
        QB, KBN, VBT, VBTOK, SGB, BIAS = (tl(i) for i in range(18, 24))
        PB, PTB = tl(24, 3), tl(27, 3)
        ACC1, ACC2, R1, R12, XIN, X2, OUTS = tl(4), tl(5), tl(32), tl(31), tl(6, 2), tl(8), tl(10, 2)
        MEMRAW, MR, XR = tl(4, 8), tl(12), tl(13)

        wsT, bsb = tl(30), tl(31)

        def blk(a, c, n=1):
            return a[:, c * P:(c + n) * P]

        def v3(a):
            return a.rearrange("p (c t) -> p c t", t=P)

        UP = [0, 512, 896, 1152]
        UN = [S - P * b for b in range(NB)]
        DO = [0, 128, 384, 768]
        DNN = [P * (b + 1) for b in range(NB)]

        names = """consts_in cst_in par_in mem_in x_in w_in0 w_in1 hi lo unit evac act_hi act_lo
            mem_sq mem_acc mem_ss mem_r x_sq x_acc x_ss x_r x_n
            mv_tok mv_ps mixed
            dve_steps act_steps pool_steps
            ab_rows ab_ps ab_tok ab_exp ab_ln ab_alog ab_g ab_cum ab_beta ab_e ab_fin ab_gc
            ge_sq ge_t ge_sig gv_done z_y z_sig
            ln_m1 ln_c ln_sq ln_m2 ln_r ln_v ln_tp ln_tok sp_w sp_o sp_done gated
            x_sc x_max x_exp x_p x_tp x_pt x_o xz_y xz_sig
            dn_y dn_sig dn_s dn_sq dn_ss dn_r dn_n
            sel gb eg bb kb dec_in dec_e dec_m kk at ai tp kbg m_lvl x1 y1 u_ps u_sb w_ps xy nk_ps nk
            vn_ps vn o_ps s_ps st o_sq o_ss o_r qg m_free
            o1_x0 o1_x1 o1_sq o1_acc o1_st o1_ss o1_r1 o1_t o1_r2 o1_r12 o1_n
            a_q a_k a_v a_vps a_vtok a_z a_abs a_l a_sp a_cum a_diag a_w a_o
            g_y g_sig b_sq b_ss b_r b_n b_v b_vps b_vtok b_bias b_sc b_add b_max b_exp b_p b_tp b_pt b_o b_bfree
            o2_x0 o2_x1 o2_xf o2_st0 o2_st1 init""".split()
        sem = {n: ctx.enter_context(nc.semaphore(n)) for n in names}
        gate_v = {n: t[:, :].rearrange("p (c h) -> p c h", h=DN) for n, t in gate.items()}
        block = ctx.enter_context(nc.Block())

        @block.sync
        def _(sp):
            def load(u, slot):
                sp.dma_start(raw[slot][:, :], w[u]).then_inc(sem[f"w_in{slot}"], 16)

            load(0, 0)
            load(1, 1)
            with sp.Fori(0, (U_END - 3) // 2) as i:
                for slot in range(2):
                    sp.wait_ge(sem["hi"], 8 * i + 4 * slot + 4)
                    sp.wait_ge(sem["lo"], 8 * i + 4 * slot + 4)
                    load(2 * i + 2 + slot, slot)
            sp.wait_ge(sem["hi"], 4 * (U_END - 2))
            sp.wait_ge(sem["lo"], 4 * (U_END - 2))
            load(U_END - 1, 0)

        @block.gpsimd
        def _(pool):
            def sel(h):
                nc.gpsimd.tensor_copy(v3(GSEL), gate_v["g"][:, :, bass.ds(h, 1)].broadcast_to([P, NB, P]))
                nc.gpsimd.tensor_copy(v3(BSEL), gate_v["beta"][:, :, bass.ds(h, 1)].broadcast_to([P, NB, P])).then_inc(sem["sel"], 1)

            nc.gpsimd.memset(SQ, 0.0).then_inc(sem["x_acc"], 1)
            for k in range(KT):
                pool.wait_ge(sem["x_sq"], k + 1)
                pool.wait_ge(sem["x_acc"], k + 1)
                nc.gpsimd.tensor_tensor(SQ, SQ, tl(k % 2), ALU.add).then_inc(sem["x_acc"], 1)
            pool.wait_ge(sem["ab_fin"], 1)
            pool.wait_ge(sem["sp_done"], GM)
            sel(0)

            def levels(h):
                pool.wait_ge(sem["at"], h + 1)
                for k in range(LEVELS):
                    if k >= 2:
                        pool.wait_ge(sem["xy"], LEVELS * h + k - 1)
                    nc.gpsimd.tensor_tensor(v3(blk(ML, NB * (k % 2), NB)), v3(AT),
                                            C[f"level{k}"].rearrange("p (c t) -> p c t", c=1).broadcast_to([P, NB, P]),
                                            ALU.mult).then_inc(sem["m_lvl"], 1)

            def head(h, last=False):
                levels(h)
                if not last:
                    pool.wait_ge(sem["bb"], h + 1)
                    sel(h + 1)

            with pool.Fori(0, DN - 1) as h:
                head(h)
            head(DN - 1, True)
            for s in range(2):
                if s == 0:
                    pool.wait_ge(sem["mixed"], M1)
                pool.dma_start(blk(XIN, NB * s, NB), xT[s]).then_inc(sem[f"o1_x{s}"], 16)
            with pool.Fori(0, KT // 2 - 1) as i:
                for s in range(2):
                    pool.wait_ge(sem["evac"], 2 * i + (U_O1 + s + 1))
                    pool.dma_start(x1_dram[2 * i + s], big[:, bass.ds((2 * i + s) * S, S)]).then_inc(sem["o1_st"], 16)
                    pool.dma_start(blk(XIN, NB * s, NB), xT[2 * i + s + 2]).then_inc(sem[f"o1_x{s}"], 16)
            for s in range(2):
                pool.wait_ge(sem["evac"], U_O1 + KT - 1 + s)
                pool.dma_start(x1_dram[KT - 2 + s], big[:, (KT - 2 + s) * S:(KT - 1 + s) * S]).then_inc(sem["o1_st"], 16)
            pool.wait_ge(sem["o1_r12"], 1)
            pool.dma_start(BIAS, rel[0]).then_inc(sem["b_bias"], 16)
            with pool.Fori(1, DN) as h:
                pool.wait_ge(sem["b_add"], NB * h)
                pool.dma_start(BIAS, rel[h]).then_inc(sem["b_bias"], 16)
            pool.wait_ge(sem["mixed"], M1 + 2 * DN)
            for s in range(2):
                pool.dma_start(blk(XIN, NB * s, NB), x1_dram[s]).then_inc(sem[f"o2_x{s}"], 16)
            with pool.Fori(0, KT // 2 - 1) as i:
                for s in range(2):
                    pool.wait_ge(sem["evac"], 2 * i + (U_O2 + s + 1))
                    pool.dma_start(outT[2 * i + s], blk(OUTS, NB * s, NB)).then_inc(sem[f"o2_st{s}"], 16)
                    pool.dma_start(blk(XIN, NB * s, NB), x1_dram[2 * i + s + 2]).then_inc(sem[f"o2_x{s}"], 16)
            for s in range(2):
                pool.wait_ge(sem["evac"], U_O2 + KT - 1 + s)
                pool.dma_start(outT[KT - 2 + s], blk(OUTS, NB * s, NB)).then_inc(sem[f"o2_st{s}"], 16)
            for s in range(2):
                pool.wait_ge(sem[f"o2_st{s}"], 8 * KT)

        @block.scalar
        def _(act):
            st = Steps(act, sem["act_steps"])
            A = nc.scalar.activation

            def hi(u, slot):
                act.wait_ge(sem[f"w_in{slot}"], 8 * (u - slot) + 16)
                if not isinstance(u, int) or u >= 2:
                    act.wait_ge(sem["unit"], u - 1)
                for q in range(4):
                    c = slice(q * S, (q + 1) * S)
                    A(w_hi[slot][:, c], raw[slot][:, c], ACT.Copy).then_inc(sem["hi"], 1)

            def sigmoid(ready, n, done):
                act.wait_ge(sem[ready], n)
                st.then(A(E, SS, ACT.Exp, scale=-1.0))
                st.then(A(E, E, ACT.Ln, bias=1.0))
                A(E, E, ACT.Exp, scale=-1.0).then_inc(sem[done], 1)

            def rsqrt(dst, src, scale, ready, n, done):
                act.wait_ge(sem[ready], n)
                st.then(A(dst, src, ACT.Ln, bias=eps[:, 0:1], scale=scale))
                A(dst, dst, ACT.Exp, scale=-0.5).then_inc(sem[done], 1)

            def operand_hi(k, n=S):
                t = bass.ds(k * n, n)
                A(act_hi[:, t], big[:, t], ACT.Copy).then_inc(sem["act_hi"], 1)

            act.preload_act_table_set("natural_log_exp_and_others")
            act.dma_start(par[:, :], params).then_inc(sem["par_in"], 16)
            act.dma_start(MEMRAW, memT).then_inc(sem["mem_in"], 16)
            act.dma_start(cst[:, :], consts).then_inc(sem["cst_in"], 16)
            act.wait_ge(sem["init"], 1)
            hi(0, 0)
            act.wait_ge(sem["par_in"], 16)
            act.wait_ge(sem["mem_in"], 16)
            act.dma_start(big[:, :].rearrange("p (k t) -> p k t", t=S), xT.rearrange("k p t -> p k t")).then_inc(sem["x_in"], 16)
            act.dma_start(wsT[:, :], ws_t).then_inc(sem["consts_in"], 16)
            act.dma_start(bsb[:, :], bs_b).then_inc(sem["consts_in"], 16)
            for k in range(KT):
                c = slice(k * MEM, (k + 1) * MEM)
                A(m_hi[:, c], MEMRAW[:, c], ACT.Copy, scale=par[:, C_MEM + k:C_MEM + k + 1]).then_inc(sem["act_hi"], 1)
            hi(1, 1)
            for k in range(KT // 2):
                if k >= 2:
                    act.wait_ge(sem["mem_acc"], k - 1)
                A(tl(k % 2), MEMRAW[:, k * S:(k + 1) * S], ACT.Square).then_inc(sem["mem_sq"], 1)
            rsqrt(MR[:, 0:MEM], pb[0][:, 0:MEM], 1.0 / D, "mem_ss", 1, "mem_r")
            act.wait_ge(sem["x_in"], 16)
            for u in range(6):
                hi(u + 2, u % 2)
                if u < 4:
                    for k in range(4 * u, 4 * u + 4):
                        act.wait_ge(sem["x_acc"] if k >= 2 else sem["mem_acc"], k if k >= 2 else KT // 2)
                        A(tl(k % 2), big[:, k * S:(k + 1) * S], ACT.Square).then_inc(sem["x_sq"], 1)
                elif u == 5:
                    rsqrt(XR, pb[1][:, :], 1.0 / D, "x_ss", 1, "x_r")
                    with act.Fori(0, KT) as k:
                        act.wait_ge(sem["x_n"], k + 1)
                        operand_hi(k)
            hi(U_AB, U_AB % 2)
            hi(U_AB + 1, (U_AB + 1) % 2)
            act.wait_ge(sem["ab_exp"], 1)
            st.then(A(gate["t"][:, :], gate["t"][:, :], ACT.Exp, scale=-1.0))
            A(gate["t"][:, :], gate["t"][:, :], ACT.Ln, bias=1.0).then_inc(sem["ab_ln"], 1)
            A(small[:, 0:DN], par[:, C_ALOG:C_ALOG + DN], ACT.Exp).then_inc(sem["ab_alog"], 1)
            A(gate["beta"][:, :], gate["beta"][:, :], ACT.Exp, scale=-1.0).then_inc(sem["ab_beta"], 1)
            act.wait_ge(sem["ab_gc"], 1)
            A(gate["ebg"][:, :], gate["gc"][:, :], ACT.Exp)
            A(gate["egl"][:, :], gate["a"][:, :], ACT.Exp)
            A(gate["ekd"][:, :], gate["t"][:, :], ACT.Exp).then_inc(sem["ab_e"], 1)
            hi(U_V + 1, (U_V + 1) % 2)

            def gelu(u, n):
                act.wait_ge(sem["evac"], u + 1)
                A(SQ, Y, ACT.Square).then_inc(sem["ge_sq"], 1)
                act.wait_ge(sem["ge_t"], n)
                st.then(A(E, SQ, ACT.Exp, scale=-GELU_SLOPE))
                st.then(A(E, E, ACT.Ln, bias=1.0))
                A(E, E, ACT.Exp, scale=-1.0).then_inc(sem["ge_sig"], 1)

            with act.Fori(0, GM // 2) as i:
                st.enter(i, 4)
                for j in range(2):
                    u0 = U_V + j
                    hi(2 * i + u0 + 2, u0 % 2)
                    gelu(2 * i + u0, 2 * i + j + 1)
                st.leave(GM // 2)
            with act.Fori(0, XA) as i:
                st.enter(i, 2)
                hi(2 * i + U_X + 2, U_X % 2)
                for b in range(2):
                    act.wait_ge(sem["x_max"], 2 * i + b + 1)
                    for c in (2 * b, 2 * b + 1):
                        m = slice((c % 2) * MEM, (c % 2 + 1) * MEM)
                        ins = A(PM[:, c * MEM:(c + 1) * MEM], pb[b][:, m], ACT.Exp, bias=small[:, c:c + 1],
                                accum_out=small[:, 4 + c:5 + c])
                ins.then_inc(sem["x_exp"], 1)
                act.wait_ge(sem["x_tp"], 2 * i + 1)
                A(v3(MVI), v3(MV).rearrange("p (b h) d -> p b h d", h=XA)[:, :, bass.ds(i, 1), :].rearrange("p b h d -> p b (h d)"),
                  ACT.Copy)
                A(PT[:, 0:S], pb[2][:, :], ACT.Copy).then_inc(sem["x_pt"], 1)
                act.wait_ge(sem["x_tp"], 2 * i + 2)
                A(PT[:, S:2 * S], pb[3][:, :], ACT.Copy).then_inc(sem["x_pt"], 1)
                hi(2 * i + U_X + 3, (U_X + 1) % 2)
                sigmoid("xz_y", i + 1, "xz_sig")
                st.leave(XA)

            def tables(h):
                act.wait_ge(sem["gb"], h + 1)
                A(EG, pb[4][:, :], ACT.Exp).then_inc(sem["eg"], 1)
                act.wait_ge(sem["dec_in"], h + 1)
                A(DEC, DEC, ACT.Exp).then_inc(sem["dec_e"], 1)

            def level(h, k):
                act.wait_ge(sem["u_ps"], LEVELS * h + k + 1)
                A(UI, pb[2][:, :], ACT.Copy).then_inc(sem["u_sb"], 1)

            def negated_keys(h):
                act.wait_ge(sem["nk_ps"], h + 1)
                A(NK, pb[4][:, :], ACT.Copy, scale=-1.0).then_inc(sem["nk"], 1)

            def new_values(h):
                for c in range(NB):
                    act.wait_ge(sem["vn_ps"], NB * h + c + 1)
                    A(VN, pb[1][:, 0:P], ACT.Copy).then_inc(sem["vn"], 1)

            def out_norm(h):
                act.wait_ge(sem["o_ps"], h + 1)
                A(OSQ, pb[5][:, :], ACT.Square).then_inc(sem["o_sq"], 1)
                rsqrt(OR, pb[0][:, :], 1.0 / P, "o_ss", h + 1, "o_r")

            def none():
                pass

            def dn_unit(h, j, pre=none, mid1=none, mid2=none):
                u0 = U_DN + j
                pre()
                hi(4 * h + u0 + 2, u0 % 2)
                mid1()
                sigmoid("dn_y", 4 * h + j + 1, "dn_sig")
                if j < 2:
                    act.wait_ge(sem["dn_s"], 2 * h + j + 1)
                    A(SQ, SS, ACT.Square).then_inc(sem["dn_sq"], 1)
                    rsqrt(E, pb[0][:, :], 1.0, "dn_ss", 2 * h + j + 1, "dn_r")
                mid2()

            def z_unit(g, pre, mid1, mid2=none):
                u0 = U_ZU
                pre()
                hi(2 * g + u0 + 2, u0 % 2)
                mid1()
                sigmoid("z_y", g + 1, "z_sig")
                mid2()

            def u_unit(g, pre=none, mid1=none):
                u0 = U_ZU + 1
                pre()
                hi(2 * g + u0 + 2, u0 % 2)
                mid1()
                gelu(2 * g + u0, GM + g + 1)

            def levels(h, *ks):
                def copies():
                    for k in ks:
                        level(h, k)
                return copies

            def states(h):
                def copies():
                    negated_keys(h)
                    new_values(h)
                return copies

            def gmlp_norm():
                for g in range(GM):
                    act.wait_ge(sem["ln_c"], g + 1)
                    A(blk(GSQ, NB * g, NB), blk(GV, NB * g, NB), ACT.Square).then_inc(sem["ln_sq"], 1)
                rsqrt(GR, pb[3][:, :], 1.0 / (GM * P), "ln_m2", 1, "ln_r")
                for g in range(GM):
                    act.wait_ge(sem["ln_tp"], g + 1)
                    A(v3(VTOK)[:, g::GM, :], v3(pb[2 + g % 2][:, :]), ACT.Copy).then_inc(sem["ln_tok"], 1)

            gmlp_norm()
            for j in range(2):
                dn_unit(0, j)
            dn_unit(0, 2, mid2=lambda: tables(0))
            dn_unit(0, 3, mid2=levels(0, 0, 1))
            with act.Fori(1, DN) as h:
                st.enter(h - 1, 4 * 2 + 2 + 1)
                p = h - 1
                dn_unit(h, 0, levels(p, 2), levels(p, 3))
                dn_unit(h, 1, levels(p, 4), levels(p, 5))

                def after_v():
                    out_norm(p)
                    tables(h)

                dn_unit(h, 2, levels(p, 6), states(p), after_v)
                dn_unit(h, 3, mid2=levels(h, 0, 1))
                st.leave(DN - 1)
            last = DN - 1
            z_unit(0, levels(last, 2), levels(last, 3))
            u_unit(0, levels(last, 4), levels(last, 5))
            z_unit(1, levels(last, 6), states(last), lambda: out_norm(last))
            u_unit(1)
            with act.Fori(GM // 2, GM) as g:
                st.enter(g - GM // 2, 4)
                z_unit(g, none, none)
                u_unit(g)
                st.leave(GM // 2)

            act.wait_ge(sem["mixed"], M1)
            act.wait_ge(sem["gated"], GM)
            act.wait_ge(sem["unit"], U_O1)
            with act.Fori(0, KT) as k:
                operand_hi(k)
            with act.Fori(0, KT // 2) as i:
                for j in range(2):
                    u0 = U_O1 + j
                    n = 2 * i + j + 1
                    hi(2 * i + u0 + 2, u0 % 2)
                    act.wait_ge(sem["evac"], 2 * i + (u0 + 1))
                    act.wait_ge(sem["o1_acc"], n)
                    x1 = big[:, bass.ds((2 * i + j) * S, S)]
                    A(SQ, x1, ACT.Square)
                    A(SS, x1, ACT.Square, scale=par[:, bass.ds(2 * i + j + C_FIN, 1)]).then_inc(sem["o1_sq"], 1)
            act.wait_ge(sem["unit"], U_D2)
            with act.Fori(0, KT) as k:
                t = bass.ds(k * S, S)
                A(act_hi[:, t], big[:, t], ACT.Copy, scale=g2[:, bass.ds(k, 1)]).then_inc(sem["act_hi"], 1)
            rsqrt(R1, pb[0][:, :], 1.0 / D, "o1_ss", 1, "o1_r1")
            rsqrt(R12, R12, 1.0 / D, "o1_t", 1, "o1_r2")

            with act.Fori(0, DN) as h:
                st.enter(h, 2 * NB + 2 + 2 + 2)
                u = 8 * h + U_D2

                def next_hi(j):
                    hi(u + j + 2, (U_D2 + j) % 2)

                for j in range(3):
                    next_hi(j)
                for b in range(NB):
                    lb = LB[:, UP[b]:UP[b] + UN[b]]
                    act.wait_ge(sem["a_z"], NB * h + b + 1)
                    st.then(A(lb, pb[b][:, 0:UN[b]], ACT.Abs))
                    st.then(A(lb, lb, ACT.Exp, scale=-1.0))
                    A(lb, lb, ACT.Ln, bias=1.0).then_inc(sem["a_l"], 1)
                next_hi(3)
                for i, b in enumerate(reversed(range(NB))):
                    wb = WB[:, UP[b]:UP[b] + UN[b]]
                    act.wait_ge(sem["a_diag"], NB * h + i + 1)
                    ins = A(wb[:, 0:P], wb[:, 0:P], ACT.Exp)
                    if UN[b] > P:
                        ins = A(wb[:, P:], pb[b][:, P:UN[b]], ACT.Exp)
                    ins.then_inc(sem["a_w"], 1)
                sigmoid("g_y", 2 * h + 1, "g_sig")
                for j in range(2):
                    next_hi(4 + j)
                    act.wait_ge(sem["evac"], u + (5 + j))
                    A(SQ, Y, ACT.Square).then_inc(sem["b_sq"], 1)
                    rsqrt(E, pb[5][:, :], 1.0 / P, "b_ss", 2 * h + j + 1, "b_r")
                for c in range(NB):
                    pc = PB[:, DO[c]:DO[c] + DNN[c]]
                    act.wait_ge(sem["b_max"], NB * h + c + 1)
                    A(pc, pc, ACT.Exp, bias=small[:, c:c + 1], accum_out=small[:, 4 + c:5 + c]).then_inc(sem["b_exp"], 1)
                next_hi(6)
                act.wait_ge(sem["b_vps"], h + 1)
                A(VBTOK, pb[4][:, :], ACT.Copy).then_inc(sem["b_vtok"], 1)
                for b in range(NB):
                    act.wait_ge(sem["b_tp"], NB * h + b + 1)
                    A(PTB[:, UP[b]:UP[b] + UN[b]], pb[b][:, 0:UN[b]], ACT.Copy).then_inc(sem["b_pt"], 1)
                next_hi(7)
                sigmoid("g_y", 2 * h + 2, "g_sig")
                st.leave(DN)
            act.wait_ge(sem["mixed"], M1 + 2 * DN)
            act.wait_ge(sem["unit"], U_O2)
            with act.Fori(0, KT) as k:
                operand_hi(k)
            with act.Fori(0, KT // 2 - 1) as i:
                for j in range(2):
                    u0 = U_O2 + j
                    hi(2 * i + u0 + 2, u0 % 2)

        @block.vector
        def _(dve):
            st = Steps(dve, sem["dve_steps"])
            V = nc.vector

            def lo(u, slot):
                for q in range(4):
                    dve.wait_ge(sem["hi"], 4 * u + (q + 1))
                    c = slice(q * S, (q + 1) * S)
                    V.tensor_tensor(w_lo[slot][:, c], raw[slot][:, c], w_hi[slot][:, c].bitcast(F32), ALU.subtract)\
                        .then_inc(sem["lo"], 1)

            def unit(u):
                dve.wait_ge(sem["unit"], u + 1)

            def operand_lo(k, before):
                t = bass.ds(k * S, S)
                dve.wait_ge(sem["act_hi"], k + (before + 1))
                V.tensor_tensor(act_lo[:, t], big[:, t], act_hi[:, t].bitcast(F32), ALU.subtract).then_inc(sem["act_lo"], 1)

            def chunks(mask):
                return mask.rearrange("p (c t) -> p c t", c=1).broadcast_to([P, NB, P])

            V.memset(eps[:, :], EPS).then_inc(sem["init"], 1)
            st.then(V.memset(SS, 0.0))
            lo(0, 0)
            dve.wait_ge(sem["par_in"], 16)
            for k in range(KT):
                c = slice(k * MEM, (k + 1) * MEM)
                dve.wait_ge(sem["act_hi"], k + 1)
                V.scalar_tensor_tensor(m_lo[:, c], MEMRAW[:, c], par[:, C_MEM + k:C_MEM + k + 1], m_hi[:, c].bitcast(F32),
                                       ALU.mult, ALU.subtract).then_inc(sem["act_lo"], 1)
            lo(1, 1)
            for k in range(KT // 2):
                dve.wait_ge(sem["mem_sq"], k + 1)
                V.tensor_tensor(SS, SS, tl(k % 2), ALU.add).then_inc(sem["mem_acc"], 1)
                dve.wait_ge(sem["mem_acc"], k + 1)
            V.tensor_tensor(SS[:, 0:MEM], SS[:, 0:MEM], SS[:, MEM:2 * MEM], ALU.add).then_inc(sem["mem_acc"], 1)
            dve.wait_ge(sem["cst_in"], 16)
            dve.wait_ge(sem["consts_in"], 32)
            st.then(V.tensor_tensor(g2[:, :], par[:, C_FIN:C_FIN + KT], par[:, C_LN2:C_LN2 + KT], ALU.mult))
            for u in range(8):
                unit(u)
                n = u // 2
                if u == 0:
                    dve.wait_ge(sem["mem_r"], 1)
                if u % 2 == 0:
                    V.tensor_tensor(MK[:, n * MEM:(n + 1) * MEM], bank[0][:, 0:MEM], MR[:, 0:MEM], ALU.mult)\
                        .then_inc(sem["evac"], 1)
                else:
                    V.tensor_tensor(SS[:, 0:MEM], bank[1][:, 0:MEM], MR[:, 0:MEM], ALU.mult).then_inc(sem["evac"], 1)
                if u < 7:
                    lo(u + 2, u % 2)
                if u % 2:
                    dve.wait_ge(sem["mv_ps"], n + 1)
                    V.tensor_copy(v3(MV)[:, n::XA, :], v3(pb[0][:, 0:MEM])).then_inc(sem["mv_tok"], 1)
                if u == 5:
                    dve.wait_ge(sem["x_r"], 1)
                    with dve.Fori(0, KT) as k:
                        x = big[:, bass.ds(k * S, S)]
                        V.scalar_tensor_tensor(x, x, par[:, bass.ds(k + C_LN, 1)], XR, ALU.mult, ALU.mult)\
                            .then_inc(sem["x_n"], 1)
            with dve.Fori(0, KT) as k:
                operand_lo(k, KT)
            lo(U_AB + 1, (U_AB + 1) % 2)
            unit(U_AB)
            V.tensor_copy(SS, bank[U_AB % 2][:, :]).then_inc(sem["evac"], 1)
            dve.wait_ge(sem["ab_ps"], 1)
            rows = v3(pb[0][:, :])
            gv = gate_v
            bias8 = par[:, C_DT:C_DT + DN].rearrange("p (c h) -> p c h", c=1).broadcast_to([P, NB, DN])
            V.tensor_scalar(gv["beta"], rows[:, :, 32:32 + DN], SILU_FLOOR, None, ALU.max)
            st.then(V.tensor_tensor(gv["a"], rows[:, :, 0:DN], bias8, ALU.add))
            st.then(V.tensor_scalar(gv["g"], gv["a"], -1.0, None, ALU.mult))
            V.tensor_tensor(gv["t"], gv["a"], gv["g"], ALU.max).then_inc(sem["ab_exp"], 1)
            dve.wait_ge(sem["ab_ln"], 1)
            st.then(V.scalar_tensor_tensor(gate["a"][:, :], gate["a"][:, :], 0.0, gate["t"][:, :], ALU.max, ALU.add))
            dve.wait_ge(sem["ab_alog"], 1)
            a8 = small[:, 0:DN].rearrange("p (c h) -> p c h", c=1).broadcast_to([P, NB, DN])
            V.scalar_tensor_tensor(gv["g"], gv["a"], -1.0, a8, ALU.mult, ALU.mult).then_inc(sem["ab_g"], 1)
            dve.wait_ge(sem["ab_beta"], 1)
            st.then(V.tensor_scalar(gate["beta"][:, :], gate["beta"][:, :], 1.0, None, ALU.add))
            st.then(V.reciprocal(gate["beta"][:, :], gate["beta"][:, :]))
            dve.wait_ge(sem["ab_cum"], 1)
            n = NB * DN
            V.tensor_copy(gate["gc"][:, :], pb[0][:, 0:n])
            st.then(V.tensor_copy(gate["a"][:, :], pb[0][:, n:2 * n]))
            V.tensor_tensor(gate["t"][:, :], gate["a"][:, :], gate["gc"][:, :], ALU.subtract).then_inc(sem["ab_gc"], 1)
            dve.wait_ge(sem["ab_e"], 1)
            V.tensor_tensor(gate["ebg"][:, :], gate["ebg"][:, :], gate["beta"][:, :], ALU.mult).then_inc(sem["ab_fin"], 1)
            lo(U_V + 1, (U_V + 1) % 2)

            def gelu(u, slot, n, dst, mid=None):
                unit(u)
                V.tensor_copy(Y, bank[slot][:, :]).then_inc(sem["evac"], 1)
                dve.wait_ge(sem["ge_sq"], n)
                st.then(V.tensor_scalar(SQ, SQ, GELU_CUBE, 1.0, ALU.mult, ALU.add))
                st.then(V.tensor_tensor(SQ, SQ, Y, ALU.mult))
                V.tensor_scalar(SQ, SQ, SILU_FLOOR / GELU_SLOPE, None, ALU.max).then_inc(sem["ge_t"], 1)
                if mid:
                    mid()
                dve.wait_ge(sem["ge_sig"], n)
                st.then(V.tensor_tensor(dst, Y, E, ALU.mult))

            def silu(u, slot, ready, done, n, dst):
                unit(u)
                V.tensor_scalar(SS, bank[slot][:, :], SILU_FLOOR, None, ALU.max).then_inc(sem[ready], 1)
                dve.wait_ge(sem[done], n)
                V.tensor_tensor(dst, bank[slot][:, :], E, ALU.mult).then_inc(sem["evac"], 1)
                dve.wait_ge(sem["evac"], u + 1)

            with dve.Fori(0, GM // 2) as i:
                st.enter(i, 2 * 3)
                for j in range(2):
                    u0 = U_V + j
                    lo(2 * i + u0 + 2, u0 % 2)
                    gelu(2 * i + u0, u0 % 2, 2 * i + j + 1, GV[:, bass.ds((2 * i + j) * S, S)])
                st.leave(GM // 2)
            with dve.Fori(0, XA) as i:
                st.enter(i, 1)
                u = 2 * i + U_X
                lo(u + 2, U_X % 2)
                unit(u)
                V.tensor_scalar(CQ, bank[U_X % 2][:, :], SCALE, None, ALU.mult).then_inc(sem["evac"], 1)
                for b in range(2):
                    dve.wait_ge(sem["x_sc"], 2 * i + b + 1)
                    V.tensor_reduce(small[:, 2 * b:2 * b + 2], pb[b][:, :].rearrange("p (c m) -> p c m", m=MEM),
                                    AX, ALU.max, negate=True).then_inc(sem["x_max"], 1)
                dve.wait_ge(sem["x_exp"], i + 1)
                st.then(V.reciprocal(small[:, 4:8], small[:, 4:8]))
                pm = PM.rearrange("p (c m) -> p c m", m=MEM)
                V.tensor_tensor(pm, pm, small[:, 4:8].rearrange("p (c m) -> p c m", m=1).broadcast_to([P, NB, MEM]),
                                ALU.mult).then_inc(sem["x_p"], 1)
                lo(u + 3, (U_X + 1) % 2)
                silu(u + 1, (U_X + 1) % 2, "xz_y", "xz_sig", i + 1, CZ)
                dve.wait_ge(sem["x_o"], i + 1)
                V.tensor_tensor(big[:, bass.ds((i + GM + DN) * S, S)], pb[4][:, :], CZ, ALU.mult).then_inc(sem["mixed"], 1)
                dve.wait_ge(sem["mixed"], i + 1)
                st.leave(XA)

            dve.wait_ge(sem["ln_m1"], 1)
            st.then(V.tensor_scalar(GMEAN, pb[2][:, :], 1.0 / (GM * P), None, ALU.mult))
            for g in range(GM):
                v = blk(GV, NB * g, NB)
                V.tensor_tensor(v, v, GMEAN, ALU.subtract).then_inc(sem["ln_c"], 1)
            dve.wait_ge(sem["ln_r"], 1)
            for g in range(GM):
                v = blk(GV, NB * g, NB)
                st.then(V.tensor_tensor(v, v, GR, ALU.mult))
                V.tensor_scalar(v, v, par[:, C_GG + g:C_GG + g + 1], par[:, C_GB + g:C_GB + g + 1], ALU.mult, ALU.add)\
                    .then_inc(sem["ln_v"], 1)
            V.tensor_tensor(v3(wsT[:, :]), v3(wsT[:, :]), chunks(C["tri_from"]), ALU.mult).then_inc(sem["sp_w"], 1)
            for g in range(GM):
                dve.wait_ge(sem["sp_o"], g + 1)
                V.tensor_tensor(v3(big[:, g * S:(g + 1) * S]), v3(pb[4 + g % 2][:, :]), chunks(blk(bsb[:, :], g)), ALU.add)\
                    .then_inc(sem["sp_done"], 1)

            def none():
                pass

            def dn_unit(h, j, pre=none, mid1=none, mid2=none):
                u0 = U_DN + j
                u = 4 * h + u0
                lo(u + 2, u0 % 2)
                pre()
                unit(u)
                b = bank[u0 % 2][:, :]

                def tap(k):
                    return par[:, bass.ds(12 * h + (C_CONV + 4 * j + k), 1)]

                st.then(V.tensor_scalar(Y, b, tap(3), None, ALU.mult))
                for k in (2, 1):
                    st.then(V.scalar_tensor_tensor(Y[:, 3 - k:], b[:, :S - 3 + k], tap(k), Y[:, 3 - k:], ALU.mult, ALU.add))
                V.scalar_tensor_tensor(Y[:, 3:], b[:, :S - 3], tap(0), Y[:, 3:], ALU.mult, ALU.add).then_inc(sem["evac"], 1)
                dve.wait_ge(sem["evac"], u + 1)
                V.tensor_scalar(SS, Y, SILU_FLOOR, None, ALU.max).then_inc(sem["dn_y"], 1)
                mid1()
                dve.wait_ge(sem["dn_sig"], 4 * h + j + 1)
                if j == 2:
                    V.tensor_tensor(VT, Y, E, ALU.mult).then_inc(sem["dn_n"], 1)
                    mid2()
                    return
                V.tensor_tensor(SS, Y, E, ALU.mult).then_inc(sem["dn_s"], 1)
                mid2()
                dve.wait_ge(sem["dn_r"], 2 * h + j + 1)
                V.scalar_tensor_tensor([QT, KTT][j], SS, SCALE if j == 0 else 1.0, E, ALU.mult, ALU.mult)\
                    .then_inc(sem["dn_n"], 1)

            def z_of_head(h, before=none):
                u0 = U_DN + 3
                u = 4 * h + u0
                unit(u)
                b = bank[u0 % 2][:, :]
                V.tensor_scalar(SS, b, SILU_FLOOR, None, ALU.max).then_inc(sem["dn_y"], 1)
                before()
                matrices(h)
                lo(u + 2, u0 % 2)
                level(h, 0)
                dve.wait_ge(sem["dn_sig"], 4 * h + 4)
                V.tensor_tensor(SZ, b, E, ALU.mult).then_inc(sem["evac"], 1)
                dve.wait_ge(sem["evac"], u + 1)
                scaled(h)
                level(h, 1)

            def z_unit(g, pre=none, mid1=none, mid2=none):
                u0 = U_ZU
                u = 2 * g + u0
                lo(u + 2, u0 % 2)
                pre()
                unit(u)
                b = bank[u0 % 2][:, :]
                V.tensor_scalar(SS, b, SILU_FLOOR, None, ALU.max).then_inc(sem["z_y"], 1)
                mid1()
                dve.wait_ge(sem["z_sig"], g + 1)
                V.tensor_tensor(GZ, b, E, ALU.mult).then_inc(sem["evac"], 1)
                dve.wait_ge(sem["evac"], u + 1)
                mid2()

            def u_unit(g, pre=none, mid=None):
                u0 = U_ZU + 1
                u = 2 * g + u0
                lo(u + 2, u0 % 2)
                pre()
                gelu(u, u0 % 2, GM + g + 1, Y, mid)
                st.then(V.tensor_tensor(Y, Y, GZ, ALU.mult))
                t = big[:, bass.ds(g * S, S)] if not isinstance(g, int) else big[:, g * S:(g + 1) * S]
                V.tensor_tensor(t, t, Y, ALU.mult).then_inc(sem["gated"], 1)
                dve.wait_ge(sem["gated"], g + 1)

            def tables(h):
                dve.wait_ge(sem["bb"], h + 1)
                V.tensor_tensor(KB, KTT, pb[2][:, :], ALU.mult).then_inc(sem["kb"], 1)
                dve.wait_ge(sem["eg"], h + 1)
                for c in range(NB):
                    ins = V.tensor_scalar(blk(DEC, c), pb[4][:, c * P:(c + 1) * P],
                                          gate["gc"][:, bass.ds(h + DN * c, 1)], 0.0, ALU.subtract, ALU.min)
                ins.then_inc(sem["dec_in"], 1)
                dve.wait_ge(sem["dec_e"], h + 1)
                st.then(V.tensor_tensor(v3(DEC), v3(DEC), chunks(C["tri_from"]), ALU.mult))

            def matrices(h):
                dve.wait_ge(sem["kk"], 2 * h + 1)
                V.tensor_tensor(AT, pb[3][:, :], DEC, ALU.mult).then_inc(sem["at"], 1)
                dve.wait_ge(sem["kk"], 2 * h + 2)
                V.tensor_tensor(AI, pb[4][:, :], DEC, ALU.mult).then_inc(sem["ai"], 1)
                V.tensor_tensor(QG, QT, EG, ALU.mult).then_inc(sem["qg"], 1)

            def scaled(h):
                def col(name):
                    return gate_v[name][:, :, bass.ds(h, 1)].broadcast_to([P, NB, P])

                dve.wait_ge(sem["tp"], 2 * h + 1)
                V.tensor_tensor(v3(KBG), v3(pb[5][:, :]), col("ebg"), ALU.mult)
                V.tensor_tensor(v3(KDEC), v3(pb[5][:, :]), col("ekd"), ALU.mult)
                dve.wait_ge(sem["tp"], 2 * h + 2)
                V.tensor_tensor(v3(VB), v3(pb[1][:, :]), col("beta"), ALU.mult).then_inc(sem["kbg"], 1)

            def level(h, k):
                n = LEVELS * h + (k + 1)
                if k == 0:
                    dve.wait_ge(sem["m_lvl"], n)
                    V.tensor_tensor(v3(YI), chunks(C["ident"]), v3(blk(ML, 0, NB)), ALU.subtract)
                    dve.wait_ge(sem["u_sb"], n)
                    V.tensor_tensor(v3(XI), chunks(C["ident"]), v3(UI), ALU.subtract).then_inc(sem["xy"], 1)
                    return
                dve.wait_ge(sem["w_ps"], (LEVELS - 1) * h + k)
                if k < LEVELS - 1:
                    V.tensor_tensor(XI, XI, pb[3][:, :], ALU.subtract)
                V.tensor_tensor(YI, YI, pb[4][:, :], ALU.subtract).then_inc(sem["xy"], 1)

            def states(h):
                for c in range(NB - 1):
                    dve.wait_ge(sem["s_ps"], (NB - 1) * h + c + 1)
                    if c == 0:
                        V.tensor_copy(ST, pb[3][:, 0:P]).then_inc(sem["st"], 1)
                    else:
                        V.scalar_tensor_tensor(ST, ST, gate["egl"][:, bass.ds(h + DN * c, 1)], pb[3][:, 0:P],
                                               ALU.mult, ALU.add).then_inc(sem["st"], 1)
                    dve.wait_ge(sem["st"], (NB - 1) * h + c + 1)

            def head_out(h):
                dve.wait_ge(sem["o_r"], h + 1)
                st.then(V.scalar_tensor_tensor(OSQ, pb[5][:, :], par[:, C_DNG:C_DNG + 1], OR, ALU.mult, ALU.mult))
                V.tensor_tensor(big[:, bass.ds((h + GM) * S, S)], OSQ, SZ, ALU.mult).then_inc(sem["mixed"], 1)
                dve.wait_ge(sem["mixed"], h + (XA + 1))

            for j in range(2):
                dn_unit(0, j)
            dn_unit(0, 2, mid2=lambda: tables(0))
            z_of_head(0)
            with dve.Fori(1, DN) as h:
                st.enter(h - 1, 3 * 3 + 1 + 1)
                p = h - 1
                dn_unit(h, 0, lambda: level(p, 2), mid2=lambda: level(p, 3))
                dn_unit(h, 1, lambda: level(p, 4), mid2=lambda: level(p, 5))
                dn_unit(h, 2, lambda: level(p, 6), lambda: states(p), lambda: tables(h))
                z_of_head(h, lambda: head_out(p))
                st.leave(DN - 1)
            last = DN - 1
            z_unit(0, lambda: level(last, 2), mid2=lambda: level(last, 3))
            u_unit(0, lambda: level(last, 4), lambda: level(last, 5))
            z_unit(1, lambda: level(last, 6), lambda: states(last))
            u_unit(1, lambda: head_out(last))
            with dve.Fori(GM // 2, GM) as g:
                st.enter(g - GM // 2, 4)
                z_unit(g)
                u_unit(g)
                st.leave(GM // 2)

            with dve.Fori(0, KT) as k:
                operand_lo(k, 2 * KT)
            V.memset(ACC1, 0.0)
            V.memset(ACC2, 0.0).then_inc(sem["o1_acc"], 1)
            with dve.Fori(0, KT // 2) as i:
                for j in range(2):
                    u0 = U_O1 + j
                    n = 2 * i + j + 1
                    lo(2 * i + u0 + 2, u0 % 2)
                    unit(2 * i + u0)
                    dve.wait_ge(sem[f"o1_x{j}"], 16 * i + 16)
                    V.tensor_tensor(big[:, bass.ds((2 * i + j) * S, S)], bank[u0 % 2][:, :], blk(XIN, NB * j, NB), ALU.add)\
                        .then_inc(sem["evac"], 1)
                    dve.wait_ge(sem["o1_sq"], n)
                    dve.wait_ge(sem["o1_acc"], n)
                    V.tensor_tensor(ACC1, ACC1, SQ, ALU.add)
                    V.tensor_tensor(ACC2, ACC2, SS, ALU.add).then_inc(sem["o1_acc"], 1)
            with dve.Fori(0, KT) as k:
                t = bass.ds(k * S, S)
                dve.wait_ge(sem["act_hi"], k + (3 * KT + 1))
                V.scalar_tensor_tensor(act_lo[:, t], big[:, t], g2[:, bass.ds(k, 1)], act_hi[:, t].bitcast(F32),
                                       ALU.mult, ALU.subtract).then_inc(sem["act_lo"], 1)
            dve.wait_ge(sem["o1_r1"], 1)
            st.then(V.tensor_tensor(R12, R1, R1, ALU.mult))
            dve.wait_ge(sem["o1_ss"], 2)
            V.tensor_tensor(R12, R12, pb[1][:, :], ALU.mult).then_inc(sem["o1_t"], 1)
            dve.wait_ge(sem["o1_r2"], 1)
            V.tensor_tensor(R12, R12, R1, ALU.mult).then_inc(sem["o1_r12"], 1)
            dve.wait_ge(sem["o1_r12"], 1)
            dve.wait_ge(sem["o1_st"], 16 * KT)

            with dve.Fori(0, DN) as h:
                st.enter(h, NB + 1 + 1 + NB + 2)
                u = 8 * h + U_D2

                def slot(j):
                    return (U_D2 + j) % 2

                def next_lo(j):
                    lo(u + j + 2, slot(j))

                def gate_silu(j, n, dst):
                    unit(u + j)
                    V.tensor_tensor(dst, bank[slot(j)][:, :], R12, ALU.mult).then_inc(sem["evac"], 1)
                    dve.wait_ge(sem["evac"], u + (j + 1))
                    V.tensor_scalar(SS, dst, SILU_FLOOR, None, ALU.max).then_inc(sem["g_y"], 1)
                    dve.wait_ge(sem["g_sig"], n)
                    st.then(V.tensor_tensor(dst, dst, E, ALU.mult))

                for j, dst in enumerate((QA, KA, VA)):
                    unit(u + j)
                    V.scalar_tensor_tensor(dst, bank[slot(j)][:, :], SCALE if j == 0 else 1.0, R12, ALU.mult, ALU.mult)\
                        .then_inc(sem["evac"], 1)
                    next_lo(j)
                dve.wait_ge(sem["a_vps"], h + 1)
                V.tensor_copy(VATOK, pb[4][:, :]).then_inc(sem["a_vtok"], 1)
                for b in range(NB):
                    spb = SPB[:, UP[b]:UP[b] + UN[b]]
                    dve.wait_ge(sem["a_l"], NB * h + b + 1)
                    st.then(V.scalar_tensor_tensor(spb, pb[b][:, 0:UN[b]], 0.0, LB[:, UP[b]:UP[b] + UN[b]], ALU.max, ALU.add))
                    V.tensor_tensor(spb[:, 0:P], spb[:, 0:P], C["strict"], ALU.mult).then_inc(sem["a_sp"], 1)
                next_lo(3)
                for i, b in enumerate(reversed(range(NB))):
                    dve.wait_ge(sem["a_cum"], NB * h + i + 1)
                    V.scalar_tensor_tensor(WB[:, UP[b]:UP[b] + P], pb[b][:, 0:P], 0.0, C["hide"], ALU.min, ALU.add)\
                        .then_inc(sem["a_diag"], 1)
                gate_silu(3, 2 * h + 1, SGA)
                for j in range(2):
                    unit(u + 4 + j)
                    V.tensor_tensor(Y, bank[slot(4 + j)][:, :], R12, ALU.mult).then_inc(sem["evac"], 1)
                    next_lo(4 + j)
                    if j == 0:
                        dve.wait_ge(sem["a_o"], h + 1)
                        V.tensor_tensor(big[:, bass.ds(h * S, S)], pb[4][:, :], SGA, ALU.mult).then_inc(sem["mixed"], 1)
                        dve.wait_ge(sem["mixed"], 2 * h + (M1 + 1))
                    dve.wait_ge(sem["b_r"], 2 * h + j + 1)
                    if j == 0:
                        st.then(V.tensor_scalar(QB, Y, par[:, C_QG:C_QG + 1], SCALE, ALU.mult, ALU.mult))
                        V.tensor_tensor(QB, QB, E, ALU.mult).then_inc(sem["b_n"], 1)
                    else:
                        V.scalar_tensor_tensor(KBN, Y, par[:, C_KG:C_KG + 1], E, ALU.mult, ALU.mult).then_inc(sem["b_n"], 1)
                dve.wait_ge(sem["b_bias"], 16 * h + 16)
                st.then(V.memset(BIAS[0:64, S - 64:S], NEG))
                for c in range(NB):
                    pc = PB[:, DO[c]:DO[c] + DNN[c]]
                    dve.wait_ge(sem["b_sc"], NB * h + c + 1)
                    V.tensor_tensor(pc, pb[c][:, 0:DNN[c]], BIAS[:, S - DNN[c]:S], ALU.add).then_inc(sem["b_add"], 1)
                    dve.wait_ge(sem["b_add"], NB * h + c + 1)
                    V.tensor_reduce(small[:, c:c + 1], pc, AX, ALU.max, negate=True).then_inc(sem["b_max"], 1)
                unit(u + 6)
                V.tensor_tensor(VBT, bank[slot(6)][:, :], R12, ALU.mult).then_inc(sem["evac"], 1)
                next_lo(6)
                for c in range(NB):
                    pc = PB[:, DO[c]:DO[c] + DNN[c]]
                    dve.wait_ge(sem["b_exp"], NB * h + c + 1)
                    st.then(V.reciprocal(small[:, 4 + c:5 + c], small[:, 4 + c:5 + c]))
                    V.tensor_scalar(pc, pc, small[:, 4 + c:5 + c], None, ALU.mult).then_inc(sem["b_p"], 1)
                next_lo(7)
                gate_silu(7, 2 * h + 2, SGB)
                dve.wait_ge(sem["b_o"], h + 1)
                V.tensor_tensor(big[:, bass.ds((h + DN) * S, S)], pb[4][:, :], SGB, ALU.mult).then_inc(sem["mixed"], 1)
                dve.wait_ge(sem["mixed"], 2 * h + (M1 + 2))
                st.leave(DN)
            with dve.Fori(0, KT) as k:
                operand_lo(k, 4 * KT)

            def out_tile(i, j, more=True):
                u0 = U_O2 + j
                n = 2 * i + j + 1
                if more:
                    lo(2 * i + u0 + 2, u0 % 2)
                dve.wait_ge(sem[f"o2_x{j}"], 16 * i + 16)
                dve.wait_ge(sem["evac"], 2 * i + u0)
                V.scalar_tensor_tensor(X2, blk(XIN, NB * j, NB), par[:, bass.ds(2 * i + j + C_FIN, 1)], R1, ALU.mult, ALU.mult)\
                    .then_inc(sem["o2_xf"], 1)
                dve.wait_ge(sem["o2_xf"], n)
                unit(2 * i + u0)
                V.tensor_tensor(blk(OUTS, NB * j, NB), bank[u0 % 2][:, :], X2, ALU.add)\
                    .then_inc(sem["evac"], 1)

            for j in range(2):
                out_tile(0, j)
            with dve.Fori(1, KT // 2 - 1) as i:
                for j in range(2):
                    dve.wait_ge(sem[f"o2_st{j}"], 16 * i)
                    out_tile(i, j)
            for j in range(2):
                dve.wait_ge(sem[f"o2_st{j}"], 16 * (KT // 2 - 1))
                out_tile(KT // 2 - 1, j, False)

        @block.tensor
        def _(pe):
            def mm(out, a, b, start=True, stop=True, skip=False):
                return nc.tensor.matmul(out, a, b, start=start, stop=stop, skip_group_check=skip)

            def tp(out, a):
                return nc.tensor.transpose(out, a, C["ident"])

            def gemm(u, slot, k0=0, k1=KT, before=None, mem=False):
                out = bank[slot][:, 0:MEM] if mem else bank[slot][:, :]
                if k0 == 0 and not mem:
                    pe.wait_ge(sem["evac"], u - 1)
                for k in range(k0, k1):
                    if k % 4 == 0:
                        pe.wait_ge(sem["hi"], 4 * u + (k // 4 + 1))
                        pe.wait_ge(sem["lo"], 4 * u + (k // 4 + 1))
                    if before is not None:
                        pe.wait_ge(sem["act_hi"], before + k + 1)
                        pe.wait_ge(sem["act_lo"], before + k + 1)
                    n = MEM if mem else S
                    ah, al = [m_hi, m_lo] if mem else [act_hi[:, :], act_lo[:, :]]
                    ah, al = ah[:, k * n:(k + 1) * n], al[:, k * n:(k + 1) * n]
                    wh, wl = w_hi[slot][:, k * P:(k + 1) * P], w_lo[slot][:, k * P:(k + 1) * P]
                    mm(out, wh, ah, k == 0, False)
                    mm(out, wh, al, False, False)
                    ins = mm(out, wl, ah, False, k == KT - 1)
                if k1 == KT:
                    ins.then_inc(sem["unit"], 1)

            def mem_pair(i, first=False):
                gemm(2 * i, 0, mem=True, before=0 if first else None)
                gemm(2 * i + 1, 1, mem=True)
                if first:
                    pe.wait_ge(sem["cst_in"], 16)
                    pe.wait_ge(sem["mem_acc"], KT // 2 + 1)
                    mm(pb[0][:, 0:MEM], C["ones"], SS[:, 0:MEM]).then_inc(sem["mem_ss"], 1)
                pe.wait_ge(sem["evac"], 2 * i + 2)
                for b in range(2):
                    ins = tp(pb[0][:, b * P:(b + 1) * P], SS[:, b * P:(b + 1) * P])
                ins.then_inc(sem["mv_ps"], 1)

            mem_pair(0, True)
            with pe.Fori(1, XA - 1) as i:
                mem_pair(i)
            pe.wait_ge(sem["consts_in"], 32)
            pe.wait_ge(sem["x_acc"], KT + 1)
            mm(pb[1][:, :], C["ones"], SQ).then_inc(sem["x_ss"], 1)
            mem_pair(XA - 1)
            gemm(U_AB, U_AB % 2, before=KT)
            gemm(U_V, U_V % 2, 0, 4)
            pe.wait_ge(sem["evac"], U_AB + 1)
            pe.wait_ge(sem["mv_tok"], XA)
            for c in range(NB):
                ins = tp(pb[0][:, c * P:(c + 1) * P], blk(SS, c))
            ins.then_inc(sem["ab_ps"], 1)
            gemm(U_V, U_V % 2, 4, 14)
            pe.wait_ge(sem["ab_g"], 1)
            n = NB * DN
            mm(pb[0][:, 0:n], C["tri_from"], gate["g"][:, :])
            mm(pb[0][:, n:2 * n], C["ones"], gate["g"][:, :]).then_inc(sem["ab_cum"], 1)
            gemm(U_V, U_V % 2, 14, KT)
            gemm(U_V + 1, (U_V + 1) % 2)
            with pe.Fori(1, GM // 2) as i:
                for j in range(2):
                    gemm(2 * i + (U_V + j), (U_V + j) % 2)
            with pe.Fori(0, XA) as i:
                u = 2 * i + U_X
                z = (U_X + 1) % 2
                gemm(u, U_X % 2)
                gemm(u + 1, z, 0, 4)
                pe.wait_ge(sem["evac"], u + 1)
                for c in range(NB):
                    ins = mm(pb[c // 2][:, (c % 2) * MEM:(c % 2 + 1) * MEM], blk(CQ, c), MK[:, bass.ds(i * MEM, MEM)])
                    if c % 2:
                        ins.then_inc(sem["x_sc"], 1)
                gemm(u + 1, z, 4, 13)
                pe.wait_ge(sem["x_p"], i + 1)
                for b in range(2):
                    for c in range(NB):
                        ins = tp(pb[2 + b][:, c * P:(c + 1) * P], PM[:, c * MEM + b * P:c * MEM + (b + 1) * P])
                    ins.then_inc(sem["x_tp"], 1)
                gemm(u + 1, z, 13, KT)
                pe.wait_ge(sem["x_pt"], 2 * i + 2)
                mm(pb[4][:, :], MVI[:, 0:P], PT[:, 0:S], True, False)
                mm(pb[4][:, :], MVI[:, P:2 * P], PT[:, S:2 * S], False, True).then_inc(sem["x_o"], 1)

            def norm_sum(h, j):
                pe.wait_ge(sem["dn_sq"], 2 * h + j + 1)
                mm(pb[0][:, :], C["ones"], SQ).then_inc(sem["dn_ss"], 1)

            def dn_gemm(h, j, k0, k1):
                gemm(4 * h + (U_DN + j), (U_DN + j) % 2, k0, k1)

            dn_gemm(0, 0, 0, 1)
            for g in range(GM):
                ins = mm(pb[2][:, :], C["ones"], blk(GV, NB * g, NB), g == 0, g == GM - 1)
            ins.then_inc(sem["ln_m1"], 1)
            dn_gemm(0, 0, 1, 8)
            for g in range(GM):
                pe.wait_ge(sem["ln_sq"], g + 1)
                ins = mm(pb[3][:, :], C["ones"], blk(GSQ, NB * g, NB), g == 0, g == GM - 1)
            ins.then_inc(sem["ln_m2"], 1)
            dn_gemm(0, 0, 8, KT)
            for g in range(GM):
                pe.wait_ge(sem["ln_v"], g + 1)
                if g == 1:
                    pe.wait_ge(sem["ln_r"], 1)
                if g >= 2:
                    pe.wait_ge(sem["ln_tok"], g - 1)
                for c in range(NB):
                    ins = tp(pb[2 + g % 2][:, c * P:(c + 1) * P], blk(GV, NB * g + c))
                ins.then_inc(sem["ln_tp"], 1)
            pe.wait_ge(sem["sp_w"], 1)
            for g in range(GM):
                pe.wait_ge(sem["ln_tok"], g + 1)
                if g == 0:
                    pe.wait_ge(sem["mixed"], XA)
                if g >= 2:
                    pe.wait_ge(sem["sp_done"], g - 1)
                for c in range(NB):
                    ins = mm(pb[4 + g % 2][:, c * P:(c + 1) * P], blk(VTOK, c * GM + g), blk(wsT[:, :], g))
                ins.then_inc(sem["sp_o"], 1)
            for j in range(2):
                dn_gemm(0, j + 1, 0, 13)
                norm_sum(0, j)
                dn_gemm(0, j + 1, 13, KT)
            def gate_rows(h):
                pe.wait_ge(sem["sel"], h + 1)
                for c in range(NB):
                    ins = mm(pb[4][:, c * P:(c + 1) * P], blk(GSEL, c), C["tri_from"])
                ins.then_inc(sem["gb"], 1)
                for c in range(NB):
                    ins = mm(pb[2][:, c * P:(c + 1) * P], blk(BSEL, c), C["ident"])
                ins.then_inc(sem["bb"], 1)

            def products(h):
                pe.wait_ge(sem["kb"], h + 1)
                pe.wait_ge(sem["dec_in"], h + 1)
                for c in range(NB):
                    ins = mm(pb[3][:, c * P:(c + 1) * P], blk(KTT, c), blk(KB, c))
                ins.then_inc(sem["kk"], 1)
                for c in range(NB):
                    ins = mm(pb[4][:, c * P:(c + 1) * P], blk(KTT, c), blk(QT, c))
                ins.then_inc(sem["kk"], 1)

            def transposes(h):
                pe.wait_ge(sem["mixed"], h + XA)
                for c in range(NB):
                    ins = tp(pb[5][:, c * P:(c + 1) * P], blk(KTT, c))
                ins.then_inc(sem["tp"], 1)
                pe.wait_ge(sem["dn_n"], 3 * h + 3)
                for c in range(NB):
                    ins = tp(pb[1][:, c * P:(c + 1) * P], blk(VT, c))
                ins.then_inc(sem["tp"], 1)

            def level_u(h, k):
                pe.wait_ge(sem["m_lvl"], LEVELS * h + (k + 1))
                if k:
                    pe.wait_ge(sem["xy"], LEVELS * h + k)
                m = blk(ML, NB * (k % 2), NB)
                for c in range(NB):
                    x = blk(XI, c) if k else C["ident"]
                    ins = mm(pb[2][:, c * P:(c + 1) * P], blk(m, c), x)
                ins.then_inc(sem["u_ps"], 1)

            def level_w(h, k):
                pe.wait_ge(sem["u_sb"], LEVELS * h + (k + 1))
                for c in range(NB):
                    if k < LEVELS - 1:
                        mm(pb[3][:, c * P:(c + 1) * P], blk(YI, c), blk(UI, c))
                    ins = mm(pb[4][:, c * P:(c + 1) * P], blk(UI, c), blk(YI, c))
                ins.then_inc(sem["w_ps"], 1)

            def negated_keys(h):
                pe.wait_ge(sem["xy"], LEVELS * (h + 1))
                pe.wait_ge(sem["kbg"], h + 1)
                for c in range(NB):
                    ins = mm(pb[4][:, c * P:(c + 1) * P], blk(KBG, c), blk(YI, c))
                ins.then_inc(sem["nk_ps"], 1)

            def new_values(h, c):
                v = pb[1][:, 0:P]
                if c:
                    pe.wait_ge(sem["st"], (NB - 1) * h + c)
                else:
                    pe.wait_ge(sem["nk"], h + 1)
                ins = mm(v, blk(YI, c), blk(VB, c), True, c == 0)
                if c:
                    ins = mm(v, blk(NK, c), ST, False, True)
                ins.then_inc(sem["vn_ps"], 1)

            def chunk_out(h, c):
                o = pb[5][:, c * P:(c + 1) * P]
                pe.wait_ge(sem["vn"], NB * h + c + 1)
                ins = mm(o, VN, blk(AI, c), True, c == 0)
                if c:
                    ins = mm(o, ST, blk(QG, c), False, True)
                if c == NB - 1:
                    ins.then_inc(sem["o_ps"], 1)
                else:
                    mm(pb[3][:, 0:P], blk(KDEC, c), VN).then_inc(sem["s_ps"], 1)

            def out_sum(h):
                pe.wait_ge(sem["o_sq"], h + 1)
                mm(pb[0][:, :], C["ones"], OSQ).then_inc(sem["o_ss"], 1)

            def beside(part, p, h=None):
                part(0, 0, 1)
                products(p)
                part(0, 1, 5)
                level_u(p, 0)
                part(0, 5, 7)
                transposes(p)
                part(0, 7, 9)
                level_u(p, 1)
                part(0, 9, 12)
                level_w(p, 1)
                part(0, 12, KT)
                for j, k in ((1, 2), (2, 4)):
                    part(j, 0, 1)
                    level_u(p, k)
                    part(j, 1, 4)
                    level_w(p, k)
                    part(j, 4, 9)
                    level_u(p, k + 1)
                    part(j, 9, 12)
                    level_w(p, k + 1)
                    part(j, 12, 15)
                    if h is not None:
                        norm_sum(h, j - 1)
                    if j == 2:
                        level_u(p, 6)
                    part(j, 15, KT)
                part(3, 0, 1)
                level_w(p, 6)
                part(3, 1, 5)
                negated_keys(p)
                part(3, 5, 6)
                for c in range(NB):
                    new_values(p, c)
                    part(3, 6 + 2 * c, 7 + 2 * c)
                    chunk_out(p, c)
                    part(3, 7 + 2 * c, 8 + 2 * c)
                if h is not None:
                    gate_rows(h)
                part(3, 14, 15)
                out_sum(p)
                part(3, 15, KT)

            dn_gemm(0, 3, 0, 13)
            gate_rows(0)
            dn_gemm(0, 3, 13, KT)
            with pe.Fori(1, DN) as h:
                beside(lambda j, k0, k1: dn_gemm(h, j, k0, k1), h - 1, h)
            beside(lambda j, k0, k1: gemm(U_ZU + j, (U_ZU + j) % 2, k0, k1), DN - 1)
            with pe.Fori(GM // 2, GM) as g:
                for j in range(2):
                    gemm(2 * g + (U_ZU + j), (U_ZU + j) % 2)

            def projection(u0, before, pairs):
                for j in range(2):
                    gemm(u0 + j, (u0 + j) % 2, before=before if j == 0 else None)
                with pe.Fori(1, pairs) as i:
                    for j in range(2):
                        gemm(2 * i + (u0 + j), (u0 + j) % 2)

            projection(U_O1, 2 * KT, KT // 2)
            pe.wait_ge(sem["o1_acc"], KT + 1)
            mm(pb[0][:, :], C["ones"], ACC1).then_inc(sem["o1_ss"], 1)
            mm(pb[1][:, :], C["ones"], ACC2).then_inc(sem["o1_ss"], 1)

            with pe.Fori(0, DN) as h:
                u = 8 * h + U_D2

                def d2(j, k0=0, k1=KT):
                    gemm(u + j, (U_D2 + j) % 2, k0, k1, before=3 * KT if j == 0 else None)

                d2(0)
                d2(1)
                d2(2)
                d2(3, 0, 2)
                pe.wait_ge(sem["evac"], u + 3)
                for c in range(NB):
                    ins = tp(pb[4][:, c * P:(c + 1) * P], blk(VA, c))
                ins.then_inc(sem["a_vps"], 1)
                for b in range(NB):
                    mm(pb[b][:, 0:UN[b]], blk(KA, b), QA[:, b * P:S], True, True).then_inc(sem["a_z"], 1)
                d2(3, 2)
                d2(4, 0, 3)
                for i, b in enumerate(reversed(range(NB))):
                    pe.wait_ge(sem["a_sp"], NB * h + b + 1)
                    if i == 0:
                        pe.wait_ge(sem["a_sp"], NB * h + NB)
                    ins = mm(pb[b][:, 0:UN[b]], C["neg_tri"], SPB[:, UP[b]:UP[b] + UN[b]], False, b == NB - 1, skip=True)
                    for later in range(b + 1, NB):
                        ins = mm(pb[b][:, (later - b) * P:UN[b]], C["neg_ones"], SPB[:, UP[later]:UP[later] + UN[later]],
                                 False, later == NB - 1, skip=True)
                    ins.then_inc(sem["a_cum"], 1)
                d2(4, 3, 12)
                pe.wait_ge(sem["a_w"], NB * h + NB)
                pe.wait_ge(sem["a_vtok"], h + 1)
                for b in range(NB):
                    ins = mm(pb[4][:, b * P:S], blk(VATOK, b), WB[:, UP[b]:UP[b] + UN[b]], b == 0, b == NB - 1, skip=True)
                ins.then_inc(sem["a_o"], 1)
                d2(4, 12)
                for j in range(2):
                    d2(5 + j, 0, 8)
                    pe.wait_ge(sem["b_sq"], 2 * h + j + 1)
                    mm(pb[5][:, :], C["ones"], SQ).then_inc(sem["b_ss"], 1)
                    d2(5 + j, 8, 12)
                    if j == 1:
                        pe.wait_ge(sem["b_n"], 2 * h + 2)
                        for c in range(NB):
                            mm(pb[c][:, 0:DNN[c]], blk(QB, c), KBN[:, 0:DNN[c]]).then_inc(sem["b_sc"], 1)
                    d2(5 + j, 12)
                d2(7, 0, 6)
                pe.wait_ge(sem["evac"], u + 7)
                pe.wait_ge(sem["mixed"], 2 * h + (M1 + 1))
                for c in range(NB):
                    ins = tp(pb[4][:, c * P:(c + 1) * P], blk(VBT, c))
                ins.then_inc(sem["b_vps"], 1)
                d2(7, 6, 12)
                pe.wait_ge(sem["b_p"], NB * h + NB)
                for b in range(NB):
                    for c in range(b, NB):
                        ins = tp(pb[b][:, (c - b) * P:(c - b + 1) * P], PB[:, DO[c] + b * P:DO[c] + (b + 1) * P])
                    ins.then_inc(sem["b_tp"], 1)
                d2(7, 12)
                pe.wait_ge(sem["b_vtok"], h + 1)
                pe.wait_ge(sem["b_pt"], NB * h + NB)
                for b in range(NB):
                    ins = mm(pb[4][:, b * P:S], blk(VBTOK, b), PTB[:, UP[b]:UP[b] + UN[b]], b == 0, b == NB - 1, skip=True)
                ins.then_inc(sem["b_o"], 1)
            projection(U_O2, 4 * KT, KT // 2)


def constants():
    j, i = np.meshgrid(np.arange(P), np.arange(P), indexing="ij")
    m = {"ident": i == j, "ones": i >= 0, "tri_from": i >= j, "neg_tri": -1.0 * (j >= i), "neg_ones": -1.0 * (i >= 0),
         "strict": i > j, "hide": np.where(i > j, 0.0, NEG)}
    for k in range(LEVELS):
        m[f"level{k}"] = (i >> k == (j >> k) + 1) & ((j >> k) % 2 == 0)
    return np.concatenate([m[n].astype(np.float32) for n in CONSTS], axis=1)


def kernel(**inputs):
    import concourse.bacc as bacc
    from concourse.bass_utils import run_bass_kernel_spmd

    f = {n: np.asarray(a) for n, a in inputs.items()}

    def tiles(m):
        return m.reshape(KT, P, -1, P).transpose(2, 1, 0, 3).reshape(-1, P, KT * P)

    w1 = f["w_in"][0]
    gm, dn, xa = GM * P, DN * P, XA * P
    at = np.cumsum([0, gm, gm, gm, dn, dn, dn, dn, DN, DN, xa, xa])
    gu, gv_, gz, dq, dk, dv, dz, da, db, cq, cz = (w1[:, at[i]:at[i + 1]] for i in range(11))
    ab = np.zeros((D, P), np.float32)
    ab[:, 0:DN] = da
    ab[:, 32:32 + DN] = db

    def interleave(*parts):
        t = [tiles(p) for p in parts]
        return np.stack(t, axis=1).reshape(-1, P, KT * P)

    kv = f["w_mem_kv"][0]
    w2 = f["w_in_2"][0]
    w = np.concatenate([
        interleave(kv[:, :xa], kv[:, xa:]), tiles(ab), tiles(gv_), interleave(cq, cz),
        interleave(dq, dk, dv, dz), interleave(gz, gu), tiles(f["w_out"][0]),
        interleave(*(w2[:, i * dn:(i + 1) * dn] for i in range(8))), tiles(f["w_out_2"][0])])
    assert w.shape[0] == U_END

    def cols(v):
        return v.reshape(-1, P).T

    conv = f["conv_w"][0].reshape(4, 3, DN, P).transpose(3, 2, 1, 0).reshape(P, DN * 3 * 4)
    params = np.concatenate([
        cols(f["ln_g"][0]), cols(f["mem_norm_g"][0]), cols(f["final_g"]), cols(f["norm_g_2"][0]),
        cols(f["gmlp_ln_g"][0]), cols(f["gmlp_ln_b"][0]), conv, cols(f["dn_norm_g"][0]), cols(f["q_norm_g_2"][0]),
        cols(f["k_norm_g_2"][0]), np.broadcast_to(f["dn_a_log"][0], (P, DN)), np.broadcast_to(f["dn_dt_bias"][0], (P, DN))],
        axis=1)
    p, x = np.arange(P)[:, None], np.arange(S)[None, :]
    rel = f["rel_bias_2"][0][:, np.clip(p - x + (S - P), -63, 256) + 63]
    arrays = {
        "w": w,
        "xT": f["x"][0].T.reshape(KT, P, S),
        "memT": f["mem"][0].T.reshape(KT, P, MEM).transpose(1, 0, 2).reshape(P, KT * MEM),
        "consts": constants(),
        "params": params,
        "ws_t": f["gmlp_ws"][0].transpose(2, 0, 1).reshape(P, GM * P),
        "bs_b": np.broadcast_to(f["gmlp_bs"][0].reshape(1, GM * P), (P, GM * P)),
        "rel": rel,
    }
    arrays = {n: np.ascontiguousarray(a) for n, a in arrays.items()}
    nc = bacc.Bacc("TRN2", target_bir_lowering=False, num_devices=1, dynamic_dma_scratch_size=4096)
    args = [nc.dram_tensor(f"in_{n}", a.shape, F32, kind="ExternalInput").ap() for n, a in arrays.items()]
    x1 = nc.dram_tensor("x1", (KT, P, S), F32, kind="Internal").ap()
    out = nc.dram_tensor("outT", (KT, P, S), F32, kind="ExternalOutput").ap()
    build(nc, *args, x1, out)
    r = run_bass_kernel_spmd(nc, [{f"in_{n}": a for n, a in arrays.items()}], core_ids=[0])
    return r.results[0]["outT"].reshape(1, D, S).transpose(0, 2, 1)
```

```python
from contextlib import ExitStack

import numpy as np

import concourse.bass as bass
from concourse import mybir

P = 128
S = 512
D = 2048
KT = D // P
NB = S // P
EPS = 1e-6
SCALE = float(P) ** -0.5
NEG = -1e30
GM, DN, XA, MEM = 4, 8, 4, 256
SILU_FLOOR = -40.0
GELU_CUBE = 0.044715
GELU_SLOPE = 2.0 * (2.0 / 3.141592653589793) ** 0.5

U_MEM = 0
U_AB = U_MEM + 2 * XA
U_V = U_AB + 1
U_X = U_V + GM
U_DN = U_X + 2 * XA
U_ZU = U_DN + 4 * DN
U_O1 = U_ZU + 2 * GM
U_D2 = U_O1 + KT
U_O2 = U_D2 + 8 * DN
U_END = U_O2 + KT
X_PART = {4: range(0, 5), 5: range(5, 10)}
X_POOL = 10
M1 = XA + DN

CONSTS = ["ident", "ones", "tri_from", "strict", "hide"] + [f"level{k}" for k in range(7)]
LEVELS = 7
C_LN, C_MEM, C_FIN, C_LN2 = 0, KT, 2 * KT, 3 * KT
C_GG, C_GB = 4 * KT, 4 * KT + GM
C_CONV = C_GB + GM
C_DNG = C_CONV + DN * 3 * 4
C_QG, C_KG = C_DNG + 1, C_DNG + 2
C_ALOG, C_DT = C_DNG + 3, C_DNG + 3 + DN
C_ALL = C_DT + DN

F32 = mybir.dt.float32
F32R = mybir.dt.float32r
ACT = mybir.ActivationFunctionType
ALU = mybir.AluOpType
AX = mybir.AxisListType.X


class Steps:

    def __init__(self, eng, sem):
        self.eng, self.sem, self.base, self.n = eng, sem, 0, 0

    def then(self, ins):
        self.n += 1
        ins.then_inc(self.sem, 1)
        self.eng.wait_ge(self.sem, self.base + self.n)

    def enter(self, i, per):
        self.start, self.per = self.n + self.base, per
        self.base, self.n = self.start + i * per, 0

    def leave(self, times):
        assert self.n == self.per, (self.n, self.per)
        self.base, self.n = self.start + times * self.per, 0


def build(nc, w, xT, memT, consts, negatives, params, ws_t, bs_b, rel, x1_dram, outT):
    with ExitStack() as ctx:
        def sb(name, shape, dt=F32):
            return ctx.enter_context(nc.sbuf_tensor(name, shape, dt))

        act_hi = sb("act_hi", [P, KT * S], F32R)
        act_lo = sb("act_lo", [P, KT * S], F32R)
        big = sb("big", [P, KT * S])
        raw = [sb(f"raw{i}", [P, KT * P]) for i in range(2)]
        w_hi = [sb(f"w_hi{i}", [P, KT * P], F32R) for i in range(2)]
        w_lo = [sb(f"w_lo{i}", [P, KT * P], F32R) for i in range(2)]
        scratch = sb("scratch", [P, 28 * S])
        parts = sb("parts", [P, 5 * S], F32R)
        sums = sb("sums", [P, 2 * P], F32R)
        cst = sb("cst", [P, len(CONSTS) * P])
        par = sb("par", [P, C_ALL])
        eps = sb("eps", [P, 1])
        g2 = sb("g2", [P, KT])
        gate = {n: sb("gate_" + n, [P, NB * DN]) for n in ("a", "t", "g", "gc", "beta", "ekd", "ebg", "egl")}
        small = sb("small", [P, 16])
        bank = [ctx.enter_context(nc.psum_tensor(f"gemm{i}", [P, S], F32)) for i in range(2)]
        pb = [ctx.enter_context(nc.psum_tensor(f"pb{i}", [P, S], F32)) for i in range(6)]

        def tl(i, n=1):
            return scratch[:, i * S:(i + n) * S]

        C = {n: cst[:, i * P:(i + 1) * P] for i, n in enumerate(CONSTS)}
        m_hi, m_lo = act_lo[:, 0:KT * MEM], act_lo[:, KT * MEM:2 * KT * MEM]
        Y, E, SS, SQ = tl(0), tl(1), tl(2), tl(3)
        GV, VTOK = tl(4, 4), tl(12, 4)
        MK, MV = tl(16, 2), tl(18, 2)
        GZ = tl(16)
        CQ, CZ, PM, PT = tl(20), tl(21), tl(22, 2), tl(24, 2)
        MVI = tl(8)[:, 0:2 * P]
        GSQ, GR, GMEAN = tl(8, 4), tl(22), tl(23)
        QT, KTT, VT, SZ = tl(16), tl(17), tl(18), tl(19)
        GSEL, BSEL, EG, DEC, KB, AT, AI, KBG = (tl(i) for i in range(20, 28))
        NK, KDEC = DEC, tl(11)
        VB, QG, XI, YI, UI = (tl(i) for i in range(4, 9))
        ML, VN, ST, OSQ, OR = tl(9, 2), tl(12)[:, 0:P], tl(15)[:, 0:P], tl(13), tl(14)
        QA, KA, VA, VATOK, SGA = (tl(i) for i in range(4, 9))
        LB, SPB, WB = (scratch[:, i * S:i * S + NB * (NB + 1) // 2 * P] for i in (9, 12, 15))
        n = NB * (NB + 1) // 2 * P
        SPHI, SPLO = parts[:, 0:n], parts[:, n:2 * n]
        QH, QL, KH, KL, SQH = (parts[:, i * S:(i + 1) * S] for i in range(5))
        SQL = KL
        QB, KBN, VBT, VBTOK, SGB, BIAS = (tl(i) for i in range(18, 24))
        PB, PTB = LB, WB
        ACC1, ACC2, R1, R12, XIN, X2, OUTS = tl(4), tl(5), tl(27), tl(26), tl(6, 2), tl(8), tl(10, 2)
        MEMRAW, MR, XR, XODD = tl(4, 8), tl(12), tl(13), tl(14)

        wsT, bsb, SUMS_IN = tl(26), tl(27), tl(15)[:, 0:2 * P]

        def blk(a, c, n=1):
            return a[:, c * P:(c + n) * P]

        def even(a, k):
            return a.rearrange("p (g two b) -> p g two b", two=2, b=1 << k)[:, :, 0, :]

        def packed(a, k):
            return a.rearrange("p (g b) -> p g b", b=1 << k)

        H = P // 2

        def v3(a):
            return a.rearrange("p (c t) -> p c t", t=P)

        UP = [0, 512, 896, 1152]
        UN = [S - P * b for b in range(NB)]
        DO = [0, 128, 384, 768]
        DNN = [P * (b + 1) for b in range(NB)]

        names = """consts_in cst_in par_in mem_in0 mem_in1 x_in0 x_in1 x_in2 x_in3 w_in0 w_in1 hi lo unit evac act_hi act_lo
            mem_sq mem_acc mem_ss mem_r x_sq x_acc x_acc2 x_ss x_r x_n x_np
            mv_tok mv_ps mixed
            dve_steps act_steps
            ab_ps ab_exp ab_ln ab_alog ab_g ab_cum ab_beta ab_e ab_fin ab_gc
            ge_sq ge_t ge_sig z_y z_sig
            ln_m1 ln_c ln_sq ln_m2 ln_r ln_v ln_tp ln_tok sp_w sp_o sp_done gated
            x_sc x_max x_exp x_p x_tp x_pt x_o xz_y xz_sig
            dn_y dn_sig dn_s dn_sq dn_ss dn_r dn_n
            sel gb eg bb kb dec_in dec_e kk at ai tp kbg m_lvl y_ps u_ps u_sb w_ps xy nk_ps nk
            vn_ps vn o_ps s_ps st o_sq o_ss o_r qg
            o1_x0 o1_x1 o1_sq o1_acc o1_st o1_ss o1_r1 o1_t o1_r2 o1_r12
            a_vps a_vtok a_hi a_lo a_z a_l a_sp a_sph a_spl a_cum a_diag a_w a_o
            g_y g_sig b_sq b_sql b_hi b_lo b_ss b_r b_n b_vps b_vtok b_bias b_sc b_add b_max b_exp b_p b_tp b_pt b_o
            o2_x0 o2_x1 o2_xf o2_st0 o2_st1 init""".split()
        sem = {n: ctx.enter_context(nc.semaphore(n)) for n in names}
        gate_v = {n: t[:, :].rearrange("p (c h) -> p c h", h=DN) for n, t in gate.items()}
        block = ctx.enter_context(nc.Block())

        @block.sync
        def _(sp):
            def load(u, slot):
                sp.dma_start(raw[slot][:, :], w[u]).then_inc(sem[f"w_in{slot}"], 16)

            load(0, 0)
            sp.wait_ge(sem["mem_in0"], 16)
            load(1, 1)
            with sp.Fori(0, (U_END - 3) // 2) as i:
                for slot in range(2):
                    sp.wait_ge(sem["hi"], 8 * i + 4 * slot + 4)
                    sp.wait_ge(sem["lo"], 8 * i + 4 * slot + 4)
                    load(2 * i + 2 + slot, slot)
            sp.wait_ge(sem["hi"], 4 * (U_END - 2))
            sp.wait_ge(sem["lo"], 4 * (U_END - 2))
            load(U_END - 1, 0)

        @block.gpsimd
        def _(pool):
            def sel(h):
                nc.gpsimd.tensor_copy(v3(GSEL), gate_v["g"][:, :, bass.ds(h, 1)].broadcast_to([P, NB, P]))
                nc.gpsimd.tensor_copy(v3(BSEL), gate_v["beta"][:, :, bass.ds(h, 1)].broadcast_to([P, NB, P])).then_inc(sem["sel"], 1)

            nc.gpsimd.memset(SQ, 0.0).then_inc(sem["x_acc"], 1)
            for i in range(KT // 2):
                pool.wait_ge(sem["x_sq"], 2 * i + 1)
                pool.wait_ge(sem["x_acc"], i + 1)
                nc.gpsimd.tensor_tensor(SQ, SQ, tl(0), ALU.add).then_inc(sem["x_acc"], 1)
            pool.wait_ge(sem["x_r"], 1)
            for k in range(X_POOL, KT):
                x = big[:, k * S:(k + 1) * S]
                nc.gpsimd.tensor_tensor(x, x, XR, ALU.mult).then_inc(sem["x_np"], 1)
            pool.wait_ge(sem["ab_fin"], 1)
            pool.wait_ge(sem["sp_done"], GM)
            sel(0)

            def levels(h):
                pool.wait_ge(sem["at"], h + 1)
                for k in range(LEVELS):
                    if k >= 2:
                        pool.wait_ge(sem["xy"], LEVELS * h + k - 1)
                    nc.gpsimd.tensor_tensor(v3(blk(ML, NB * (k % 2), NB)), v3(AT),
                                            C[f"level{k}"].rearrange("p (c t) -> p c t", c=1).broadcast_to([P, NB, P]),
                                            ALU.mult).then_inc(sem["m_lvl"], 1)

            def head(h, last=False):
                levels(h)
                if not last:
                    pool.wait_ge(sem["bb"], h + 1)
                    sel(h + 1)

            with pool.Fori(0, DN - 1) as h:
                head(h)
            head(DN - 1, True)
            for s in range(2):
                if s == 0:
                    pool.wait_ge(sem["mixed"], M1)
                pool.dma_start(blk(XIN, NB * s, NB), xT[s]).then_inc(sem[f"o1_x{s}"], 16)
            with pool.Fori(0, KT // 2 - 1) as i:
                for s in range(2):
                    pool.wait_ge(sem["evac"], 2 * i + (U_O1 + s + 1))
                    pool.dma_start(x1_dram[2 * i + s], big[:, bass.ds((2 * i + s) * S, S)]).then_inc(sem["o1_st"], 16)
                    pool.dma_start(blk(XIN, NB * s, NB), xT[2 * i + s + 2]).then_inc(sem[f"o1_x{s}"], 16)
            for s in range(2):
                pool.wait_ge(sem["evac"], U_O1 + KT - 1 + s)
                pool.dma_start(x1_dram[KT - 2 + s], big[:, (KT - 2 + s) * S:(KT - 1 + s) * S]).then_inc(sem["o1_st"], 16)
            pool.wait_ge(sem["o1_r12"], 1)
            pool.dma_start(BIAS, rel[0]).then_inc(sem["b_bias"], 16)
            with pool.Fori(1, DN) as h:
                pool.wait_ge(sem["b_add"], NB * h)
                pool.dma_start(BIAS, rel[h]).then_inc(sem["b_bias"], 16)
            pool.wait_ge(sem["mixed"], M1 + 2 * DN)
            for s in range(2):
                pool.dma_start(blk(XIN, NB * s, NB), x1_dram[s]).then_inc(sem[f"o2_x{s}"], 16)
            with pool.Fori(0, KT // 2 - 1) as i:
                for s in range(2):
                    pool.wait_ge(sem["evac"], 2 * i + (U_O2 + s + 1))
                    pool.dma_start(outT[2 * i + s], blk(OUTS, NB * s, NB)).then_inc(sem[f"o2_st{s}"], 16)
                    pool.dma_start(blk(XIN, NB * s, NB), x1_dram[2 * i + s + 2]).then_inc(sem[f"o2_x{s}"], 16)
            for s in range(2):
                pool.wait_ge(sem["evac"], U_O2 + KT - 1 + s)
                pool.dma_start(outT[KT - 2 + s], blk(OUTS, NB * s, NB)).then_inc(sem[f"o2_st{s}"], 16)
            for s in range(2):
                pool.wait_ge(sem[f"o2_st{s}"], 8 * KT)

        @block.scalar
        def _(act):
            st = Steps(act, sem["act_steps"])
            A = nc.scalar.activation

            def hi(u, slot):
                act.wait_ge(sem[f"w_in{slot}"], 8 * (u - slot) + 16)
                if not isinstance(u, int) or u >= 2:
                    act.wait_ge(sem["unit"], u - 1)
                for q in range(4):
                    c = slice(q * S, (q + 1) * S)
                    A(w_hi[slot][:, c], raw[slot][:, c], ACT.Copy).then_inc(sem["hi"], 1)

            def sigmoid(ready, n, done):
                act.wait_ge(sem[ready], n)
                st.then(A(E, SS, ACT.Exp, scale=-1.0))
                st.then(A(E, E, ACT.Ln, bias=1.0))
                A(E, E, ACT.Exp, scale=-1.0).then_inc(sem[done], 1)

            def rsqrt(dst, src, scale, ready, n, done):
                act.wait_ge(sem[ready], n)
                st.then(A(dst, src, ACT.Ln, bias=eps[:, 0:1], scale=scale))
                A(dst, dst, ACT.Exp, scale=-0.5).then_inc(sem[done], 1)

            def operand_hi(k, n=S):
                t = bass.ds(k * n, n) if not isinstance(k, int) else slice(k * n, (k + 1) * n)
                A(act_hi[:, t], big[:, t], ACT.Copy).then_inc(sem["act_hi"], 1)

            act.preload_act_table_set("natural_log_exp_and_others")
            act.dma_start(par[:, :], params).then_inc(sem["par_in"], 16)
            for j in range(2):
                half = slice(j * KT // 2 * MEM, (j + 1) * KT // 2 * MEM)
                act.dma_start(MEMRAW[:, half], memT[:, half]).then_inc(sem[f"mem_in{j}"], 16)
            act.wait_ge(sem["init"], 1)
            hi(0, 0)
            act.wait_ge(sem["par_in"], 16)
            act.wait_ge(sem["mem_in0"], 16)
            act.dma_start(cst[:, :], consts).then_inc(sem["cst_in"], 16)

            def load_x(q):
                act.dma_start(blk(big[:, :], NB * NB * q, NB * NB).rearrange("p (k t) -> p k t", t=S),
                              xT[4 * q:4 * q + 4].rearrange("k p t -> p k t")).then_inc(sem[f"x_in{q}"], 16)

            load_x(0)
            for k in range(KT):
                c = slice(k * MEM, (k + 1) * MEM)
                if k == KT // 2:
                    act.wait_ge(sem["mem_in1"], 16)
                A(m_hi[:, c], MEMRAW[:, c], ACT.Copy, scale=par[:, C_MEM + k:C_MEM + k + 1]).then_inc(sem["act_hi"], 1)
            hi(1, 1)
            load_x(1)
            for k in range(KT // 2):
                if k >= 2:
                    act.wait_ge(sem["mem_acc"], k - 1)
                A(tl(k % 2), MEMRAW[:, k * S:(k + 1) * S], ACT.Square).then_inc(sem["mem_sq"], 1)
            rsqrt(MR[:, 0:MEM], pb[0][:, 0:MEM], 1.0 / D, "mem_ss", 1, "mem_r")
            load_x(2)
            for u in range(7):
                hi(u + 2, u % 2)
                if u == 0:
                    load_x(3)
                if u == 1:
                    act.dma_start(wsT[:, :], ws_t).then_inc(sem["consts_in"], 16)
                    act.dma_start(bsb[:, :], bs_b).then_inc(sem["consts_in"], 16)
                    act.dma_start(SUMS_IN, negatives).then_inc(sem["consts_in"], 16)
                if u < 4:
                    for k in {0: (), 1: range(8)}.get(u, range(4 * u, 4 * u + 4)):
                        if k % 4 == 0:
                            act.wait_ge(sem[f"x_in{k // 4}"], 16)
                        if k >= 2:
                            act.wait_ge(sem[["x_acc", "x_acc2"][k % 2]], k // 2 + 1)
                        else:
                            act.wait_ge(sem["mem_acc"], KT // 2)
                        A(tl(k % 2), big[:, k * S:(k + 1) * S], ACT.Square).then_inc(sem["x_sq"], 1)
                else:
                    if u == 4:
                        rsqrt(XR, pb[1][:, :], 1.0 / D, "x_ss", 1, "x_r")
                    for k in X_PART.get(u, ()):
                        act.wait_ge(sem["x_n"], k + 1)
                        operand_hi(k)
                    if u == 6:
                        for k in range(X_POOL, KT):
                            act.wait_ge(sem["x_np"], k - X_POOL + 1)
                            A(act_hi[:, k * S:(k + 1) * S], big[:, k * S:(k + 1) * S], ACT.Copy,
                              scale=par[:, C_LN + k:C_LN + k + 1]).then_inc(sem["act_hi"], 1)
            hi(U_AB + 1, (U_AB + 1) % 2)
            act.wait_ge(sem["consts_in"], 48)
            A(sums[:, :], SUMS_IN, ACT.Copy)
            act.wait_ge(sem["ab_exp"], 1)
            st.then(A(gate["t"][:, :], gate["t"][:, :], ACT.Exp, scale=-1.0))
            A(gate["t"][:, :], gate["t"][:, :], ACT.Ln, bias=1.0).then_inc(sem["ab_ln"], 1)
            A(small[:, 0:DN], par[:, C_ALOG:C_ALOG + DN], ACT.Exp).then_inc(sem["ab_alog"], 1)
            A(gate["beta"][:, :], gate["beta"][:, :], ACT.Exp, scale=-1.0).then_inc(sem["ab_beta"], 1)
            act.wait_ge(sem["ab_gc"], 1)
            A(gate["ebg"][:, :], gate["gc"][:, :], ACT.Exp)
            A(gate["egl"][:, :], gate["a"][:, :], ACT.Exp)
            A(gate["ekd"][:, :], gate["t"][:, :], ACT.Exp).then_inc(sem["ab_e"], 1)
            hi(U_V + 1, (U_V + 1) % 2)

            def gelu(u, n):
                act.wait_ge(sem["evac"], u + 1)
                A(SQ, Y, ACT.Square).then_inc(sem["ge_sq"], 1)
                act.wait_ge(sem["ge_t"], n)
                st.then(A(E, SQ, ACT.Exp, scale=-GELU_SLOPE))
                st.then(A(E, E, ACT.Ln, bias=1.0))
                A(E, E, ACT.Exp, scale=-1.0).then_inc(sem["ge_sig"], 1)

            with act.Fori(0, GM // 2) as i:
                st.enter(i, 4)
                for j in range(2):
                    u0 = U_V + j
                    hi(2 * i + u0 + 2, u0 % 2)
                    gelu(2 * i + u0, 2 * i + j + 1)
                st.leave(GM // 2)
            with act.Fori(0, XA) as i:
                st.enter(i, 2)
                hi(2 * i + U_X + 2, U_X % 2)
                for b in range(2):
                    act.wait_ge(sem["x_max"], 2 * i + b + 1)
                    for c in (2 * b, 2 * b + 1):
                        m = slice((c % 2) * MEM, (c % 2 + 1) * MEM)
                        ins = A(PM[:, c * MEM:(c + 1) * MEM], pb[b][:, m], ACT.Exp, bias=small[:, c:c + 1],
                                accum_out=small[:, 4 + c:5 + c])
                ins.then_inc(sem["x_exp"], 1)
                act.wait_ge(sem["x_tp"], 2 * i + 1)
                A(v3(MVI), v3(MV).rearrange("p (b h) d -> p b h d", h=XA)[:, :, bass.ds(i, 1), :].rearrange("p b h d -> p b (h d)"),
                  ACT.Copy)
                A(PT[:, 0:S], pb[2][:, :], ACT.Copy).then_inc(sem["x_pt"], 1)
                act.wait_ge(sem["x_tp"], 2 * i + 2)
                A(PT[:, S:2 * S], pb[3][:, :], ACT.Copy).then_inc(sem["x_pt"], 1)
                hi(2 * i + U_X + 3, (U_X + 1) % 2)
                sigmoid("xz_y", i + 1, "xz_sig")
                st.leave(XA)

            def tables(h):
                act.wait_ge(sem["gb"], h + 1)
                A(EG, pb[4][:, :], ACT.Exp).then_inc(sem["eg"], 1)
                act.wait_ge(sem["dec_in"], h + 1)
                A(DEC, DEC, ACT.Exp).then_inc(sem["dec_e"], 1)

            def level(h, k):
                if k >= 2:
                    act.wait_ge(sem["y_ps"], (LEVELS - 2) * h + (k - 1))
                    A(YI, pb[4][:, :], ACT.Copy)
                act.wait_ge(sem["u_ps"], LEVELS * h + k + 1)
                n = S if k == 0 else S // 2
                A(UI[:, 0:n], pb[2][:, 0:n], ACT.Copy).then_inc(sem["u_sb"], 1)

            def negated_keys(h):
                act.wait_ge(sem["nk_ps"], h + 1)
                A(NK, pb[4][:, :], ACT.Copy, scale=-1.0).then_inc(sem["nk"], 1)

            def new_values(h):
                for c in range(NB):
                    act.wait_ge(sem["vn_ps"], NB * h + c + 1)
                    A(VN, pb[1][:, 0:P], ACT.Copy).then_inc(sem["vn"], 1)

            def out_norm(h):
                act.wait_ge(sem["o_ps"], h + 1)
                A(OSQ, pb[5][:, :], ACT.Square).then_inc(sem["o_sq"], 1)
                rsqrt(OR, pb[0][:, :], 1.0 / P, "o_ss", h + 1, "o_r")

            def none():
                pass

            def dn_unit(h, j, pre=none, mid1=none, mid2=none):
                u0 = U_DN + j
                pre()
                hi(4 * h + u0 + 2, u0 % 2)
                mid1()
                sigmoid("dn_y", 4 * h + j + 1, "dn_sig")
                if j < 2:
                    act.wait_ge(sem["dn_s"], 2 * h + j + 1)
                    A(SQ, SS, ACT.Square).then_inc(sem["dn_sq"], 1)
                    rsqrt(E, pb[0][:, :], 1.0, "dn_ss", 2 * h + j + 1, "dn_r")
                mid2()

            def z_unit(g, pre, mid1, mid2=none):
                u0 = U_ZU
                pre()
                hi(2 * g + u0 + 2, u0 % 2)
                mid1()
                sigmoid("z_y", g + 1, "z_sig")
                mid2()

            def u_unit(g, pre=none, mid1=none):
                u0 = U_ZU + 1
                pre()
                hi(2 * g + u0 + 2, u0 % 2)
                mid1()
                gelu(2 * g + u0, GM + g + 1)

            def levels(h, *ks):
                def copies():
                    for k in ks:
                        level(h, k)
                return copies

            def states(h):
                def copies():
                    negated_keys(h)
                    new_values(h)
                return copies

            def gmlp_norm():
                for g in range(GM):
                    act.wait_ge(sem["ln_c"], g + 1)
                    A(blk(GSQ, NB * g, NB), blk(GV, NB * g, NB), ACT.Square).then_inc(sem["ln_sq"], 1)
                rsqrt(GR, pb[3][:, :], 1.0 / (GM * P), "ln_m2", 1, "ln_r")
                for g in range(GM):
                    act.wait_ge(sem["ln_tp"], g + 1)
                    A(v3(VTOK)[:, g::GM, :], v3(pb[2 + g % 2][:, :]), ACT.Copy).then_inc(sem["ln_tok"], 1)

            gmlp_norm()
            for j in range(2):
                dn_unit(0, j)
            dn_unit(0, 2, mid2=lambda: tables(0))
            dn_unit(0, 3, mid2=levels(0, 0, 1))
            with act.Fori(1, DN) as h:
                st.enter(h - 1, 4 * 2 + 2 + 1)
                p = h - 1
                dn_unit(h, 0, levels(p, 2), levels(p, 3))
                dn_unit(h, 1, levels(p, 4), levels(p, 5))

                def after_v():
                    out_norm(p)
                    tables(h)

                dn_unit(h, 2, levels(p, 6), states(p), after_v)
                dn_unit(h, 3, mid2=levels(h, 0, 1))
                st.leave(DN - 1)
            last = DN - 1
            z_unit(0, levels(last, 2), levels(last, 3))
            u_unit(0, levels(last, 4), levels(last, 5))
            z_unit(1, levels(last, 6), states(last), lambda: out_norm(last))
            u_unit(1)
            z_unit(GM - 2, none, none)
            u_unit(GM - 2)
            z_unit(GM - 1, none, none)
            act.wait_ge(sem["evac"], U_O1)
            A(SQ, Y, ACT.Square).then_inc(sem["ge_sq"], 1)
            act.wait_ge(sem["mixed"], M1)
            for k in range(3):
                operand_hi(k)
            act.wait_ge(sem["ge_t"], 2 * GM)
            st.then(A(E, SQ, ACT.Exp, scale=-GELU_SLOPE))
            st.then(A(E, E, ACT.Ln, bias=1.0))
            A(E, E, ACT.Exp, scale=-1.0).then_inc(sem["ge_sig"], 1)
            act.wait_ge(sem["gated"], GM - 1)
            for k in range(3, KT):
                if k == KT - 1:
                    act.wait_ge(sem["gated"], GM)
                operand_hi(k)
            hi(U_O1 + 1, (U_O1 + 1) % 2)

            with act.Fori(0, KT // 2) as i:
                for j in range(2):
                    u0 = U_O1 + j
                    n = 2 * i + j + 1
                    act.wait_ge(sem["evac"], 2 * i + (u0 + 1))
                    act.wait_ge(sem["o1_acc"], n)
                    x1 = big[:, bass.ds((2 * i + j) * S, S)]
                    A(SQ, x1, ACT.Square)
                    A(SS, x1, ACT.Square, scale=par[:, bass.ds(2 * i + j + C_FIN, 1)]).then_inc(sem["o1_sq"], 1)
                    hi(2 * i + u0 + 2, u0 % 2)
            act.wait_ge(sem["unit"], U_D2)
            with act.Fori(0, KT) as k:
                t = bass.ds(k * S, S)
                A(act_hi[:, t], big[:, t], ACT.Copy, scale=g2[:, bass.ds(k, 1)]).then_inc(sem["act_hi"], 1)
            rsqrt(R1, pb[0][:, :], 1.0 / D, "o1_ss", 1, "o1_r1")
            rsqrt(R12, R12, 1.0 / D, "o1_t", 1, "o1_r2")

            with act.Fori(0, DN) as h:
                st.enter(h, 2 * NB + 2 + 2 + 2 + 2)
                u = 8 * h + U_D2

                def next_hi(j):
                    hi(u + j + 2, (U_D2 + j) % 2)

                for j in range(3):
                    next_hi(j)
                    if j < 2:
                        act.wait_ge(sem["evac"], u + (j + 1))
                        A([QH, KH][j], [QA, KA][j], ACT.Copy).then_inc(sem["a_hi"], 1)
                for b in range(NB):
                    lb = LB[:, UP[b]:UP[b] + UN[b]]
                    act.wait_ge(sem["a_z"], NB * h + b + 1)
                    st.then(A(lb, pb[b][:, 0:UN[b]], ACT.Abs))
                    st.then(A(lb, lb, ACT.Exp, scale=-1.0))
                    A(lb, lb, ACT.Ln, bias=1.0).then_inc(sem["a_l"], 1)
                next_hi(3)
                act.wait_ge(sem["a_sp"], NB * (h + 1))
                A(SPHI, SPB, ACT.Copy).then_inc(sem["a_sph"], 1)
                for i, b in enumerate(reversed(range(NB))):
                    wb = WB[:, UP[b]:UP[b] + UN[b]]
                    act.wait_ge(sem["a_diag"], NB * h + i + 1)
                    ins = A(wb[:, 0:P], wb[:, 0:P], ACT.Exp)
                    if UN[b] > P:
                        ins = A(wb[:, P:], pb[b][:, P:UN[b]], ACT.Exp)
                    ins.then_inc(sem["a_w"], 1)
                sigmoid("g_y", 2 * h + 1, "g_sig")
                for j in range(2):
                    act.wait_ge(sem["evac"], u + (5 + j))
                    st.then(A(SQ, Y, ACT.Square))
                    A(SQH, SQ, ACT.Copy).then_inc(sem["b_sq"], 1)
                    next_hi(4 + j)
                    rsqrt(E, pb[5][:, :], -1.0 / P, "b_ss", 2 * h + j + 1, "b_r")
                    act.wait_ge(sem["b_n"], 2 * h + j + 1)
                    A([QH, KH][j], [QB, KBN][j], ACT.Copy).then_inc(sem["b_hi"], 1)
                for c in range(NB):
                    pc = PB[:, DO[c]:DO[c] + DNN[c]]
                    act.wait_ge(sem["b_max"], NB * h + c + 1)
                    A(pc, pc, ACT.Exp, bias=small[:, c:c + 1], accum_out=small[:, 4 + c:5 + c]).then_inc(sem["b_exp"], 1)
                next_hi(6)
                act.wait_ge(sem["b_vps"], h + 1)
                A(VBTOK, pb[4][:, :], ACT.Copy).then_inc(sem["b_vtok"], 1)
                for b in range(NB):
                    act.wait_ge(sem["b_tp"], NB * h + b + 1)
                    A(PTB[:, UP[b]:UP[b] + UN[b]], pb[b][:, 0:UN[b]], ACT.Copy).then_inc(sem["b_pt"], 1)
                sigmoid("g_y", 2 * h + 2, "g_sig")
                next_hi(7)
                st.leave(DN)
            act.wait_ge(sem["mixed"], M1 + 2 * DN)
            act.wait_ge(sem["unit"], U_O2)
            with act.Fori(0, KT) as k:
                operand_hi(k)
            with act.Fori(0, KT // 2 - 1) as i:
                for j in range(2):
                    u0 = U_O2 + j
                    hi(2 * i + u0 + 2, u0 % 2)

        @block.vector
        def _(dve):
            st = Steps(dve, sem["dve_steps"])
            V = nc.vector

            def lo(u, slot):
                for q in range(4):
                    dve.wait_ge(sem["hi"], 4 * u + (q + 1))
                    c = slice(q * S, (q + 1) * S)
                    V.tensor_tensor(w_lo[slot][:, c], raw[slot][:, c], w_hi[slot][:, c].bitcast(F32), ALU.subtract)\
                        .then_inc(sem["lo"], 1)

            def unit(u):
                dve.wait_ge(sem["unit"], u + 1)

            def operand_lo(k, before):
                t = bass.ds(k * S, S) if not isinstance(k, int) else slice(k * S, (k + 1) * S)
                dve.wait_ge(sem["act_hi"], k + (before + 1))
                V.tensor_tensor(act_lo[:, t], big[:, t], act_hi[:, t].bitcast(F32), ALU.subtract).then_inc(sem["act_lo"], 1)

            def chunks(mask):
                return mask.rearrange("p (c t) -> p c t", c=1).broadcast_to([P, NB, P])

            V.memset(eps[:, :], EPS).then_inc(sem["init"], 1)
            st.then(V.memset(SS, 0.0))
            lo(0, 0)
            dve.wait_ge(sem["par_in"], 16)
            for k in range(KT):
                c = slice(k * MEM, (k + 1) * MEM)
                dve.wait_ge(sem["act_hi"], k + 1)
                V.scalar_tensor_tensor(m_lo[:, c], MEMRAW[:, c], par[:, C_MEM + k:C_MEM + k + 1], m_hi[:, c].bitcast(F32),
                                       ALU.mult, ALU.subtract).then_inc(sem["act_lo"], 1)
            lo(1, 1)
            for k in range(KT // 2):
                dve.wait_ge(sem["mem_sq"], k + 1)
                V.tensor_tensor(SS, SS, tl(k % 2), ALU.add).then_inc(sem["mem_acc"], 1)
                dve.wait_ge(sem["mem_acc"], k + 1)
            V.tensor_tensor(SS[:, 0:MEM], SS[:, 0:MEM], SS[:, MEM:2 * MEM], ALU.add).then_inc(sem["mem_acc"], 1)
            st.then(V.tensor_tensor(g2[:, :], par[:, C_FIN:C_FIN + KT], par[:, C_LN2:C_LN2 + KT], ALU.mult))
            V.memset(XODD, 0.0).then_inc(sem["x_acc2"], 1)

            def mem_out(u):
                unit(u)
                dst = SS[:, 0:MEM] if u % 2 else MK[:, u // 2 * MEM:(u // 2 + 1) * MEM]
                V.tensor_tensor(dst, bank[u % 2][:, 0:MEM], MR[:, 0:MEM], ALU.mult).then_inc(sem["evac"], 1)

            dve.wait_ge(sem["mem_r"], 1)
            for u in range(8):
                if u != 1:
                    mem_out(u)
                if u == 0:
                    mem_out(1)
                if u < 7:
                    lo(u + 2, u % 2)
                if u % 2:
                    n = u // 2
                    dve.wait_ge(sem["mv_ps"], n + 1)
                    V.tensor_copy(v3(MV)[:, n::XA, :], v3(pb[0][:, 0:MEM])).then_inc(sem["mv_tok"], 1)
                if u < 4:
                    for k in {0: (), 1: (1, 3, 5, 7)}.get(u, (4 * u + 1, 4 * u + 3)):
                        dve.wait_ge(sem["x_sq"], k + 1)
                        dve.wait_ge(sem["x_acc2"], k // 2 + 1)
                        V.tensor_tensor(XODD, XODD, tl(1), ALU.add).then_inc(sem["x_acc2"], 1)
                if u == 4:
                    dve.wait_ge(sem["x_r"], 1)
                for k in X_PART.get(u, ()):
                    x = big[:, k * S:(k + 1) * S]
                    V.scalar_tensor_tensor(x, x, par[:, C_LN + k:C_LN + k + 1], XR, ALU.mult, ALU.mult)\
                        .then_inc(sem["x_n"], 1)
            with dve.Fori(0, X_POOL) as k:
                operand_lo(k, KT)
            for k in range(X_POOL, KT):
                t = slice(k * S, (k + 1) * S)
                dve.wait_ge(sem["act_hi"], KT + k + 1)
                V.scalar_tensor_tensor(act_lo[:, t], big[:, t], par[:, C_LN + k:C_LN + k + 1], act_hi[:, t].bitcast(F32),
                                       ALU.mult, ALU.subtract).then_inc(sem["act_lo"], 1)
            lo(U_AB + 1, (U_AB + 1) % 2)
            unit(U_AB)
            V.tensor_copy(SS, bank[U_AB % 2][:, :]).then_inc(sem["evac"], 1)
            dve.wait_ge(sem["ab_ps"], 1)
            rows = v3(pb[0][:, :])
            gv = gate_v
            bias8 = par[:, C_DT:C_DT + DN].rearrange("p (c h) -> p c h", c=1).broadcast_to([P, NB, DN])
            V.tensor_scalar(gv["beta"], rows[:, :, 32:32 + DN], SILU_FLOOR, None, ALU.max)
            st.then(V.tensor_tensor(gv["a"], rows[:, :, 0:DN], bias8, ALU.add))
            st.then(V.tensor_scalar(gv["g"], gv["a"], -1.0, None, ALU.mult))
            V.tensor_tensor(gv["t"], gv["a"], gv["g"], ALU.max).then_inc(sem["ab_exp"], 1)
            dve.wait_ge(sem["ab_ln"], 1)
            st.then(V.scalar_tensor_tensor(gate["a"][:, :], gate["a"][:, :], 0.0, gate["t"][:, :], ALU.max, ALU.add))
            dve.wait_ge(sem["ab_alog"], 1)
            a8 = small[:, 0:DN].rearrange("p (c h) -> p c h", c=1).broadcast_to([P, NB, DN])
            V.scalar_tensor_tensor(gv["g"], gv["a"], -1.0, a8, ALU.mult, ALU.mult).then_inc(sem["ab_g"], 1)
            dve.wait_ge(sem["ab_beta"], 1)
            st.then(V.tensor_scalar(gate["beta"][:, :], gate["beta"][:, :], 1.0, None, ALU.add))
            st.then(V.reciprocal(gate["beta"][:, :], gate["beta"][:, :]))
            dve.wait_ge(sem["ab_cum"], 1)
            n = NB * DN
            V.tensor_copy(gate["gc"][:, :], pb[0][:, 0:n])
            st.then(V.tensor_copy(gate["a"][:, :], pb[0][:, n:2 * n]))
            V.tensor_tensor(gate["t"][:, :], gate["a"][:, :], gate["gc"][:, :], ALU.subtract).then_inc(sem["ab_gc"], 1)
            dve.wait_ge(sem["ab_e"], 1)
            V.tensor_tensor(gate["ebg"][:, :], gate["ebg"][:, :], gate["beta"][:, :], ALU.mult).then_inc(sem["ab_fin"], 1)
            lo(U_V + 1, (U_V + 1) % 2)

            def gelu(u, slot, n, dst, mid=None):
                unit(u)
                V.tensor_copy(Y, bank[slot][:, :]).then_inc(sem["evac"], 1)
                dve.wait_ge(sem["ge_sq"], n)
                st.then(V.tensor_scalar(SQ, SQ, GELU_CUBE, 1.0, ALU.mult, ALU.add))
                st.then(V.tensor_tensor(SQ, SQ, Y, ALU.mult))
                V.tensor_scalar(SQ, SQ, SILU_FLOOR / GELU_SLOPE, None, ALU.max).then_inc(sem["ge_t"], 1)
                if mid:
                    mid()
                dve.wait_ge(sem["ge_sig"], n)
                st.then(V.tensor_tensor(dst, Y, E, ALU.mult))

            def silu(u, slot, ready, done, n, dst):
                unit(u)
                V.tensor_scalar(SS, bank[slot][:, :], SILU_FLOOR, None, ALU.max).then_inc(sem[ready], 1)
                dve.wait_ge(sem[done], n)
                V.tensor_tensor(dst, bank[slot][:, :], E, ALU.mult).then_inc(sem["evac"], 1)
                dve.wait_ge(sem["evac"], u + 1)

            with dve.Fori(0, GM // 2) as i:
                st.enter(i, 2 * 3)
                for j in range(2):
                    u0 = U_V + j
                    lo(2 * i + u0 + 2, u0 % 2)
                    gelu(2 * i + u0, u0 % 2, 2 * i + j + 1, GV[:, bass.ds((2 * i + j) * S, S)])
                st.leave(GM // 2)
            with dve.Fori(0, XA) as i:
                st.enter(i, 1)
                u = 2 * i + U_X
                unit(u)
                V.tensor_scalar(CQ, bank[U_X % 2][:, :], SCALE, None, ALU.mult).then_inc(sem["evac"], 1)
                lo(u + 2, U_X % 2)
                for b in range(2):
                    dve.wait_ge(sem["x_sc"], 2 * i + b + 1)
                    V.tensor_reduce(small[:, 2 * b:2 * b + 2], pb[b][:, :].rearrange("p (c m) -> p c m", m=MEM),
                                    AX, ALU.max, negate=True).then_inc(sem["x_max"], 1)
                dve.wait_ge(sem["x_exp"], i + 1)
                st.then(V.reciprocal(small[:, 4:8], small[:, 4:8]))
                pm = PM.rearrange("p (c m) -> p c m", m=MEM)
                V.tensor_tensor(pm, pm, small[:, 4:8].rearrange("p (c m) -> p c m", m=1).broadcast_to([P, NB, MEM]),
                                ALU.mult).then_inc(sem["x_p"], 1)
                lo(u + 3, (U_X + 1) % 2)
                silu(u + 1, (U_X + 1) % 2, "xz_y", "xz_sig", i + 1, CZ)
                dve.wait_ge(sem["x_o"], i + 1)
                V.tensor_tensor(big[:, bass.ds((i + DN) * S, S)], pb[4][:, :], CZ, ALU.mult).then_inc(sem["mixed"], 1)
                dve.wait_ge(sem["mixed"], i + 1)
                st.leave(XA)

            dve.wait_ge(sem["ln_m1"], 1)
            st.then(V.tensor_scalar(GMEAN, pb[2][:, :], 1.0 / (GM * P), None, ALU.mult))
            for g in range(GM):
                v = blk(GV, NB * g, NB)
                V.tensor_tensor(v, v, GMEAN, ALU.subtract).then_inc(sem["ln_c"], 1)
            dve.wait_ge(sem["ln_r"], 1)
            for g in range(GM):
                v = blk(GV, NB * g, NB)
                st.then(V.tensor_tensor(v, v, GR, ALU.mult))
                V.tensor_scalar(v, v, par[:, C_GG + g:C_GG + g + 1], par[:, C_GB + g:C_GB + g + 1], ALU.mult, ALU.add)\
                    .then_inc(sem["ln_v"], 1)
            dve.wait_ge(sem["cst_in"], 16)
            dve.wait_ge(sem["consts_in"], 48)
            V.tensor_tensor(v3(wsT[:, :]), v3(wsT[:, :]), chunks(C["tri_from"]), ALU.mult).then_inc(sem["sp_w"], 1)
            for g in range(GM):
                dve.wait_ge(sem["sp_o"], g + 1)
                V.tensor_tensor(v3(big[:, (M1 + g) * S:(M1 + g + 1) * S]), v3(pb[4 + g % 2][:, :]), chunks(blk(bsb[:, :], g)), ALU.add)\
                    .then_inc(sem["sp_done"], 1)

            def none():
                pass

            def dn_unit(h, j, pre=none, mid1=none, mid2=none):
                u0 = U_DN + j
                u = 4 * h + u0
                lo(u + 2, u0 % 2)
                pre()
                unit(u)
                b = bank[u0 % 2][:, :]

                def tap(k):
                    return par[:, bass.ds(12 * h + (C_CONV + 4 * j + k), 1)]

                st.then(V.tensor_scalar(Y, b, tap(3), None, ALU.mult))
                for k in (2, 1):
                    st.then(V.scalar_tensor_tensor(Y[:, 3 - k:], b[:, :S - 3 + k], tap(k), Y[:, 3 - k:], ALU.mult, ALU.add))
                V.scalar_tensor_tensor(Y[:, 3:], b[:, :S - 3], tap(0), Y[:, 3:], ALU.mult, ALU.add).then_inc(sem["evac"], 1)
                dve.wait_ge(sem["evac"], u + 1)
                V.tensor_scalar(SS, Y, SILU_FLOOR, None, ALU.max).then_inc(sem["dn_y"], 1)
                mid1()
                dve.wait_ge(sem["dn_sig"], 4 * h + j + 1)
                if j == 2:
                    V.tensor_tensor(VT, Y, E, ALU.mult).then_inc(sem["dn_n"], 1)
                    mid2()
                    return
                V.tensor_tensor(SS, Y, E, ALU.mult).then_inc(sem["dn_s"], 1)
                mid2()
                dve.wait_ge(sem["dn_r"], 2 * h + j + 1)
                V.scalar_tensor_tensor([QT, KTT][j], SS, SCALE if j == 0 else 1.0, E, ALU.mult, ALU.mult)\
                    .then_inc(sem["dn_n"], 1)

            def z_of_head(h, before=none):
                u0 = U_DN + 3
                u = 4 * h + u0
                unit(u)
                b = bank[u0 % 2][:, :]
                V.tensor_scalar(SS, b, SILU_FLOOR, None, ALU.max).then_inc(sem["dn_y"], 1)
                before()
                matrices(h)
                level(h, 0)
                lo(u + 2, u0 % 2)
                dve.wait_ge(sem["dn_sig"], 4 * h + 4)
                V.tensor_tensor(SZ, b, E, ALU.mult).then_inc(sem["evac"], 1)
                dve.wait_ge(sem["evac"], u + 1)
                scaled(h)
                level(h, 1)

            def z_unit(g, pre=none, mid1=none, mid2=none):
                u0 = U_ZU
                u = 2 * g + u0
                lo(u + 2, u0 % 2)
                pre()
                unit(u)
                b = bank[u0 % 2][:, :]
                V.tensor_scalar(SS, b, SILU_FLOOR, None, ALU.max).then_inc(sem["z_y"], 1)
                mid1()
                dve.wait_ge(sem["z_sig"], g + 1)
                V.tensor_tensor(GZ, b, E, ALU.mult).then_inc(sem["evac"], 1)
                dve.wait_ge(sem["evac"], u + 1)
                mid2()

            def u_unit(g, pre=none, mid=None):
                u0 = U_ZU + 1
                u = 2 * g + u0
                lo(u + 2, u0 % 2)
                pre()
                gelu(u, u0 % 2, GM + g + 1, Y, mid)
                st.then(V.tensor_tensor(Y, Y, GZ, ALU.mult))
                t = big[:, bass.ds((g + M1) * S, S)] if not isinstance(g, int) else big[:, (M1 + g) * S:(M1 + g + 1) * S]
                V.tensor_tensor(t, t, Y, ALU.mult).then_inc(sem["gated"], 1)
                dve.wait_ge(sem["gated"], g + 1)

            def tables(h):
                dve.wait_ge(sem["bb"], h + 1)
                V.tensor_tensor(KB, KTT, pb[2][:, :], ALU.mult).then_inc(sem["kb"], 1)
                dve.wait_ge(sem["eg"], h + 1)
                for c in range(NB):
                    ins = V.tensor_scalar(blk(DEC, c), pb[4][:, c * P:(c + 1) * P],
                                          gate["gc"][:, bass.ds(h + DN * c, 1)], 0.0, ALU.subtract, ALU.min)
                ins.then_inc(sem["dec_in"], 1)
                dve.wait_ge(sem["dec_e"], h + 1)
                st.then(V.tensor_tensor(v3(DEC), v3(DEC), chunks(C["tri_from"]), ALU.mult))

            def matrices(h):
                dve.wait_ge(sem["kk"], 2 * h + 1)
                V.tensor_tensor(AT, pb[3][:, :], DEC, ALU.mult).then_inc(sem["at"], 1)
                dve.wait_ge(sem["kk"], 2 * h + 2)
                V.tensor_tensor(AI, pb[4][:, :], DEC, ALU.mult).then_inc(sem["ai"], 1)
                V.tensor_tensor(QG, QT, EG, ALU.mult).then_inc(sem["qg"], 1)

            def scaled(h):
                def col(name):
                    return gate_v[name][:, :, bass.ds(h, 1)].broadcast_to([P, NB, P])

                dve.wait_ge(sem["tp"], 2 * h + 1)
                V.tensor_tensor(v3(KBG), v3(pb[5][:, :]), col("ebg"), ALU.mult)
                V.tensor_tensor(v3(KDEC), v3(pb[5][:, :]), col("ekd"), ALU.mult)
                dve.wait_ge(sem["tp"], 2 * h + 2)
                V.tensor_tensor(v3(VB), v3(pb[1][:, :]), col("beta"), ALU.mult).then_inc(sem["kbg"], 1)

            def level(h, k):
                n = LEVELS * h + (k + 1)
                if k == 0:
                    dve.wait_ge(sem["m_lvl"], n)
                    V.tensor_tensor(v3(YI), chunks(C["ident"]), v3(blk(ML, 0, NB)), ALU.subtract)
                    dve.wait_ge(sem["u_sb"], n)
                    V.tensor_tensor(v3(XI), chunks(C["ident"]), v3(UI), ALU.subtract).then_inc(sem["xy"], 1)
                    return
                dve.wait_ge(sem["w_ps"], (LEVELS - 1) * h + k)
                if k < LEVELS - 1:
                    V.tensor_tensor(even(XI, k), even(XI, k), packed(pb[3][:, 0:S // 2], k), ALU.subtract).then_inc(sem["xy"], 1)
                else:
                    y = v3(YI)[0:H, :, H:P]
                    V.tensor_tensor(y, y, packed(pb[4][0:H, 0:S // 2], k), ALU.subtract).then_inc(sem["xy"], 1)

            def states(h):
                for c in range(NB - 1):
                    dve.wait_ge(sem["s_ps"], (NB - 1) * h + c + 1)
                    if c == 0:
                        V.tensor_copy(ST, pb[3][:, 0:P]).then_inc(sem["st"], 1)
                    else:
                        V.scalar_tensor_tensor(ST, ST, gate["egl"][:, bass.ds(h + DN * c, 1)], pb[3][:, 0:P],
                                               ALU.mult, ALU.add).then_inc(sem["st"], 1)
                    dve.wait_ge(sem["st"], (NB - 1) * h + c + 1)

            def head_out(h):
                dve.wait_ge(sem["o_r"], h + 1)
                st.then(V.scalar_tensor_tensor(OSQ, pb[5][:, :], par[:, C_DNG:C_DNG + 1], OR, ALU.mult, ALU.mult))
                V.tensor_tensor(big[:, bass.ds(h * S, S)], OSQ, SZ, ALU.mult).then_inc(sem["mixed"], 1)
                dve.wait_ge(sem["mixed"], h + (XA + 1))

            for j in range(2):
                dn_unit(0, j)
            dn_unit(0, 2, mid2=lambda: tables(0))
            z_of_head(0)
            with dve.Fori(1, DN) as h:
                st.enter(h - 1, 3 * 3 + 1 + 1)
                p = h - 1
                dn_unit(h, 0, lambda: level(p, 2), mid2=lambda: level(p, 3))
                dn_unit(h, 1, lambda: level(p, 4), mid2=lambda: level(p, 5))
                dn_unit(h, 2, lambda: level(p, 6), lambda: states(p), lambda: tables(h))
                z_of_head(h, lambda: head_out(p))
                st.leave(DN - 1)
            last = DN - 1
            z_unit(0, lambda: level(last, 2), mid2=lambda: level(last, 3))
            u_unit(0, lambda: level(last, 4), lambda: level(last, 5))
            z_unit(1, lambda: level(last, 6), lambda: states(last))
            u_unit(1, lambda: head_out(last))
            z_unit(GM - 2)
            u_unit(GM - 2)
            z_unit(GM - 1)
            gelu(U_O1 - 1, (U_O1 - 1) % 2, 2 * GM, Y, lambda: [operand_lo(k, 2 * KT) for k in range(3)])
            st.then(V.tensor_tensor(Y, Y, GZ, ALU.mult))
            t = big[:, (KT - 1) * S:KT * S]
            V.tensor_tensor(t, t, Y, ALU.mult).then_inc(sem["gated"], 1)
            for k in range(3, KT):
                operand_lo(k, 2 * KT)
            lo(U_O1 + 1, (U_O1 + 1) % 2)

            V.memset(ACC1, 0.0)
            V.memset(ACC2, 0.0).then_inc(sem["o1_acc"], 1)
            with dve.Fori(0, KT // 2) as i:
                for j in range(2):
                    u0 = U_O1 + j
                    n = 2 * i + j + 1
                    unit(2 * i + u0)
                    dve.wait_ge(sem[f"o1_x{j}"], 16 * i + 16)
                    V.tensor_tensor(big[:, bass.ds((2 * i + j) * S, S)], bank[u0 % 2][:, :], blk(XIN, NB * j, NB), ALU.add)\
                        .then_inc(sem["evac"], 1)
                    dve.wait_ge(sem["o1_sq"], n)
                    dve.wait_ge(sem["o1_acc"], n)
                    V.tensor_tensor(ACC1, ACC1, SQ, ALU.add)
                    V.tensor_tensor(ACC2, ACC2, SS, ALU.add).then_inc(sem["o1_acc"], 1)
                    lo(2 * i + u0 + 2, u0 % 2)
            with dve.Fori(0, KT) as k:
                t = bass.ds(k * S, S)
                dve.wait_ge(sem["act_hi"], k + (3 * KT + 1))
                V.scalar_tensor_tensor(act_lo[:, t], big[:, t], g2[:, bass.ds(k, 1)], act_hi[:, t].bitcast(F32),
                                       ALU.mult, ALU.subtract).then_inc(sem["act_lo"], 1)
            dve.wait_ge(sem["o1_r1"], 1)
            st.then(V.tensor_tensor(R12, R1, R1, ALU.mult))
            dve.wait_ge(sem["o1_ss"], 2)
            V.tensor_tensor(R12, R12, pb[1][:, :], ALU.mult).then_inc(sem["o1_t"], 1)
            dve.wait_ge(sem["o1_r2"], 1)
            V.tensor_tensor(R12, R12, R1, ALU.mult).then_inc(sem["o1_r12"], 1)
            dve.wait_ge(sem["o1_r12"], 1)
            dve.wait_ge(sem["o1_st"], 16 * KT)

            with dve.Fori(0, DN) as h:
                st.enter(h, NB + 1 + 1 + NB + 2)
                u = 8 * h + U_D2

                def slot(j):
                    return (U_D2 + j) % 2

                def next_lo(j):
                    lo(u + j + 2, slot(j))

                def gate_silu(j, n, dst):
                    unit(u + j)
                    V.tensor_tensor(dst, bank[slot(j)][:, :], R12, ALU.mult).then_inc(sem["evac"], 1)
                    dve.wait_ge(sem["evac"], u + (j + 1))
                    V.tensor_scalar(SS, dst, SILU_FLOOR, None, ALU.max).then_inc(sem["g_y"], 1)
                    dve.wait_ge(sem["g_sig"], n)
                    st.then(V.tensor_tensor(dst, dst, E, ALU.mult))

                for j, dst in enumerate((QA, KA, VA)):
                    unit(u + j)
                    V.scalar_tensor_tensor(dst, bank[slot(j)][:, :], SCALE if j == 0 else 1.0, R12, ALU.mult, ALU.mult)\
                        .then_inc(sem["evac"], 1)
                    next_lo(j)
                    if j < 2:
                        dve.wait_ge(sem["a_hi"], 2 * h + j + 1)
                        V.tensor_tensor([QL, KL][j], dst, [QH, KH][j].bitcast(F32), ALU.subtract).then_inc(sem["a_lo"], 1)
                dve.wait_ge(sem["a_vps"], h + 1)
                V.tensor_copy(VATOK, pb[4][:, :]).then_inc(sem["a_vtok"], 1)
                for b in range(NB):
                    spb = SPB[:, UP[b]:UP[b] + UN[b]]
                    dve.wait_ge(sem["a_l"], NB * h + b + 1)
                    st.then(V.scalar_tensor_tensor(spb, pb[b][:, 0:UN[b]], 0.0, LB[:, UP[b]:UP[b] + UN[b]], ALU.max, ALU.add))
                    V.tensor_tensor(spb[:, 0:P], spb[:, 0:P], C["strict"], ALU.mult).then_inc(sem["a_sp"], 1)
                next_lo(3)
                dve.wait_ge(sem["a_sph"], h + 1)
                V.tensor_tensor(SPLO, SPB, SPHI.bitcast(F32), ALU.subtract).then_inc(sem["a_spl"], 1)
                for i, b in enumerate(reversed(range(NB))):
                    dve.wait_ge(sem["a_cum"], NB * h + i + 1)
                    V.scalar_tensor_tensor(WB[:, UP[b]:UP[b] + P], pb[b][:, 0:P], 0.0, C["hide"], ALU.min, ALU.add)\
                        .then_inc(sem["a_diag"], 1)
                gate_silu(3, 2 * h + 1, SGA)
                for j in range(2):
                    unit(u + 4 + j)
                    V.tensor_tensor(Y, bank[slot(4 + j)][:, :], R12, ALU.mult).then_inc(sem["evac"], 1)
                    dve.wait_ge(sem["b_sq"], 2 * h + j + 1)
                    V.tensor_tensor(SQL, SQ, SQH.bitcast(F32), ALU.subtract).then_inc(sem["b_sql"], 1)
                    next_lo(4 + j)
                    if j == 0:
                        dve.wait_ge(sem["a_o"], h + 1)
                        V.tensor_tensor(big[:, bass.ds(h * S, S)], pb[4][:, :], SGA, ALU.mult).then_inc(sem["mixed"], 1)
                        dve.wait_ge(sem["mixed"], 2 * h + (M1 + 1))
                    dve.wait_ge(sem["b_r"], 2 * h + j + 1)
                    if j == 0:
                        st.then(V.tensor_scalar(QB, Y, par[:, C_QG:C_QG + 1], SCALE, ALU.mult, ALU.mult))
                        V.tensor_tensor(QB, QB, E, ALU.mult).then_inc(sem["b_n"], 1)
                    else:
                        V.scalar_tensor_tensor(KBN, Y, par[:, C_KG:C_KG + 1], E, ALU.mult, ALU.mult).then_inc(sem["b_n"], 1)
                    dve.wait_ge(sem["b_hi"], 2 * h + j + 1)
                    V.tensor_tensor([QL, KL][j], [QB, KBN][j], [QH, KH][j].bitcast(F32), ALU.subtract)\
                        .then_inc(sem["b_lo"], 1)
                dve.wait_ge(sem["b_bias"], 16 * h + 16)
                st.then(V.memset(BIAS[0:64, S - 64:S], NEG))
                for c in range(NB):
                    pc = PB[:, DO[c]:DO[c] + DNN[c]]
                    dve.wait_ge(sem["b_sc"], NB * h + c + 1)
                    V.tensor_tensor(pc, pb[c][:, 0:DNN[c]], BIAS[:, S - DNN[c]:S], ALU.add).then_inc(sem["b_add"], 1)
                    dve.wait_ge(sem["b_add"], NB * h + c + 1)
                    V.tensor_reduce(small[:, c:c + 1], pc, AX, ALU.max, negate=True).then_inc(sem["b_max"], 1)
                unit(u + 6)
                V.tensor_tensor(VBT, bank[slot(6)][:, :], R12, ALU.mult).then_inc(sem["evac"], 1)
                next_lo(6)
                for c in range(NB):
                    pc = PB[:, DO[c]:DO[c] + DNN[c]]
                    dve.wait_ge(sem["b_exp"], NB * h + c + 1)
                    st.then(V.reciprocal(small[:, 4 + c:5 + c], small[:, 4 + c:5 + c]))
                    V.tensor_scalar(pc, pc, small[:, 4 + c:5 + c], None, ALU.mult).then_inc(sem["b_p"], 1)
                gate_silu(7, 2 * h + 2, SGB)
                dve.wait_ge(sem["b_o"], h + 1)
                V.tensor_tensor(big[:, bass.ds((h + DN) * S, S)], pb[4][:, :], SGB, ALU.mult).then_inc(sem["mixed"], 1)
                dve.wait_ge(sem["mixed"], 2 * h + (M1 + 2))
                next_lo(7)
                st.leave(DN)
            with dve.Fori(0, KT) as k:
                operand_lo(k, 4 * KT)

            def out_tile(i, j, more=True):
                u0 = U_O2 + j
                n = 2 * i + j + 1
                if more:
                    lo(2 * i + u0 + 2, u0 % 2)
                dve.wait_ge(sem[f"o2_x{j}"], 16 * i + 16)
                dve.wait_ge(sem["evac"], 2 * i + u0)
                V.scalar_tensor_tensor(X2, blk(XIN, NB * j, NB), par[:, bass.ds(2 * i + j + C_FIN, 1)], R1, ALU.mult, ALU.mult)\
                    .then_inc(sem["o2_xf"], 1)
                dve.wait_ge(sem["o2_xf"], n)
                unit(2 * i + u0)
                V.tensor_tensor(blk(OUTS, NB * j, NB), bank[u0 % 2][:, :], X2, ALU.add)\
                    .then_inc(sem["evac"], 1)

            for j in range(2):
                out_tile(0, j)
            with dve.Fori(1, KT // 2 - 1) as i:
                for j in range(2):
                    dve.wait_ge(sem[f"o2_st{j}"], 16 * i)
                    out_tile(i, j)
            for j in range(2):
                dve.wait_ge(sem[f"o2_st{j}"], 16 * (KT // 2 - 1))
                out_tile(KT // 2 - 1, j, False)

        @block.tensor
        def _(pe):
            def mm(out, a, b, start=True, stop=True, skip=False):
                return nc.tensor.matmul(out, a, b, start=start, stop=stop, skip_group_check=skip)

            def tp(out, a):
                return nc.tensor.transpose(out, a, C["ident"])

            def mm3(out, a, b, i, cols):
                mm(out, blk(a[0], i), b[0][:, cols], True, False)
                mm(out, blk(a[0], i), b[1][:, cols], False, False)
                return mm(out, blk(a[1], i), b[0][:, cols], False, True)

            def gemm(u, slot, k0=0, k1=KT, before=None, mem=False):
                out = bank[slot][:, 0:MEM] if mem else bank[slot][:, :]
                if k0 == 0 and not mem:
                    pe.wait_ge(sem["evac"], u - 1)
                for k in range(k0, k1):
                    if k % 4 == 0:
                        pe.wait_ge(sem["hi"], 4 * u + (k // 4 + 1))
                        pe.wait_ge(sem["lo"], 4 * u + (k // 4 + 1))
                    if before is not None:
                        pe.wait_ge(sem["act_hi"], before + k + 1)
                        pe.wait_ge(sem["act_lo"], before + k + 1)
                    n = MEM if mem else S
                    ah, al = [m_hi, m_lo] if mem else [act_hi[:, :], act_lo[:, :]]
                    ah, al = ah[:, k * n:(k + 1) * n], al[:, k * n:(k + 1) * n]
                    wh, wl = w_hi[slot][:, k * P:(k + 1) * P], w_lo[slot][:, k * P:(k + 1) * P]
                    mm(out, wh, ah, k == 0, False)
                    mm(out, wh, al, False, False)
                    ins = mm(out, wl, ah, False, k == KT - 1)
                if k1 == KT:
                    ins.then_inc(sem["unit"], 1)

            def mem_pair(i, first=False, x_sum=False):
                gemm(2 * i, 0, mem=True, before=0 if first else None)
                if x_sum:
                    pe.wait_ge(sem["x_acc"], KT // 2 + 1)
                    pe.wait_ge(sem["x_acc2"], KT // 2 + 1)
                    mm(pb[1][:, :], C["ones"], SQ, True, False)
                    mm(pb[1][:, :], C["ones"], XODD, False, True).then_inc(sem["x_ss"], 1)
                gemm(2 * i + 1, 1, mem=True)
                if first:
                    pe.wait_ge(sem["cst_in"], 16)
                    pe.wait_ge(sem["mem_acc"], KT // 2 + 1)
                    mm(pb[0][:, 0:MEM], C["ones"], SS[:, 0:MEM]).then_inc(sem["mem_ss"], 1)
                pe.wait_ge(sem["evac"], 2 * i + 2)
                for b in range(2):
                    ins = tp(pb[0][:, b * P:(b + 1) * P], SS[:, b * P:(b + 1) * P])
                ins.then_inc(sem["mv_ps"], 1)

            mem_pair(0, True)
            mem_pair(1)
            mem_pair(2, x_sum=True)
            mem_pair(3)
            gemm(U_AB, U_AB % 2, before=KT)
            gemm(U_V, U_V % 2, 0, 4)
            pe.wait_ge(sem["evac"], U_AB + 1)
            pe.wait_ge(sem["mv_tok"], XA)
            for c in range(NB):
                ins = tp(pb[0][:, c * P:(c + 1) * P], blk(SS, c))
            ins.then_inc(sem["ab_ps"], 1)
            gemm(U_V, U_V % 2, 4, 14)
            pe.wait_ge(sem["ab_g"], 1)
            n = NB * DN
            mm(pb[0][:, 0:n], C["tri_from"], gate["g"][:, :])
            mm(pb[0][:, n:2 * n], C["ones"], gate["g"][:, :]).then_inc(sem["ab_cum"], 1)
            gemm(U_V, U_V % 2, 14, KT)
            gemm(U_V + 1, (U_V + 1) % 2)
            with pe.Fori(1, GM // 2) as i:
                for j in range(2):
                    gemm(2 * i + (U_V + j), (U_V + j) % 2)
            with pe.Fori(0, XA) as i:
                u = 2 * i + U_X
                z = (U_X + 1) % 2
                gemm(u, U_X % 2)
                gemm(u + 1, z, 0, 4)
                pe.wait_ge(sem["evac"], u + 1)
                for c in range(NB):
                    ins = mm(pb[c // 2][:, (c % 2) * MEM:(c % 2 + 1) * MEM], blk(CQ, c), MK[:, bass.ds(i * MEM, MEM)])
                    if c % 2:
                        ins.then_inc(sem["x_sc"], 1)
                gemm(u + 1, z, 4, 13)
                pe.wait_ge(sem["x_p"], i + 1)
                for b in range(2):
                    for c in range(NB):
                        ins = tp(pb[2 + b][:, c * P:(c + 1) * P], PM[:, c * MEM + b * P:c * MEM + (b + 1) * P])
                    ins.then_inc(sem["x_tp"], 1)
                gemm(u + 1, z, 13, KT)
                pe.wait_ge(sem["x_pt"], 2 * i + 2)
                mm(pb[4][:, :], MVI[:, 0:P], PT[:, 0:S], True, False)
                mm(pb[4][:, :], MVI[:, P:2 * P], PT[:, S:2 * S], False, True).then_inc(sem["x_o"], 1)

            def norm_sum(h, j):
                pe.wait_ge(sem["dn_sq"], 2 * h + j + 1)
                mm(pb[0][:, :], C["ones"], SQ).then_inc(sem["dn_ss"], 1)

            def dn_gemm(h, j, k0, k1):
                gemm(4 * h + (U_DN + j), (U_DN + j) % 2, k0, k1)

            dn_gemm(0, 0, 0, 1)
            for g in range(GM):
                ins = mm(pb[2][:, :], C["ones"], blk(GV, NB * g, NB), g == 0, g == GM - 1)
            ins.then_inc(sem["ln_m1"], 1)
            dn_gemm(0, 0, 1, 8)
            for g in range(GM):
                pe.wait_ge(sem["ln_sq"], g + 1)
                ins = mm(pb[3][:, :], C["ones"], blk(GSQ, NB * g, NB), g == 0, g == GM - 1)
            ins.then_inc(sem["ln_m2"], 1)
            dn_gemm(0, 0, 8, KT)
            for g in range(GM):
                pe.wait_ge(sem["ln_v"], g + 1)
                if g == 1:
                    pe.wait_ge(sem["ln_r"], 1)
                if g >= 2:
                    pe.wait_ge(sem["ln_tok"], g - 1)
                for c in range(NB):
                    ins = tp(pb[2 + g % 2][:, c * P:(c + 1) * P], blk(GV, NB * g + c))
                ins.then_inc(sem["ln_tp"], 1)
            pe.wait_ge(sem["sp_w"], 1)
            for g in range(GM):
                pe.wait_ge(sem["ln_tok"], g + 1)
                if g == 0:
                    pe.wait_ge(sem["mixed"], XA)
                if g >= 2:
                    pe.wait_ge(sem["sp_done"], g - 1)
                for c in range(NB):
                    ins = mm(pb[4 + g % 2][:, c * P:(c + 1) * P], blk(VTOK, c * GM + g), blk(wsT[:, :], g))
                ins.then_inc(sem["sp_o"], 1)
            for j in range(2):
                dn_gemm(0, j + 1, 0, 15)
                norm_sum(0, j)
                dn_gemm(0, j + 1, 15, KT)
            def gate_rows(h):
                pe.wait_ge(sem["sel"], h + 1)
                for c in range(NB):
                    ins = mm(pb[4][:, c * P:(c + 1) * P], blk(GSEL, c), C["tri_from"])
                ins.then_inc(sem["gb"], 1)
                for c in range(NB):
                    ins = tp(pb[2][:, c * P:(c + 1) * P], blk(BSEL, c))
                ins.then_inc(sem["bb"], 1)

            def products(h):
                pe.wait_ge(sem["kb"], h + 1)
                pe.wait_ge(sem["dec_in"], h + 1)
                for c in range(NB):
                    ins = mm(pb[3][:, c * P:(c + 1) * P], blk(KTT, c), blk(KB, c))
                ins.then_inc(sem["kk"], 1)
                for c in range(NB):
                    ins = mm(pb[4][:, c * P:(c + 1) * P], blk(KTT, c), blk(QT, c))
                ins.then_inc(sem["kk"], 1)

            def transposes(h):
                pe.wait_ge(sem["mixed"], h + XA)
                for c in range(NB):
                    ins = tp(pb[5][:, c * P:(c + 1) * P], blk(KTT, c))
                ins.then_inc(sem["tp"], 1)
                pe.wait_ge(sem["dn_n"], 3 * h + 3)
                for c in range(NB):
                    ins = tp(pb[1][:, c * P:(c + 1) * P], blk(VT, c))
                ins.then_inc(sem["tp"], 1)

            def level_u(h, k):
                pe.wait_ge(sem["m_lvl"], LEVELS * h + (k + 1))
                if k:
                    pe.wait_ge(sem["xy"], LEVELS * h + k)
                if k >= 2:
                    for c in range(NB):
                        ins = tp(pb[4][:, c * P:(c + 1) * P], blk(XI, c))
                    ins.then_inc(sem["y_ps"], 1)
                m = blk(ML, NB * (k % 2), NB)
                for c in range(NB):
                    if k == 0:
                        ins = tp(pb[2][:, c * P:(c + 1) * P], blk(m, c))
                    else:
                        ins = mm(packed(pb[2][:, c * H:(c + 1) * H], k), blk(m, c), even(blk(XI, c), k))
                ins.then_inc(sem["u_ps"], 1)

            def level_w(h, k):
                pe.wait_ge(sem["u_sb"], LEVELS * h + (k + 1))
                for c in range(NB):
                    half = slice(c * H, (c + 1) * H)
                    if k < LEVELS - 1:
                        ins = mm(pb[3][:, half], blk(YI, c), UI[:, half])
                    else:
                        ins = mm(pb[4][0:H, half], UI[:, half], YI[:, c * P + H:(c + 1) * P])
                ins.then_inc(sem["w_ps"], 1)

            def negated_keys(h):
                pe.wait_ge(sem["xy"], LEVELS * (h + 1))
                pe.wait_ge(sem["kbg"], h + 1)
                for c in range(NB):
                    ins = mm(pb[4][:, c * P:(c + 1) * P], blk(KBG, c), blk(YI, c))
                ins.then_inc(sem["nk_ps"], 1)

            def new_values(h, c):
                v = pb[1][:, 0:P]
                if c:
                    pe.wait_ge(sem["st"], (NB - 1) * h + c)
                else:
                    pe.wait_ge(sem["nk"], h + 1)
                ins = mm(v, blk(YI, c), blk(VB, c), True, c == 0)
                if c:
                    ins = mm(v, blk(NK, c), ST, False, True)
                ins.then_inc(sem["vn_ps"], 1)

            def chunk_out(h, c):
                o = pb[5][:, c * P:(c + 1) * P]
                pe.wait_ge(sem["vn"], NB * h + c + 1)
                ins = mm(o, VN, blk(AI, c), True, c == 0)
                if c:
                    ins = mm(o, ST, blk(QG, c), False, True)
                if c == NB - 1:
                    ins.then_inc(sem["o_ps"], 1)
                else:
                    mm(pb[3][:, 0:P], blk(KDEC, c), VN).then_inc(sem["s_ps"], 1)

            def out_sum(h):
                pe.wait_ge(sem["o_sq"], h + 1)
                mm(pb[0][:, :], C["ones"], OSQ).then_inc(sem["o_ss"], 1)

            def beside(part, p, h=None):
                part(0, 0, 4)
                products(p)
                part(0, 4, 7)
                transposes(p)
                part(0, 7, 9)
                level_u(p, 0)
                part(0, 9, 12)
                level_u(p, 1)
                part(0, 12, 14)
                level_w(p, 1)
                part(0, 14, KT)
                for j, k in ((1, 2), (2, 4)):
                    part(j, 0, 1)
                    level_u(p, k)
                    part(j, 1, 4)
                    level_w(p, k)
                    part(j, 4, 9)
                    level_u(p, k + 1)
                    part(j, 9, 12)
                    level_w(p, k + 1)
                    part(j, 12, 15)
                    if h is not None:
                        norm_sum(h, j - 1)
                    if j == 2:
                        level_u(p, 6)
                    part(j, 15, KT)
                part(3, 0, 1)
                level_w(p, 6)
                part(3, 1, 5)
                negated_keys(p)
                part(3, 5, 6)
                for c in range(NB):
                    new_values(p, c)
                    part(3, 6 + 2 * c, 7 + 2 * c)
                    chunk_out(p, c)
                    part(3, 7 + 2 * c, 8 + 2 * c)
                if h is not None:
                    gate_rows(h)
                part(3, 14, 15)
                out_sum(p)
                part(3, 15, KT)

            dn_gemm(0, 3, 0, 13)
            gate_rows(0)
            dn_gemm(0, 3, 13, KT)
            with pe.Fori(1, DN) as h:
                beside(lambda j, k0, k1: dn_gemm(h, j, k0, k1), h - 1, h)
            beside(lambda j, k0, k1: gemm(U_ZU + j, (U_ZU + j) % 2, k0, k1), DN - 1)
            with pe.Fori(GM // 2, GM) as g:
                for j in range(2):
                    gemm(2 * g + (U_ZU + j), (U_ZU + j) % 2)

            def projection(u0, before, pairs):
                for j in range(2):
                    gemm(u0 + j, (u0 + j) % 2, before=before if j == 0 else None)
                with pe.Fori(1, pairs) as i:
                    for j in range(2):
                        gemm(2 * i + (u0 + j), (u0 + j) % 2)

            projection(U_O1, 2 * KT, KT // 2)
            pe.wait_ge(sem["o1_acc"], KT + 1)
            mm(pb[0][:, :], C["ones"], ACC1).then_inc(sem["o1_ss"], 1)
            mm(pb[1][:, :], C["ones"], ACC2).then_inc(sem["o1_ss"], 1)

            with pe.Fori(0, DN) as h:
                u = 8 * h + U_D2

                def d2(j, k0=0, k1=KT):
                    gemm(u + j, (U_D2 + j) % 2, k0, k1, before=3 * KT if j == 0 else None)

                d2(0)
                d2(1)
                d2(2)
                d2(3, 0, 2)
                pe.wait_ge(sem["evac"], u + 3)
                for c in range(NB):
                    ins = tp(pb[4][:, c * P:(c + 1) * P], blk(VA, c))
                ins.then_inc(sem["a_vps"], 1)
                pe.wait_ge(sem["a_lo"], 2 * h + 2)
                for b in range(NB):
                    mm3(pb[b][:, 0:UN[b]], (KH, KL), (QH, QL), b, slice(b * P, S)).then_inc(sem["a_z"], 1)
                d2(3, 2)
                d2(4, 0, 8)
                pe.wait_ge(sem["a_spl"], h + 1)
                for b in reversed(range(NB)):
                    for key in range(b, NB):
                        m = sums[:, 0:P] if key == b else sums[:, P:2 * P]
                        out, cols = pb[b][:, (key - b) * P:UN[b]], slice(UP[key], UP[key] + UN[key])
                        mm(out, m, SPHI[:, cols], False, False, skip=True)
                        ins = mm(out, m, SPLO[:, cols], False, key == NB - 1, skip=True)
                    ins.then_inc(sem["a_cum"], 1)
                d2(4, 8, 14)
                pe.wait_ge(sem["a_w"], NB * h + NB)
                pe.wait_ge(sem["a_vtok"], h + 1)
                for b in range(NB):
                    ins = mm(pb[4][:, b * P:S], blk(VATOK, b), WB[:, UP[b]:UP[b] + UN[b]], b == 0, b == NB - 1, skip=True)
                ins.then_inc(sem["a_o"], 1)
                d2(4, 14)
                for j in range(2):
                    d2(5 + j, 0, 8)
                    pe.wait_ge(sem["b_sql"], 2 * h + j + 1)
                    mm(pb[5][:, :], sums[:, P:2 * P], SQH, True, False)
                    mm(pb[5][:, :], sums[:, P:2 * P], SQL, False, True).then_inc(sem["b_ss"], 1)
                    d2(5 + j, 8, 14)
                    if j == 1:
                        pe.wait_ge(sem["b_lo"], 2 * h + 2)
                        for c in range(NB):
                            mm3(pb[c][:, 0:DNN[c]], (QH, QL), (KH, KL), c, slice(0, DNN[c])).then_inc(sem["b_sc"], 1)
                    d2(5 + j, 14)
                d2(7, 0, 6)
                pe.wait_ge(sem["evac"], u + 7)
                pe.wait_ge(sem["mixed"], 2 * h + (M1 + 1))
                for c in range(NB):
                    ins = tp(pb[4][:, c * P:(c + 1) * P], blk(VBT, c))
                ins.then_inc(sem["b_vps"], 1)
                d2(7, 6, 12)
                pe.wait_ge(sem["b_p"], NB * h + NB)
                for b in range(NB):
                    for c in range(b, NB):
                        ins = tp(pb[b][:, (c - b) * P:(c - b + 1) * P], PB[:, DO[c] + b * P:DO[c] + (b + 1) * P])
                    ins.then_inc(sem["b_tp"], 1)
                d2(7, 12)
                pe.wait_ge(sem["b_vtok"], h + 1)
                pe.wait_ge(sem["b_pt"], NB * h + NB)
                for b in range(NB):
                    ins = mm(pb[4][:, b * P:S], blk(VBTOK, b), PTB[:, UP[b]:UP[b] + UN[b]], b == 0, b == NB - 1, skip=True)
                ins.then_inc(sem["b_o"], 1)
            projection(U_O2, 4 * KT, KT // 2)


def negatives():
    return np.concatenate([-np.tril(np.ones((P, P), np.float32)), -np.ones((P, P), np.float32)], axis=1)


def constants():
    j, i = np.meshgrid(np.arange(P), np.arange(P), indexing="ij")
    m = {"ident": i == j, "ones": i >= 0, "tri_from": i >= j,
         "strict": i > j, "hide": np.where(i > j, 0.0, NEG)}
    for k in range(LEVELS):
        m[f"level{k}"] = (i >> k == (j >> k) + 1) & ((j >> k) % 2 == 0)
    return np.concatenate([m[n].astype(np.float32) for n in CONSTS], axis=1)


def kernel(**inputs):
    import concourse.bacc as bacc
    from concourse.bass_utils import run_bass_kernel_spmd

    f = {n: np.asarray(a) for n, a in inputs.items()}

    def tiles(m):
        return m.reshape(KT, P, -1, P).transpose(2, 1, 0, 3).reshape(-1, P, KT * P)

    w1 = f["w_in"][0]
    gm, dn, xa = GM * P, DN * P, XA * P
    at = np.cumsum([0, gm, gm, gm, dn, dn, dn, dn, DN, DN, xa, xa])
    gu, gv_, gz, dq, dk, dv, dz, da, db, cq, cz = (w1[:, at[i]:at[i + 1]] for i in range(11))
    ab = np.zeros((D, P), np.float32)
    ab[:, 0:DN] = da
    ab[:, 32:32 + DN] = db

    def interleave(*parts):
        t = [tiles(p) for p in parts]
        return np.stack(t, axis=1).reshape(-1, P, KT * P)

    kv = f["w_mem_kv"][0]
    w2 = f["w_in_2"][0]
    w = np.concatenate([
        interleave(kv[:, :xa], kv[:, xa:]), tiles(ab), tiles(gv_), interleave(cq, cz),
        interleave(dq, dk, dv, dz), interleave(gz, gu), tiles(np.concatenate([f["w_out"][0][gm:], f["w_out"][0][:gm]])),
        interleave(*(w2[:, i * dn:(i + 1) * dn] for i in range(8))), tiles(f["w_out_2"][0])])
    assert w.shape[0] == U_END

    def cols(v):
        return v.reshape(-1, P).T

    conv = f["conv_w"][0].reshape(4, 3, DN, P).transpose(3, 2, 1, 0).reshape(P, DN * 3 * 4)
    params = np.concatenate([
        cols(f["ln_g"][0]), cols(f["mem_norm_g"][0]), cols(f["final_g"]), cols(f["norm_g_2"][0]),
        cols(f["gmlp_ln_g"][0]), cols(f["gmlp_ln_b"][0]), conv, cols(f["dn_norm_g"][0]), cols(f["q_norm_g_2"][0]),
        cols(f["k_norm_g_2"][0]), np.broadcast_to(f["dn_a_log"][0], (P, DN)), np.broadcast_to(f["dn_dt_bias"][0], (P, DN))],
        axis=1)
    p, x = np.arange(P)[:, None], np.arange(S)[None, :]
    rel = f["rel_bias_2"][0][:, np.clip(p - x + (S - P), -63, 256) + 63]
    arrays = {
        "w": w,
        "xT": f["x"][0].T.reshape(KT, P, S),
        "memT": f["mem"][0].T.reshape(KT, P, MEM).transpose(1, 0, 2).reshape(P, KT * MEM),
        "consts": constants(),
        "negatives": negatives(),
        "params": params,
        "ws_t": f["gmlp_ws"][0].transpose(2, 0, 1).reshape(P, GM * P),
        "bs_b": np.broadcast_to(f["gmlp_bs"][0].reshape(1, GM * P), (P, GM * P)),
        "rel": rel,
    }
    arrays = {n: np.ascontiguousarray(a) for n, a in arrays.items()}
    nc = bacc.Bacc("TRN2", target_bir_lowering=False, num_devices=1, dynamic_dma_scratch_size=4096)
    args = [nc.dram_tensor(f"in_{n}", a.shape, F32, kind="ExternalInput").ap() for n, a in arrays.items()]
    x1 = nc.dram_tensor("x1", (KT, P, S), F32, kind="Internal").ap()
    out = nc.dram_tensor("outT", (KT, P, S), F32, kind="ExternalOutput").ap()
    build(nc, *args, x1, out)
    r = run_bass_kernel_spmd(nc, [{f"in_{n}": a for n, a in arrays.items()}], core_ids=[0])
    return r.results[0]["outT"].reshape(1, D, S).transpose(0, 2, 1)
```
